# Optimizing a Trainium2 kernel written in Bass

```python
import math
import jax, jax.numpy as jnp
from jax import lax
import numpy as np

D_MODEL = 1024
BATCH = 1
SEQ = 1024
DEPTH = 1

N_MIXERS = 2
N_LAYERS_A = (DEPTH + N_MIXERS - 1) // N_MIXERS
N_LAYERS_B = DEPTH // N_MIXERS
N_META = 16
D_RNN = D_MODEL
N_LRU_BLOCKS = 4
LRU_BLOCK = D_RNN // N_LRU_BLOCKS
CONV_WIDTH = 4
LRU_C = 8.0
HEAD_DIM = 64
N_Q_HEADS = D_MODEL // HEAD_DIM
N_KV_HEADS = 4
Q_PER_KV = N_Q_HEADS // N_KV_HEADS
WINDOW = 128
QKV_WIDTH = (N_Q_HEADS + 2 * N_KV_HEADS) * HEAD_DIM
N_BUCKETS = 32
MAX_EXACT = N_BUCKETS // 2
MAX_DISTANCE = WINDOW
N_EXPERTS = 64
TOP_K = 8
N_GROUPS = 8
TOPK_GROUPS = 4
D_EXPERT = 256
D_SHARED = 256
ROUTED_SCALE = 2.5
EXPERT_BLOCK = 256
ALPHA = (2 * DEPTH) ** 0.25
BETA = (8 * DEPTH) ** -0.25
LN_EPS = 1e-5

kernel_name = "hybrid_rglru_swa_sink_moe_deepnorm"

def _layer_norm(z, g, b):
    zf = z.astype(jnp.float32)
    mu = jnp.mean(zf, axis=-1, keepdims=True)
    var = jnp.mean(jnp.square(zf - mu), axis=-1, keepdims=True)
    out = (zf - mu) * lax.rsqrt(var + LN_EPS) * g.astype(jnp.float32) + b.astype(jnp.float32)
    return out.astype(z.dtype)

def _linear_combine(c1, c2):
    a1, b1 = c1
    a2, b2 = c2
    return a1 * a2, a2 * b1 + b2

def _rglru_mixer(h, w_in, b_in, conv_w, conv_b, w_gates, b_gates, a_param, w_out):
    B, L, _ = h.shape
    u = h @ w_in + b_in
    y = jax.nn.gelu(u[..., :D_RNN], approximate=True)
    xr = u[..., D_RNN:]
    xp = jnp.pad(xr, ((0, 0), (CONV_WIDTH - 1, 0), (0, 0)))
    xc = conv_b + xp[:, 0:L] * conv_w[0]
    for k in range(1, CONV_WIDTH):
        xc = xc + xp[:, k:k + L] * conv_w[k]
    g = jnp.einsum('blnc,ncd->blnd', xc.reshape(B, L, N_LRU_BLOCKS, LRU_BLOCK), w_gates) + b_gates
    gate_x = jax.nn.sigmoid(g[..., :LRU_BLOCK].astype(jnp.float32)).reshape(B, L, D_RNN)
    gate_a = jax.nn.sigmoid(g[..., LRU_BLOCK:].astype(jnp.float32)).reshape(B, L, D_RNN)
    log_a = -LRU_C * gate_a * jax.nn.softplus(-a_param.astype(jnp.float32))
    a = jnp.exp(log_a)
    mult = jnp.sqrt(-jnp.expm1(2.0 * log_a))
    bx = xc.astype(jnp.float32) * gate_x * mult
    _, hs = lax.associative_scan(_linear_combine, (a, bx), axis=1)
    return (y * hs.astype(h.dtype)) @ w_out

def _t5_bucket(d):
    d = jnp.maximum(d, 0)
    df = jnp.maximum(d, 1).astype(jnp.float32)
    large = MAX_EXACT + (jnp.log(df / MAX_EXACT) / math.log(MAX_DISTANCE / MAX_EXACT)
                         * (N_BUCKETS - MAX_EXACT)).astype(jnp.int32)
    large = jnp.minimum(large, N_BUCKETS - 1)
    return jnp.where(d < MAX_EXACT, d, large)

def _rel_bias(rel_table, d):
    b = rel_table[_t5_bucket(d)]
    return jnp.moveaxis(b, -1, 0).reshape(N_KV_HEADS, Q_PER_KV, *d.shape).astype(jnp.float32)

def _sink_attend(s, mask, sinks_hg, v):
    s = jnp.where(mask, s, -jnp.inf)
    sink = sinks_hg[None, :, :, None, None]
    m = jnp.maximum(jnp.max(s, axis=-1, keepdims=True), sink)
    p = jnp.exp(s - m)
    denom = jnp.sum(p, axis=-1, keepdims=True) + jnp.exp(sink - m)
    return jnp.einsum('bhgqk,bkhd->bqhgd', (p / denom).astype(v.dtype), v)

def _swa_mixer(h, w_qkv, sinks, w_o, rel_table):
    B, L, _ = h.shape
    n_blocks = (L - N_META) // WINDOW
    qkv = h @ w_qkv
    q = (qkv[..., :N_Q_HEADS * HEAD_DIM] * HEAD_DIM ** -0.5).reshape(B, L, N_KV_HEADS, Q_PER_KV, HEAD_DIM)
    k = qkv[..., N_Q_HEADS * HEAD_DIM:(N_Q_HEADS + N_KV_HEADS) * HEAD_DIM].reshape(B, L, N_KV_HEADS, HEAD_DIM)
    v = qkv[..., (N_Q_HEADS + N_KV_HEADS) * HEAD_DIM:].reshape(B, L, N_KV_HEADS, HEAD_DIM)
    sinks_hg = sinks.astype(jnp.float32).reshape(N_KV_HEADS, Q_PER_KV)
    qm, km, vm = q[:, :N_META], k[:, :N_META], v[:, :N_META]
    d_mm = jnp.arange(N_META)[:, None] - jnp.arange(N_META)[None, :]
    s_mm = jnp.einsum('bqhgd,bkhd->bhgqk', qm, km).astype(jnp.float32) + _rel_bias(rel_table, d_mm)
    o_meta = _sink_attend(s_mm, d_mm >= 0, sinks_hg, vm)

    def to_blocks(t):
        return jnp.moveaxis(t[:, N_META:].reshape(B, n_blocks, WINDOW, *t.shape[2:]), 1, 0)

    qb, kb, vb = to_blocks(q), to_blocks(k), to_blocks(v)
    kp = jnp.concatenate([jnp.zeros_like(kb[:1]), kb[:-1]], axis=0)
    vp = jnp.concatenate([jnp.zeros_like(vb[:1]), vb[:-1]], axis=0)
    qi = jnp.arange(WINDOW)[:, None]
    kj = jnp.arange(2 * WINDOW)[None, :]
    d_loc = WINDOW + qi - kj
    in_win = (d_loc >= 0) & (d_loc < WINDOW)
    in_cur = kj >= WINDOW
    m_idx = jnp.arange(N_META)[None, :]
    meta_vis = jnp.ones((WINDOW, N_META), dtype=bool)

    def block(args):
        n, q_n, kp_n, kc_n, vp_n, vc_n = args
        keys = jnp.concatenate([km, kp_n, kc_n], axis=1)
        vals = jnp.concatenate([vm, vp_n, vc_n], axis=1)
        d = jnp.concatenate([N_META + n * WINDOW + qi - m_idx, d_loc], axis=1)
        mask = jnp.concatenate([meta_vis, in_win & ((n > 0) | in_cur)], axis=1)
        s = jnp.einsum('bqhgd,bkhd->bhgqk', q_n, keys).astype(jnp.float32) + _rel_bias(rel_table, d)
        return _sink_attend(s, mask, sinks_hg, vals)

    o_blk = lax.map(block, (jnp.arange(n_blocks), qb, kp, kb, vp, vb))
    o_real = jnp.moveaxis(o_blk, 0, 1).reshape(B, L - N_META, N_Q_HEADS * HEAD_DIM)
    o = jnp.concatenate([o_meta.reshape(B, N_META, N_Q_HEADS * HEAD_DIM), o_real], axis=1)
    return o @ w_o

def _swiglu(x, w_gu, w_down):
    f = w_down.shape[0]
    gu = x @ w_gu
    return (jax.nn.silu(gu[..., :f]) * gu[..., f:]) @ w_down

def _route(xt, router_w, router_bias):
    n = xt.shape[0]
    scores = jax.nn.sigmoid(xt.astype(jnp.float32) @ router_w.astype(jnp.float32))
    choice = scores + router_bias.astype(jnp.float32)
    grp = choice.reshape(n, N_GROUPS, N_EXPERTS // N_GROUPS)
    grp_score = jnp.sum(lax.top_k(grp, 2)[0], axis=-1)
    _, gidx = lax.top_k(grp_score, TOPK_GROUPS)
    gmask = jnp.any(gidx[..., :, None] == jnp.arange(N_GROUPS), axis=-2)
    emask = jnp.repeat(gmask, N_EXPERTS // N_GROUPS, axis=-1)
    _, idx = lax.top_k(jnp.where(emask, choice, -jnp.inf), TOP_K)
    w = jnp.take_along_axis(scores, idx, axis=-1)
    w = w / (jnp.sum(w, axis=-1, keepdims=True) + 1e-20) * ROUTED_SCALE
    return idx, w

def _routed_experts(xt, idx, wts, w_gu, w_down):
    n, d = xt.shape
    n_assign = n * TOP_K
    flat_e = idx.reshape(-1)
    flat_tok = jnp.arange(n_assign, dtype=jnp.int32) // TOP_K
    flat_w = wts.reshape(-1)
    order = jnp.argsort(flat_e)
    sorted_e = flat_e[order]
    counts = jnp.bincount(flat_e, length=N_EXPERTS)
    padded = (counts + EXPERT_BLOCK - 1) // EXPERT_BLOCK * EXPERT_BLOCK
    start = jnp.cumsum(counts) - counts
    pend = jnp.cumsum(padded)
    pstart = pend - padded
    dest = pstart[sorted_e] + (jnp.arange(n_assign) - start[sorted_e])
    n_blocks = (n_assign + N_EXPERTS * (EXPERT_BLOCK - 1) + EXPERT_BLOCK - 1) // EXPERT_BLOCK
    rows_total = n_blocks * EXPERT_BLOCK
    row_tok = jnp.full((rows_total,), n, dtype=jnp.int32).at[dest].set(flat_tok[order])
    row_w = jnp.zeros((rows_total,), wts.dtype).at[dest].set(flat_w[order])
    block_e = jnp.minimum(jnp.searchsorted(pend, jnp.arange(n_blocks) * EXPERT_BLOCK, side='right'),
                          N_EXPERTS - 1)
    x_pad = jnp.concatenate([xt, jnp.zeros((1, d), xt.dtype)], axis=0)
    f = w_down.shape[1]

    def body(b, acc):
        rows = lax.dynamic_slice(row_tok, (b * EXPERT_BLOCK,), (EXPERT_BLOCK,))
        rw = lax.dynamic_slice(row_w, (b * EXPERT_BLOCK,), (EXPERT_BLOCK,))
        e = block_e[b]
        gu = x_pad[rows] @ w_gu[e]
        y = ((jax.nn.silu(gu[:, :f]) * gu[:, f:]) @ w_down[e]) * rw[:, None]
        return acc.at[rows].add(y)

    acc = lax.fori_loop(0, n_blocks, body, jnp.zeros((n + 1, d), xt.dtype))
    return acc[:n]

def _moe(h, router_w, router_bias, w_gu, w_down, sh_w_gu, sh_w_down):
    B, L, D = h.shape
    xt = h.reshape(B * L, D)
    idx, w = _route(xt, router_w, router_bias)
    routed = _routed_experts(xt, idx, w.astype(xt.dtype), w_gu, w_down)
    shared = _swiglu(xt, sh_w_gu, sh_w_down)
    return (routed + shared).reshape(B, L, D)

def setup_inputs(seed: int = 0) -> dict:
    key = jax.random.key(seed)
    ks = jax.random.split(key, 24)
    f32 = jnp.float32
    nrm = lambda k, s, sc: jax.random.normal(k, s, f32) * sc
    u = jax.random.uniform(ks[8], (N_LAYERS_A, D_RNN), f32, minval=0.9, maxval=0.999)
    s8 = u ** (1.0 / LRU_C)
    a_param = jnp.log(s8) - jnp.log1p(-s8)
    return {
        "x": nrm(ks[0], (BATCH, SEQ, D_MODEL), 1.0),
        "meta_tokens": nrm(ks[1], (N_META, D_MODEL), 1.0),
        "rg_w_in": nrm(ks[2], (N_LAYERS_A, D_MODEL, 2 * D_RNN), D_MODEL ** -0.5),
        "rg_b_in": nrm(ks[3], (N_LAYERS_A, 2 * D_RNN), 0.01),
        "rg_conv_w": nrm(ks[4], (N_LAYERS_A, CONV_WIDTH, D_RNN), CONV_WIDTH ** -0.5),
        "rg_conv_b": nrm(ks[5], (N_LAYERS_A, D_RNN), 0.01),
        "rg_w_gates": nrm(ks[6], (N_LAYERS_A, N_LRU_BLOCKS, LRU_BLOCK, 2 * LRU_BLOCK), LRU_BLOCK ** -0.5),
        "rg_b_gates": nrm(ks[7], (N_LAYERS_A, N_LRU_BLOCKS, 2 * LRU_BLOCK), 0.01),
        "rg_a_param": a_param,
        "rg_w_out": nrm(ks[9], (N_LAYERS_A, D_RNN, D_MODEL), D_RNN ** -0.5 * BETA),
        "attn_w_qkv": nrm(ks[10], (N_LAYERS_B, D_MODEL, QKV_WIDTH), D_MODEL ** -0.5),
        "attn_sinks": nrm(ks[11], (N_LAYERS_B, N_Q_HEADS), 1.0),
        "attn_w_o": nrm(ks[12], (N_LAYERS_B, N_Q_HEADS * HEAD_DIM, D_MODEL), (N_Q_HEADS * HEAD_DIM) ** -0.5 * BETA),
        "rel_bias_table": nrm(ks[13], (N_BUCKETS, N_Q_HEADS), 0.5),
        "ln_gain": 1.0 + nrm(ks[14], (DEPTH, 2, D_MODEL), 0.02),
        "ln_bias": nrm(ks[15], (DEPTH, 2, D_MODEL), 0.02),
        "router_w": nrm(ks[16], (DEPTH, D_MODEL, N_EXPERTS), D_MODEL ** -0.5),
        "router_bias": nrm(ks[17], (DEPTH, N_EXPERTS), 0.01),
        "expert_w_gu": nrm(ks[18], (DEPTH, N_EXPERTS, D_MODEL, 2 * D_EXPERT), D_MODEL ** -0.5),
        "expert_w_down": nrm(ks[19], (DEPTH, N_EXPERTS, D_EXPERT, D_MODEL), D_EXPERT ** -0.5 * BETA),
        "shared_w_gu": nrm(ks[20], (DEPTH, D_MODEL, 2 * D_SHARED), D_MODEL ** -0.5),
        "shared_w_down": nrm(ks[21], (DEPTH, D_SHARED, D_MODEL), D_SHARED ** -0.5 * BETA),
    }

def reference(x, meta_tokens, rg_w_in, rg_b_in, rg_conv_w, rg_conv_b, rg_w_gates, rg_b_gates,
              rg_a_param, rg_w_out, attn_w_qkv, attn_sinks, attn_w_o, rel_bias_table, ln_gain,
              ln_bias, router_w, router_bias, expert_w_gu, expert_w_down, shared_w_gu, shared_w_down):
    B = x.shape[0]
    meta = jnp.broadcast_to(meta_tokens[None].astype(x.dtype), (B, N_META, D_MODEL))
    h = jnp.concatenate([meta, x], axis=1)
    for i in range(DEPTH):
        j = i // N_MIXERS
        if i % N_MIXERS == 0:
            mix = _rglru_mixer(h, rg_w_in[j], rg_b_in[j], rg_conv_w[j], rg_conv_b[j],
                               rg_w_gates[j], rg_b_gates[j], rg_a_param[j], rg_w_out[j])
        else:
            mix = _swa_mixer(h, attn_w_qkv[j], attn_sinks[j], attn_w_o[j], rel_bias_table)
        h = _layer_norm(ALPHA * h + mix, ln_gain[i, 0], ln_bias[i, 0])
        ffn = _moe(h, router_w[i], router_bias[i], expert_w_gu[i], expert_w_down[i],
                   shared_w_gu[i], shared_w_down[i])
        h = _layer_norm(ALPHA * h + ffn, ln_gain[i, 1], ln_bias[i, 1])
    return h[:, N_META:]


_drawn_inputs = setup_inputs


def setup_inputs(seed=0):
    import zlib

    import numpy as np

    out = dict(_drawn_inputs(seed))
    spreads = {}
    factors = {'rg_b_gates': 16.76}
    for name, (base, spread) in spreads.items():
        noise = np.random.default_rng([zlib.crc32(name.encode()), seed]).standard_normal(out[name].shape)
        drawn = base * np.exp(spread * noise) if base else spread * noise
        out[name] = __import__('jax').numpy.asarray(drawn.astype(out[name].dtype))
    for name, factor in factors.items():
        out[name] = (out[name] * factor).astype(out[name].dtype)
    return out
```

```python
import math

import concourse.bass as bass
import numpy as np
from concourse import mybir
from concourse.alu_op_type import AluOpType as ALU

ACT = mybir.ActivationFunctionType
AX = mybir.AxisListType.X
F32 = mybir.dt.float32
F32R = mybir.dt.float32r
BF16 = mybir.dt.bfloat16
I32 = mybir.dt.int32
U32 = mybir.dt.uint32

P = 128
D = 1024
KT = D // P
N_META = 16
SEQ = 1024
L = N_META + SEQ
CHUNK = 348
LP = 3 * CHUNK
TILES = -(-L // P)
ROWS = [min(P, L - i * P) for i in range(TILES)]
LRU_BLOCKS = 4
LB = D // LRU_BLOCKS
LT = LB // P
CONV = 4
LRU_C = 8.0
E = 64
TOP_K = 8
GROUPS = 8
GSIZE = E // GROUPS
TOP_GROUPS = 4
F = 256
FT = F // P
ROUTED_SCALE = 2.5
ALPHA = 2.0 ** 0.25
LN_EPS = 1e-5
BIG = 3e38

BLOCK = 168
REST = BLOCK - P
NB_MAX = -(-L // BLOCK)
STRIDE = NB_MAX * BLOCK
LIST_COLS = -(-((E + 1) * STRIDE + 2 * BLOCK) // P)
LIST = LIST_COLS * P
T_MAX = E + (L * TOP_K) // BLOCK + 1
PAIRS = L * TOP_K
PAD = 2048
assert PAD >= STRIDE + BLOCK and PAD & (PAD - 1) == 0

QX = KT // 2
STEPS = 4
SEED = 2 * STEPS
assert STEPS == QX == 2 * FT == 2 * (D // 512)

C_BIN, C_CW, C_CB, C_BG, C_AP = 0, 16, 48, 56, 72
C_N = 80


class SbufMap:

    def __init__(self, nc):
        self.nc = nc
        self.base = -(-nc.sbuf_base // 64) * 64

    def at(self, name, offset, shape, dtype):
        return self.nc.alloc_sbuf_tensor_at(name, list(shape), dtype, offset=self.base + offset)


class Chain:

    def __init__(self, eng, sem):
        self.eng, self.sem, self.n = eng, sem, 0

    def step(self, ins):
        self.n += 1
        ins.then_inc(self.sem, 1)
        self.eng.wait_ge(self.sem, self.n)


def split_product(pe, out, lhs, rhs, first, last):
    pe.matmul(out, lhs[0], rhs[0], start=first, stop=False)
    pe.matmul(out, lhs[0], rhs[1], start=False, stop=False)
    return pe.matmul(out, lhs[1], rhs[0], start=False, stop=last)


def build(nc, hT, h_rows, w_in, chan, w_gates, w_out, ln, router_w, router_b, w_gu, w_down,
          sh_gu, sh_down, out):
    m = SbufMap(nc)
    sem = lambda name: nc.alloc_semaphore(name)
    bank = nc.alloc_psum_tensor("bank", [P, 8, 512], F32)

    h1_rows = nc.dram_tensor("h1_rows", (L + PAD // TOP_K, D), F32).ap()
    pair_list = nc.dram_tensor("pair_list", (LIST, 2), I32).ap()
    pair_rows = nc.dram_tensor("pair_rows", (PAIRS + PAD, D), F32).ap()
    sched_dram = nc.dram_tensor("sched_dram", (P, 4), I32).ap()

    o = 203520
    ident = m.at("ident", o, [P, P], F32)
    tri = m.at("tri", o + 512, [P, P], BF16)
    ones = m.at("ones", o + 768, [P, P], BF16)
    iota_e_i = m.at("iota_e_i", o + 1024, [P, E], I32)
    iota_e = m.at("iota_e", o + 1280, [P, E], F32)
    list_start_i = m.at("list_start_i", o + 1536, [P, E], I32)
    list_start = m.at("list_start", o + 1792, [P, E], F32)
    block_id = m.at("block_id", o + 2112, [P, 1], F32)
    block_id_i = m.at("block_id_i", o + 2144, [P, 1], I32)
    place = m.at("place", o + 2176, [P, TILES, TOP_K], I32)
    weight = m.at("weight", o + 2464, [P, TILES, TOP_K], F32)
    rbias = m.at("rbias", o + 2752, [P, E], F32)
    sched_row = m.at("sched_row", o + 3008, [1, 4 * P], I32)
    par = m.at("par", o + 5056, [P, C_N], F32)
    lru_coef = m.at("lru_coef", o + 5376, [P, 2, KT], F32)
    sp_tmp = m.at("sp_tmp", o + 5440, [P, 4, KT], F32)
    stats = m.at("stats", o + 5568, [P, 2, 6], F32)
    mv = m.at("mv", o + 5632, [P, 2], F32)
    rstd = m.at("rstd", o + 5664, [P, 2], F32)
    mask = m.at("mask", o + 5696, [P, E], BF16)
    cum = m.at("cum", o + 5824, [P, 2, E], BF16)

    pair_id = m.at("pair_id", 212192, [P, TILES, TOP_K, 2], I32)
    pair = [m.at(f"pair{j}", 203328 + 32 * j, [P, 2, 2], I32) for j in range(2)]
    to_row = [m.at(f"to_row{j}", 203392 + 32 * j, [P, 2], I32) for j in range(2)]

    hT_raw = m.at("hT_raw", 0, [P, KT, LP], F32)
    hT_lo = m.at("hT_lo", 0, [P, KT, LP], F32R)
    hT_hi = m.at("hT_hi", 33408, [P, KT, LP], F32R)
    NW = 3
    win_raw = [m.at(f"win_raw{j}", 66816 + 8192 * j, [P, KT, P], F32) for j in range(NW)]
    win_lo = [m.at(f"win_lo{j}", 66816 + 8192 * j, [P, KT, P], F32R) for j in range(NW)]
    win_hi = [m.at(f"win_hi{j}", 66816 + 8192 * j + 4096, [P, KT, P], F32R) for j in range(NW)]
    wg_raw = m.at("wg_raw", 91392, [P, LT, 2 * LB], F32)
    wg_lo = m.at("wg_lo", 91392, [P, LT, 2 * LB], F32R)
    wg_hi = m.at("wg_hi", 91392 + 4096, [P, LT, 2 * LB], F32R)
    zT = m.at("zT", 99584, [P, KT, LP], F32)
    xr = m.at("xr", 132992, [P, LT, LP + CONV - 1], F32)
    xc = m.at("xc", 141376, [P, LT, LP], F32)
    xc_hi = m.at("xc_hi", 149728, [P, LT, LP], F32R)
    xc_lo = m.at("xc_lo", 158080, [P, LT, LP], F32R)
    gate_x = m.at("gate_x", 166432, [P, LT, LP], F32)
    gate_a = m.at("gate_a", 174784, [P, LT, LP], F32)
    decay = m.at("decay", 183136, [P, LT, LP], F32)
    th = m.at("th", 191488, [P, LT, LP], F32)
    pads = m.at("pads", 191488, [P, LIST_COLS, 2], I32)
    wout_raw = m.at("wout_raw", 0, [P, KT, D], F32)
    wout_lo = m.at("wout_lo", 0, [P, KT, D], F32R)
    wout_hi = m.at("wout_hi", 33408, [P, KT, D], F32R)
    z_hi = [m.at(f"z_hi{j}", 66816 + 4096 * j, [P, KT, P], F32R) for j in range(2)]
    z_lo = [m.at(f"z_lo{j}", 75008 + 4096 * j, [P, KT, P], F32R) for j in range(2)]
    h_in = m.at("h_in", 83200, [P, D], F32)
    hot = m.at("hot", 87296, [P, TOP_K, E], F32)
    picked = m.at("picked", 89344, [P, TOP_K, E], F32)
    ln_b = m.at("ln_b", 91392, [P, 2, D], F32)
    rw = m.at("rw", 209600, [P, KT, E], F32)
    scores = m.at("scores", 32768, [P, E], F32)
    choice = m.at("choice", 33024, [P, E], F32)
    top_of = m.at("top_of", 66176, [P, GROUPS, 8], F32)
    rowval = m.at("rowval", 66432, [P, E], F32)
    small = m.at("small", 211648, [P, 10, 8], F32)
    idx_u = m.at("idx_u", 211968, [P, 2, 8], U32)
    ghot = m.at("ghot", 212032, [P, TOP_GROUPS, GROUPS], F32)
    expert = m.at("expert", 212160, [P, TOP_K], F32)
    h1T = m.at("h1T", 132992, [P, KT, LP], F32)
    h1 = m.at("h1", 166432, [P, TILES, D], F32)
    sgu = m.at("sgu", 0, [P, KT, 2 * F], F32)
    sdn = m.at("sdn", 16384, [P, FT, D], F32)
    sg = m.at("sg", 24576, [P, FT, LP], F32)
    sh = m.at("sh", 32960, [P, FT, LP], F32)
    cnt = m.at("cnt", 123392, [P, 6, E], F32)
    sched = m.at("sched", 124928, [P, 8], F32)
    sched_i = m.at("sched_i", 124960, [P, 4], I32)
    wgu = [m.at(f"wgu{j}", 41472 + 16384 * j, [P, KT, 2 * F], F32) for j in range(2)]
    wd_raw = [m.at(f"wd_raw{j}", 74240 + 16384 * j, [P, FT, D], F32) for j in range(2)]
    wd_lo = [m.at(f"wd_lo{j}", 74240 + 16384 * j, [P, FT, D], F32R) for j in range(2)]
    wd_hi = [m.at(f"wd_hi{j}", 74240 + 16384 * j + 8192, [P, FT, D], F32R) for j in range(2)]
    xg = [m.at(f"xg{j}", 107008 + 8192 * j, [P, 2, D], F32) for j in range(2)]
    ysb = [m.at(f"ysb{j}", 8192 * j, [P, 2, D], F32) for j in range(2)]
    xT = m.at("xT", 16384, [P, KT, BLOCK], F32)
    gact = m.at("gact", 22528, [P, FT, BLOCK], F32)
    hid = m.at("hid", 24064, [P, FT, BLOCK], F32)
    hid_hi = m.at("hid_hi", 128000, [P, FT, 2 * P], F32R)
    hid_lo = m.at("hid_lo", 130048, [P, FT, 2 * P], F32R)
    got = [m.at(f"got{j}", 41472 + 32768 * j, [P, TOP_K, D], F32) for j in range(2)]
    ln_f = m.at("ln_f", 32768, [P, 2, D], F32)

    consts_ready = sem("consts_ready")
    places_ready, pads_ready = sem("places_ready"), sem("pads_ready")
    list_cleared = sem("list_cleared")
    par_loaded = sem("par_loaded")
    hT_loaded = [sem(f"hT_loaded{k}") for k in range(KT)]
    hT_hi_ready, hT_lo_ready = sem("hT_hi_ready"), sem("hT_lo_ready")
    win_loaded = [sem(f"win_loaded{j}") for j in range(NW)]
    win_hi_ready, win_lo_ready = sem("win_hi_ready"), sem("win_lo_ready")
    wg_loaded = sem("wg_loaded")
    wg_hi_ready, wg_lo_ready = sem("wg_hi_ready"), sem("wg_lo_ready")
    tile_done = sem("tile_done")
    tile_read = sem("tile_read")
    conv_done = sem("conv_done")
    xc_split = sem("xc_split")
    coef_ready = sem("coef_ready")
    th_ready = sem("th_ready")
    mult2_ready = sem("mult2_ready")
    mult_ready = sem("mult_ready")
    scan_done = sem("scan_done")
    dve_step = sem("dve_step")
    act_step = sem("act_step")
    pool_step = sem("pool_step")
    wout_loaded = sem("wout_loaded")
    dve_steps, pool_n = [], [0]

    def in_col(n, j):
        return (D if j < LT else 0) + n * LB + (j % LT) * P

    N_IN = 2 * LT * LRU_BLOCKS
    PER = 4 * LT

    with nc.Block() as block:
        @block.sync
        def _(sp):
            def load_win(q):
                n, j = divmod(q, 2 * LT)
                if q >= NW:
                    n0, j0 = divmod(q - NW, 2 * LT)
                    sp.wait_ge(tile_done, PER * n0 + j0 + 1)
                c = in_col(n, j)
                sp.dma_start(win_raw[q % NW][:, :, :],
                             w_in[:, c:c + P].rearrange("(k p) c -> p k c", p=P)
                             ).then_inc(win_loaded[q % NW], 16)

            def load_wg(n):
                if n:
                    sp.wait_ge(tile_done, PER * n)
                sp.dma_start(wg_raw[:, :, :], w_gates[n].rearrange("(k p) c -> p k c", p=P)
                             ).then_inc(wg_loaded, 16)

            load_win(0)
            for k in range(KT):
                sp.dma_start(hT_raw[:, k, 0:L], hT[k * P:(k + 1) * P, :]).then_inc(hT_loaded[k], 16)
                if k == 0:
                    sp.dma_start(par[:, :], chan).then_inc(par_loaded, 16)
            load_win(1)
            load_win(2)
            load_wg(0)
            sp.wait_ge(pads_ready, 2)
            sp.dma_start(pair_list.rearrange("(p c) w -> p c w", p=P), pads[:, :, :]
                         ).then_inc(list_cleared, 16)
            for q in range(NW, N_IN):
                load_win(q)
                if q % (2 * LT) == 2 and q > 2 * LT:
                    load_wg(q // (2 * LT))
            sp.wait_ge(tile_done, PER * (LRU_BLOCKS - 1) + 2 * LT)
            sp.dma_start(wout_raw[:, :, :], w_out.rearrange("(k p) c -> p k c", p=P)
                         ).then_inc(wout_loaded, 16)

        @block.gpsimd
        def _(pool):
            s = Chain(pool, pool_step)
            s.step(pool.memset(hT_raw[:, :, L:LP], 0.0))
            s.step(pool.memset(xr[:, :, 0:CONV - 1], 0.0))
            s.step(pool.memset(ident[:, :], 0.0))
            s.step(pool.affine_select(out=ident[:, :], in_=ident[:, :], compare_op=ALU.not_equal,
                                      fill=1.0, base=0, pattern=[[-1, P]], channel_multiplier=1))
            s.step(pool.memset(ones[:, :], 1.0))
            s.step(pool.affine_select(out=tri[:, :], in_=ones[:, :], compare_op=ALU.is_gt,
                                      fill=0.0, base=0, pattern=[[1, P]], channel_multiplier=-1))
            s.step(pool.iota(iota_e_i[:, :], pattern=[[1, E]], base=0, channel_multiplier=0))
            s.step(pool.iota(list_start_i[:, :], pattern=[[STRIDE, E]], base=0,
                             channel_multiplier=0))
            s.step(pool.iota(block_id_i[:, :], pattern=[[1, 1]], base=0, channel_multiplier=1))
            s.step(pool.tensor_copy(iota_e[:, :], iota_e_i[:, :]))
            s.step(pool.tensor_copy(list_start[:, :], list_start_i[:, :]))
            s.step(pool.tensor_copy(block_id[:, :], block_id_i[:, :]))
            s.step(pool.memset(cum[:, 0, :], 0.0))
            for what in range(2):
                pool.iota(pads[:, :, what], pattern=[[1, LIST_COLS]], base=0,
                          channel_multiplier=LIST_COLS).then_inc(places_ready, 1)
            for b in range(2):
                s.step(pool.memset(pair[b][:, :, :], 0))
            s.step(pool.iota(pair_id[:, :, :, 0], pattern=[[P, TILES], [0, TOP_K]], base=0,
                             channel_multiplier=1))
            pool.iota(pair_id[:, :, :, 1], pattern=[[P * TOP_K, TILES], [1, TOP_K]], base=0,
                      channel_multiplier=TOP_K).then_inc(consts_ready, 1)

            def lo_win(q):
                n, j = divmod(q, 2 * LT)
                pool.wait_ge(win_hi_ready, q + 1)
                pool.tensor_tensor(win_lo[q % NW][:, :, :], win_raw[q % NW][:, :, :],
                                   win_hi[q % NW][:, :, :].bitcast(F32), ALU.subtract
                                   ).then_inc(win_lo_ready, 1)

            for n in range(LRU_BLOCKS):
                for j in range(2 * LT):
                    lo_win(2 * LT * n + j)
                pool.wait_ge(wg_hi_ready, n + 1)
                pool.tensor_tensor(wg_lo[:, :, :], wg_raw[:, :, :], wg_hi[:, :, :].bitcast(F32),
                                   ALU.subtract).then_inc(wg_lo_ready, 1)
            pool_n[0] = s.n

        @block.tensor
        def _(pe):
            for n in range(LRU_BLOCKS):
                for j in range(PER):
                    s = PER * n + j
                    b0 = 3 * (s % 2)
                    if s >= 2:
                        pe.wait_ge(tile_read, s - 1)
                    if j < 2 * LT:
                        q = 2 * LT * n + j
                        pe.wait_ge(win_hi_ready, q + 1)
                        pe.wait_ge(win_lo_ready, q + 1)
                        kt, w = KT, (win_hi[q % NW], win_lo[q % NW])
                        x, c0 = (hT_hi, hT_lo), 0
                    else:
                        pe.wait_ge(xc_split, LT * (n + 1))
                        pe.wait_ge(wg_hi_ready, n + 1)
                        pe.wait_ge(wg_lo_ready, n + 1)
                        kt, w = LT, (wg_hi, wg_lo)
                        x, c0 = (xc_hi, xc_lo), (j - 2 * LT) * P
                    for k in range(kt):
                        if s == 0:
                            pe.wait_ge(hT_hi_ready, k + 1)
                            pe.wait_ge(hT_lo_ready, k + 1)
                        for c in range(3):
                            last = split_product(
                                pe, bank[:, b0 + c, 0:CHUNK],
                                [a[:, k, c0:c0 + P] for a in w],
                                [a[:, k, c * CHUNK:(c + 1) * CHUNK] for a in x],
                                k == 0, k == kt - 1)
                    last.then_inc(tile_done, 1)

        @block.scalar
        def _(act):
            rows3 = lambda a: a.rearrange("p (c t) -> p c t", c=3)

            def psum_tile(s):
                act.wait_ge(tile_done, s + 1)
                b0 = 3 * (s % 2)
                return bank[:, b0:b0 + 3, 0:CHUNK]

            def hi_win(q):
                act.wait_ge(win_loaded[q % NW], 16 * (q // NW + 1))
                if q >= NW:
                    n0, j0 = divmod(q - NW, 2 * LT)
                    act.wait_ge(tile_done, PER * n0 + j0 + 1)
                act.activation(win_hi[q % NW][:, :, :], win_raw[q % NW][:, :, :], ACT.Copy
                               ).then_inc(win_hi_ready, 1)

            hi_win(0)
            act.wait_ge(pool_step, 1)
            for k in range(KT):
                act.wait_ge(hT_loaded[k], 16)
                act.activation(hT_hi[:, k, :], hT_raw[:, k, :], ACT.Copy).then_inc(hT_hi_ready, 1)
            hi_win(1)
            hi_win(2)
            act.wait_ge(par_loaded, 16)
            act.activation(sp_tmp[:, 0, :], par[:, C_AP:C_AP + KT], ACT.Abs).then_inc(act_step, 1)
            act.wait_ge(act_step, 1)
            act.activation(sp_tmp[:, 0, :], sp_tmp[:, 0, :], ACT.Exp, scale=-1.0
                           ).then_inc(act_step, 1)
            act.wait_ge(pool_step, 2)
            for n in range(LRU_BLOCKS):
                s = PER * n
                act.wait_ge(wg_loaded, 16 * (n + 1))
                if n:
                    act.wait_ge(tile_done, s)
                act.activation(wg_hi[:, :, :], wg_raw[:, :, :], ACT.Copy).then_inc(wg_hi_ready, 1)
                for j in range(2 * LT):
                    q = 2 * LT * n + j
                    src = psum_tile(s + j)
                    ch = n * LT + j % LT
                    if j < LT:
                        if n:
                            act.wait_ge(conv_done, LT * (n - 1) + j + 1)
                        act.activation(rows3(xr[:, j, CONV - 1:]), src, ACT.Identity,
                                       bias=par[:, C_BIN + KT + ch:C_BIN + KT + ch + 1]
                                       ).then_inc(tile_read, 1)
                    else:
                        act.activation(rows3(zT[:, ch, :]), src, ACT.Gelu_apprx_tanh,
                                       bias=par[:, C_BIN + ch:C_BIN + ch + 1]
                                       ).then_inc(tile_read, 1)
                    if q + NW < N_IN:
                        hi_win(q + NW)
                if n:
                    act.wait_ge(scan_done, LT * n)
                for j in range(2 * LT, PER):
                    c = j % LT
                    to = gate_x if j < 3 * LT else gate_a
                    b = C_BG + n * 2 * LT + j - 2 * LT
                    src = psum_tile(s + j)
                    act.activation(rows3(to[:, c, :]), src, ACT.Sigmoid, bias=par[:, b:b + 1]
                                   ).then_inc(tile_read, 1)
                act.wait_ge(tile_read, s + PER)
                if n == 0:
                    act.wait_ge(coef_ready, 1)
                    act.wait_ge(list_cleared, 16)
                for c in range(LT):
                    ch = n * LT + c
                    act.activation(decay[:, c, :], gate_a[:, c, :], ACT.Exp,
                                   scale=lru_coef[:, 0, ch:ch + 1])
                    act.activation(th[:, c, :], gate_a[:, c, :], ACT.Tanh,
                                   scale=lru_coef[:, 1, ch:ch + 1]).then_inc(th_ready, 1)
                for c in range(LT):
                    act.wait_ge(mult2_ready, LT * n + c + 1)
                    act.activation(th[:, c, :], th[:, c, :], ACT.Sqrt).then_inc(mult_ready, 1)

        @block.vector
        def _(dve):
            s = Chain(dve, dve_step)
            dve.wait_ge(pool_step, 1)
            for k in range(KT):
                dve.wait_ge(hT_hi_ready, k + 1)
                dve.tensor_tensor(hT_lo[:, k, :], hT_raw[:, k, :], hT_hi[:, k, :].bitcast(F32),
                                  ALU.subtract).then_inc(hT_lo_ready, 1)
            dve.wait_ge(places_ready, 2)
            for what, (first, window) in enumerate(((L, PAD // TOP_K), (PAIRS, PAD))):
                s.step(dve.tensor_scalar(pads[:, :, what], pads[:, :, what], window - 1, None,
                                         ALU.bitwise_and))
                dve.tensor_scalar(pads[:, :, what], pads[:, :, what], first, None, ALU.add
                                  ).then_inc(pads_ready, 1)
            a, e, r, q2 = par[:, C_AP:C_AP + KT], sp_tmp[:, 0, :], sp_tmp[:, 1, :], sp_tmp[:, 2, :]
            v = sp_tmp[:, 3, :]
            dve.wait_ge(act_step, 2)
            dve.wait_ge(par_loaded, 16)
            s.step(dve.tensor_scalar(r, e, 2.0, None, ALU.add))
            s.step(dve.reciprocal(r, r))
            s.step(dve.tensor_tensor(r, e, r, ALU.mult))
            s.step(dve.tensor_tensor(q2, r, r, ALU.mult))
            s.step(dve.tensor_scalar(v, q2, 1.0 / 19, 1.0 / 17, ALU.mult, ALU.add))
            for d in (15, 13, 11, 9, 7, 5, 3, 1):
                s.step(dve.tensor_tensor(v, v, q2, ALU.mult))
                s.step(dve.tensor_scalar(v, v, 1.0 / d, None, ALU.add))
            s.step(dve.scalar_tensor_tensor(v, v, 2.0, r, ALU.mult, ALU.mult))
            s.step(dve.tensor_scalar(r, a, -1.0, 0.0, ALU.mult, ALU.max))
            s.step(dve.tensor_tensor(v, v, r, ALU.add))
            s.step(dve.tensor_scalar(lru_coef[:, 0, :], v, -LRU_C, None, ALU.mult))
            dve.tensor_scalar(lru_coef[:, 1, :], v, LRU_C, None, ALU.mult).then_inc(coef_ready, 1)

            for n in range(LRU_BLOCKS):
                for c in range(LT):
                    ch = n * LT + c
                    cw = lambda k: par[:, C_CW + k * KT + ch:C_CW + k * KT + ch + 1]
                    dve.wait_ge(tile_read, PER * n + c + 1)
                    s.step(dve.tensor_scalar(xc[:, c, :], xr[:, c, 0:LP], cw(0),
                                             par[:, C_CB + ch:C_CB + ch + 1], ALU.mult, ALU.add))
                    for k in range(1, CONV):
                        s.step(dve.scalar_tensor_tensor(xc[:, c, :], xr[:, c, k:k + LP], cw(k),
                                                        xc[:, c, :], ALU.mult, ALU.add))
                    dve.tensor_copy(xc_hi[:, c, :], xc[:, c, :]).then_inc(conv_done, 1)
                    dve.wait_ge(conv_done, ch + 1)
                    dve.tensor_tensor(xc_lo[:, c, :], xc[:, c, :], xc_hi[:, c, :].bitcast(F32),
                                      ALU.subtract).then_inc(xc_split, 1)
                for c in range(LT):
                    dve.wait_ge(th_ready, LT * n + c + 1)
                    s.step(dve.tensor_scalar(gate_a[:, c, :], th[:, c, :], 1.0, None, ALU.add))
                    s.step(dve.reciprocal(gate_a[:, c, :], gate_a[:, c, :]))
                    dve.scalar_tensor_tensor(th[:, c, :], th[:, c, :], 2.0, gate_a[:, c, :],
                                             ALU.mult, ALU.mult).then_inc(mult2_ready, 1)
                for c in range(LT):
                    s.step(dve.tensor_tensor(gate_x[:, c, :], xc[:, c, :], gate_x[:, c, :],
                                             ALU.mult))
                    dve.wait_ge(mult_ready, LT * n + c + 1)
                    s.step(dve.tensor_tensor(gate_x[:, c, :], gate_x[:, c, :], th[:, c, :],
                                             ALU.mult))
                    s.step(dve.tensor_tensor_scan(xc[:, c, :], decay[:, c, :], gate_x[:, c, :],
                                                  0.0, ALU.mult, ALU.add))
                    ch = n * LT + c
                    dve.tensor_tensor(zT[:, ch, :], zT[:, ch, :], xc[:, c, :], ALU.mult
                                      ).then_inc(scan_done, 1)
            dve_steps.append(s.n)

    wout_hi_ready, wout_lo_ready = sem("wout_hi_ready"), sem("wout_lo_ready")
    b_loaded = sem("b_loaded")
    h_loaded, h_used = sem("h_loaded"), sem("h_used")
    z_hi_ready, z_lo_ready = sem("z_hi_ready"), sem("z_lo_ready")
    z_clear = sem("z_clear")
    mix_ready, var_ready, std_ready = sem("mix_ready"), sem("var_ready"), sem("std_ready")
    centred, norm_ready = sem("centred"), sem("norm_ready")
    turned, h1T_moved = sem("turned"), sem("h1T_moved")
    logits_ready, scores_ready = sem("logits_ready"), sem("scores_ready")
    mask_ready, rank_ready, rank_read = sem("mask_ready"), sem("rank_ready"), sem("rank_read")
    h1_stored = sem("h1_stored")
    place_ready, listed = sem("place_ready"), sem("listed")
    pool_steps = pool_n[0]

    cols = lambda i: slice(i * P, i * P + ROWS[i])

    with nc.Block() as block:
        @block.sync
        def _(sp):
            sp.dma_start(ln_b[:, :, :], ln[0:2, :].unsqueeze(0).to_broadcast([P, 2, D])
                         ).then_inc(b_loaded, 16)
            sp.dma_start(rw[:, :, :], router_w.rearrange("(k p) e -> p k e", p=P)
                         ).then_inc(b_loaded, 16)
            sp.dma_start(rbias[:, :], router_b.to_broadcast([P, E])).then_inc(b_loaded, 16)
            for i, r in enumerate(ROWS):
                if i:
                    sp.wait_ge(h_used, i)
                sp.dma_start(h_in[0:r, :], h_rows[i * P:i * P + r, :]).then_inc(h_loaded, 16)
                if i >= 1:
                    sp.wait_ge(norm_ready, i)
                    sp.dma_start(h1_rows[cols(i - 1), :], h1[0:ROWS[i - 1], i - 1, :]
                                 ).then_inc(h1_stored, 16)
            i = TILES - 1
            sp.wait_ge(norm_ready, TILES)
            sp.dma_start(h1_rows[cols(i), :], h1[0:ROWS[i], i, :]).then_inc(h1_stored, 16)

        @block.gpsimd
        def _(pool):
            s = Chain(pool, pool_step)
            s.n = pool_steps
            pool.memset(h1T[:, :, L:LP], 0.0).then_inc(z_clear, 1)
            pool.wait_ge(list_cleared, 16)

            def enlist(i):
                r = ROWS[i]
                pool.wait_ge(place_ready, i + 1)
                for j in range(TOP_K):
                    pool.indirect_dma_start(
                        out=pair_list,
                        out_offset=bass.IndirectOffsetOnAxis(ap=place[0:r, i, j:j + 1], axis=0),
                        in_=pair_id[0:r, i, j, :], in_offset=None).then_inc(listed, 16)

            for i, r in enumerate(ROWS):
                pool.wait_ge(centred, i + 1)
                if i == 0:
                    pool.wait_ge(b_loaded, 48)
                s.step(pool.tensor_tensor(h1[0:r, i, :], h1[0:r, i, :], ln_b[0:r, 0, :], ALU.mult))
                pool.tensor_tensor(h1[0:r, i, :], h1[0:r, i, :], ln_b[0:r, 1, :], ALU.add
                                   ).then_inc(norm_ready, 1)
                if i >= 4:
                    enlist(i - 4)
            for i in range(TILES - 4, TILES):
                enlist(i)
            pool.wait_ge(listed, 16 * TILES * TOP_K)
            pool_n[0] = s.n

        @block.tensor
        def _(pe):
            def mix(i):
                if i >= 2:
                    pe.wait_ge(h_used, i - 1)
                pe.wait_ge(z_hi_ready, i + 1)
                pe.wait_ge(z_lo_ready, i + 1)
                for k in range(KT):
                    if i == 0:
                        pe.wait_ge(wout_hi_ready, k + 1)
                        pe.wait_ge(wout_lo_ready, k + 1)
                    for n in range(2):
                        mm = split_product(pe, bank[:, 2 * (i % 2) + n, :],
                                           (z_hi[i % 2][:, k, :], z_lo[i % 2][:, k, :]),
                                           [w[:, k, n * 512:(n + 1) * 512]
                                            for w in (wout_hi, wout_lo)], k == 0, k == KT - 1)
                mm.then_inc(mix_ready, 1)

            def turn(i):
                r = ROWS[i]
                pe.wait_ge(norm_ready, i + 1)
                if i == 0:
                    pe.wait_ge(consts_ready, 1)
                if i:
                    pe.wait_ge(h1T_moved, i)
                for k in range(KT):
                    mm = pe.transpose(bank[:, 4 + k // 4, (k % 4) * P:(k % 4) * P + r],
                                      h1[0:r, i, k * P:(k + 1) * P], ident[0:r, 0:r])
                mm.then_inc(turned, 1)

            def logits(i):
                r = ROWS[i]
                pe.wait_ge(h1T_moved, i + 1)
                if i == 0:
                    pe.wait_ge(b_loaded, 48)
                if i >= 2:
                    pe.wait_ge(rank_read, i - 1)
                for k in range(KT):
                    mm = pe.matmul(bank[0:r, 6 + i % 2, 0:E], h1T[:, k, cols(i)], rw[:, k, :],
                                   start=(k == 0), stop=(k == KT - 1))
                mm.then_inc(logits_ready, 1)

            def rank(i):
                r = ROWS[i]
                pe.wait_ge(mask_ready, i + 1)
                pe.matmul(bank[0:r, 6 + i % 2, E:2 * E], ones[:, 0:r], cum[:, i % 2, :],
                          start=True, stop=False)
                pe.matmul(bank[0:r, 6 + i % 2, E:2 * E], tri[0:r, 0:r], mask[0:r, :],
                          start=False, stop=True).then_inc(rank_ready, 1)

            for i in range(TILES + 3):
                if i < TILES:
                    mix(i)
                if 0 <= i - 1 < TILES:
                    turn(i - 1)
                if 0 <= i - 2 < TILES:
                    logits(i - 2)
                if 0 <= i - 3:
                    rank(i - 3)

        @block.scalar
        def _(act):
            def split_z(i):
                r = ROWS[i]
                if i >= 2:
                    act.wait_ge(mix_ready, i - 1)
                act.activation(z_hi[i % 2][:, :, 0:r], zT[:, :, cols(i)], ACT.Copy
                               ).then_inc(z_hi_ready, 1)

            split_z(0)
            act.wait_ge(wout_loaded, 16)
            for k in range(KT):
                act.activation(wout_hi[:, k, :], wout_raw[:, k, :], ACT.Copy
                               ).then_inc(wout_hi_ready, 1)
            split_z(1)
            for i in range(TILES + 2):
                if i < TILES:
                    r = ROWS[i]
                    act.wait_ge(var_ready, i + 1)
                    act.activation(rstd[0:r, 0:1], rstd[0:r, 0:1], ACT.Sqrt).then_inc(std_ready, 1)
                if i + 2 < TILES:
                    split_z(i + 2)
                if 0 <= i - 1 < TILES:
                    t, r = i - 1, ROWS[i - 1]
                    act.wait_ge(turned, t + 1)
                    if t == 0:
                        act.wait_ge(z_clear, 1)
                    act.activation(h1T[:, :, cols(t)],
                                   bank[:, 4:6, :].rearrange("p b (k t) -> p (b k) t", t=P)[:, :, 0:r],
                                   ACT.Copy).then_inc(h1T_moved, 1)
                if 0 <= i - 2:
                    t, r = i - 2, ROWS[i - 2]
                    act.wait_ge(logits_ready, t + 1)
                    if t:
                        act.wait_ge(mask_ready, t)
                    act.activation(scores[0:r, :], bank[0:r, 6 + t % 2, 0:E], ACT.Sigmoid
                                   ).then_inc(scores_ready, 1)

        @block.vector
        def _(dve):
            s = Chain(dve, dve_step)
            s.n = dve_steps[-1]

            def split_z(i):
                r = ROWS[i]
                dve.wait_ge(z_hi_ready, i + 1)
                dve.tensor_tensor(z_lo[i % 2][:, :, 0:r], zT[:, :, cols(i)],
                                  z_hi[i % 2][:, :, 0:r].bitcast(F32), ALU.subtract
                                  ).then_inc(z_lo_ready, 1)

            def norm_begin(i):
                r = ROWS[i]
                dve.wait_ge(mix_ready, i + 1)
                dve.wait_ge(h_loaded, 16 * (i + 1))
                dve.scalar_tensor_tensor(
                    h1[0:r, i, :].rearrange("p (b n) -> p b n", b=2),
                    h_in[0:r, :].rearrange("p (b n) -> p b n", b=2), ALPHA,
                    bank[0:r, 2 * (i % 2):2 * (i % 2) + 2, :], ALU.mult, ALU.add
                    ).then_inc(h_used, 1)
                dve.wait_ge(h_used, i + 1)
                s.step(dve.bn_stats(stats[0:r, 0, :], h1[0:r, i, 0:512]))
                s.step(dve.bn_stats(stats[0:r, 1, :], h1[0:r, i, 512:D]))
                s.step(dve.bn_aggr(mv[0:r, :], stats[0:r, :, :]))
                dve.tensor_scalar(rstd[0:r, 0:1], mv[0:r, 1:2], LN_EPS, None, ALU.add
                                  ).then_inc(var_ready, 1)

            def norm_end(i):
                r = ROWS[i]
                dve.wait_ge(std_ready, i + 1)
                s.step(dve.reciprocal(rstd[0:r, 1:2], rstd[0:r, 0:1]))
                dve.tensor_scalar(h1[0:r, i, :], h1[0:r, i, :], mv[0:r, 0:1], rstd[0:r, 1:2],
                                  ALU.subtract, ALU.mult).then_inc(centred, 1)

            def route(i):
                r = ROWS[i]
                sm = lambda j: small[0:r, j, :]
                dve.wait_ge(scores_ready, i + 1)
                s.step(dve.tensor_tensor(choice[0:r, :], scores[0:r, :], rbias[0:r, :], ALU.add))
                for g in range(GROUPS):
                    ins = dve.max(top_of[0:r, g, :], choice[0:r, g * GSIZE:(g + 1) * GSIZE])
                s.step(ins)
                s.step(dve.tensor_tensor(sm(0), top_of[0:r, :, 0], top_of[0:r, :, 1], ALU.add))
                s.step(dve.max(sm(1), sm(0)))
                s.step(dve.max_index(idx_u[0:r, 0, :], sm(1), sm(0)))
                s.step(dve.tensor_copy(sm(2), idx_u[0:r, 0, :]))
                s.step(dve.tensor_tensor(
                    ghot[0:r, :, :],
                    iota_e[0:r, 0:GROUPS].unsqueeze(1).to_broadcast([r, TOP_GROUPS, GROUPS]),
                    sm(2)[:, 0:TOP_GROUPS].unsqueeze(2).to_broadcast([r, TOP_GROUPS, GROUPS]),
                    ALU.is_equal))
                s.step(dve.tensor_reduce(sm(3), ghot[0:r, :, :].rearrange("p j g -> p g j"), AX,
                                         ALU.add))
                s.step(dve.tensor_scalar(sm(4), sm(3), -1.0, BIG, ALU.add, ALU.mult))
                by_group = choice[0:r, :].rearrange("p (g m) -> p g m", g=GROUPS)
                wide = lambda v: v.unsqueeze(2).to_broadcast([r, GROUPS, GSIZE])
                s.step(dve.tensor_tensor(by_group, by_group, wide(sm(3)), ALU.mult))
                s.step(dve.tensor_tensor(by_group, by_group, wide(sm(4)), ALU.add))
                s.step(dve.max(sm(5), choice[0:r, :]))
                s.step(dve.max_index(idx_u[0:r, 1, :], sm(5), choice[0:r, :]))
                s.step(dve.tensor_copy(expert[0:r, :], idx_u[0:r, 1, :]))
                s.step(dve.tensor_tensor(
                    hot[0:r, :, :], iota_e[0:r, :].unsqueeze(1).to_broadcast([r, TOP_K, E]),
                    expert[0:r, :].unsqueeze(2).to_broadcast([r, TOP_K, E]), ALU.is_equal))
                s.step(dve.tensor_tensor(
                    picked[0:r, :, :], hot[0:r, :, :],
                    scores[0:r, :].unsqueeze(1).to_broadcast([r, TOP_K, E]), ALU.mult))
                s.step(dve.tensor_reduce(sm(7), picked[0:r, :, :], AX, ALU.add))
                s.step(dve.tensor_reduce(sm(8)[:, 0:1], sm(7), AX, ALU.add))
                s.step(dve.tensor_scalar(sm(8)[:, 1:2], sm(8)[:, 0:1], 1e-20, None, ALU.add))
                s.step(dve.reciprocal(sm(8)[:, 2:3], sm(8)[:, 1:2]))
                s.step(dve.tensor_scalar(weight[0:r, i, :], sm(7), sm(8)[:, 2:3], ROUTED_SCALE,
                                         ALU.mult, ALU.mult))
                with nc.allow_low_precision(reason="at most one 1 is summed"):
                    dve.tensor_reduce(mask[0:r, :], hot[0:r, :, :].rearrange("p j e -> p e j"),
                                      AX, ALU.add).then_inc(mask_ready, 1)

            def places(i):
                r = ROWS[i]
                dve.wait_ge(rank_ready, i + 1)
                dve.tensor_tensor(rowval[0:r, :], list_start[0:r, :],
                                  bank[0:r, 6 + i % 2, E:2 * E], ALU.add).then_inc(rank_read, 1)
                dve.wait_ge(rank_read, i + 1)
                if i + 1 < TILES:
                    s.step(dve.tensor_tensor(cum[:, (i + 1) % 2, :], cum[:, i % 2, :],
                                             mask[:, :], ALU.add))
                s.step(dve.tensor_tensor(
                    picked[0:r, :, :], hot[0:r, :, :],
                    rowval[0:r, :].unsqueeze(1).to_broadcast([r, TOP_K, E]), ALU.mult))
                s.step(dve.tensor_reduce(small[0:r, 9, :], picked[0:r, :, :], AX, ALU.add))
                dve.tensor_copy(place[0:r, i, :], small[0:r, 9, :]).then_inc(place_ready, 1)

            dve.wait_ge(consts_ready, 1)
            dve.wait_ge(b_loaded, 48)
            split_z(0)
            for k in range(KT):
                dve.wait_ge(wout_hi_ready, k + 1)
                dve.tensor_tensor(wout_lo[:, k, :], wout_raw[:, k, :],
                                  wout_hi[:, k, :].bitcast(F32), ALU.subtract
                                  ).then_inc(wout_lo_ready, 1)
            split_z(1)
            for i in range(TILES + 3):
                if i < TILES:
                    norm_begin(i)
                if 0 <= i - 3:
                    places(i - 3)
                if i < TILES:
                    norm_end(i)
                if 0 <= i - 2 < TILES:
                    route(i - 2)
                if i + 2 < TILES:
                    split_z(i + 2)
            dve_steps.append(s.n)

    sh_loaded = sem("sh_loaded")
    count_ready = sem("count_ready")
    sched_ready, sched_stored, sched_loaded = (sem("sched_ready"), sem("sched_stored"),
                                               sem("sched_loaded"))
    sh_up, sh_act, sh_ready = sem("sh_up"), sem("sh_act"), sem("sh_ready")
    sh_down_done, sh_read = sem("sh_down_done"), sem("sh_read")
    hid_clear = sem("hid_clear")
    x_turned, up_done, down_done = sem("x_turned"), sem("up_done"), sem("down_done")
    pair_free = sem("pair_free")
    xT_moved, hid_ready, hid_step = sem("xT_moved"), sem("hid_ready"), sem("hid_step")
    y_act, y_dve, ysb_free = sem("y_act"), sem("y_dve"), sem("ysb_free")
    y_stored = [sem(f"y_stored{j}") for j in range(2)]
    rows3 = lambda a: a.rearrange("p (c t) -> p c t", c=3)
    DOWN_BANKS = [6, 0, 2]

    with nc.Block() as block:
        @block.sync
        def _(sp):
            sp.dma_start(sgu[:, :, :], sh_gu.rearrange("(k p) c -> p k c", p=P)
                         ).then_inc(sh_loaded, 16)
            sp.dma_start(sdn[:, :, :], sh_down.rearrange("(k p) c -> p k c", p=P)
                         ).then_inc(sh_loaded, 16)
            sp.wait_ge(hid_clear, 1)
            sp.dma_start(h1_rows[L:, :].rearrange("(p r) (b n) -> p (r b) n", p=P, b=2),
                         hid_hi[:, :, :].bitcast(F32).rearrange("p f t -> p (f t)").unsqueeze(1)
                         .to_broadcast([P, 2 * PAD // TOP_K // P, 512])).then_inc(h1_stored, 16)
            sp.wait_ge(sched_ready, 3)
            sp.dma_start(sched_dram, sched_i[:, :]).then_inc(sched_stored, 16)
            sp.wait_ge(sched_stored, 16)
            sp.dma_start(sched_row[:, :], sched_dram.rearrange("(o b) c -> o (b c)", o=1)
                         ).then_inc(sched_loaded, 16)
            sp.wait_ge(sched_loaded, 16)
            sp.wait_ge(h1_stored, 16 * TILES + 16)

        @block.gpsimd
        def _(pool):
            pool.memset(hid_hi[:, :, :].bitcast(F32), 0.0).then_inc(hid_clear, 1)
            pool.memset(hid_lo[:, :, :].bitcast(F32), 0.0).then_inc(hid_clear, 1)

        @block.tensor
        def _(pe):
            r, t = ROWS[-1], TILES - 1
            pe.matmul(bank[:, 7, 0:E], ones[:, :], cum[:, t % 2, :], start=True, stop=False)
            pe.matmul(bank[:, 7, 0:E], ones[0:r, :], mask[0:r, :], start=False, stop=True
                      ).then_inc(count_ready, 1)
            pe.wait_ge(sh_loaded, 32)
            for f in range(FT):
                if f:
                    pe.wait_ge(sh_act, f)
                    pe.wait_ge(sh_ready, f)
                for half in range(2):
                    for k in range(KT):
                        for c in range(3):
                            mm = pe.matmul(bank[:, 3 * half + c, 0:CHUNK],
                                           sgu[:, k, half * F + f * P:half * F + (f + 1) * P],
                                           h1T[:, k, c * CHUNK:(c + 1) * CHUNK],
                                           start=(k == 0), stop=(k == KT - 1))
                    mm.then_inc(sh_up, 1)
            pe.wait_ge(sh_ready, FT)
            pe.wait_ge(sched_ready, 1)
            for i, r in enumerate(ROWS):
                b = DOWN_BANKS[i % 3]
                if i >= 3:
                    pe.wait_ge(sh_read, i - 2)
                for n in range(2):
                    for k in range(FT):
                        mm = pe.matmul(bank[0:r, b + n, :], sh[:, k, cols(i)],
                                       sdn[:, k, n * 512:(n + 1) * 512],
                                       start=(k == 0), stop=(k == FT - 1))
                mm.then_inc(sh_down_done, 1)

        @block.scalar
        def _(act):
            for f in range(FT):
                act.wait_ge(sh_up, 2 * f + 1)
                act.activation(rows3(sg[:, f, :]), bank[:, 0:3, 0:CHUNK], ACT.Silu
                               ).then_inc(sh_act, 1)

        @block.vector
        def _(dve):
            s = Chain(dve, dve_step)
            s.n = dve_steps[-1]
            n_tok, n_blk, ends, done, part, one = (cnt[:, j, :] for j in range(6))
            sc = lambda j: sched[:, j:j + 1]
            dve.wait_ge(count_ready, 1)
            dve.tensor_copy(n_tok, bank[:, 7, 0:E]).then_inc(sched_ready, 1)
            dve.wait_ge(sched_ready, 1)
            s.step(dve.tensor_scalar(n_blk, n_tok, float(BLOCK), 1.0, ALU.is_gt, ALU.add))
            for k in range(2, NB_MAX):
                s.step(dve.scalar_tensor_tensor(n_blk, n_tok, float(k * BLOCK), n_blk, ALU.is_gt,
                                                ALU.add))
            s.step(dve.memset(one, 1.0))
            s.step(dve.tensor_tensor_scan(ends, one, n_blk, 0.0, ALU.mult, ALU.add))
            s.step(dve.tensor_scalar(done, ends, block_id[:, 0:1], None, ALU.is_le))
            s.step(dve.tensor_reduce(sc(0), done, AX, ALU.add))
            s.step(dve.tensor_tensor(part, n_blk, done, ALU.mult))
            s.step(dve.tensor_reduce(sc(1), part, AX, ALU.add))
            s.step(dve.tensor_tensor(sc(2), block_id[:, 0:1], sc(1), ALU.subtract))
            s.step(dve.tensor_scalar(sc(3), sc(0), float(STRIDE), None, ALU.mult))
            s.step(dve.scalar_tensor_tensor(sc(4), sc(2), float(BLOCK), sc(3), ALU.mult, ALU.add))
            s.step(dve.tensor_scalar(sc(5), sc(0), float(E - 1), None, ALU.min))
            s.step(dve.tensor_copy(sched_i[:, 0:1], sc(4)))
            s.step(dve.tensor_copy(sched_i[:, 1:2], sc(5)))
            s.step(dve.tensor_scalar(sc(6), ends[:, E - 1:E], 1.0, None, ALU.add))
            s.step(dve.tensor_copy(sched_i[:, 3:4], sc(6)))
            s.step(dve.tensor_scalar(sched_i[:, 2:3], sched_i[:, 3:4], 1, 1,
                                     ALU.logical_shift_right, ALU.logical_shift_left))
            dve.sem_inc(sched_ready, 2)
            for done_sem, count in ((up_done, SEED), (down_done, SEED), (x_turned, SEED),
                                    (pair_free, 2), (xT_moved, 1), (hid_ready, FT),
                                    (hid_step, FT), (y_act, 2), (y_dve, 2), (ysb_free, 2)):
                dve.sem_inc(done_sem, count)
            for f in range(FT):
                dve.wait_ge(sh_act, f + 1)
                dve.wait_ge(sh_up, 2 * f + 2)
                dve.tensor_tensor(rows3(sh[:, f, :]), rows3(sg[:, f, :]), bank[:, 3:6, 0:CHUNK],
                                  ALU.mult).then_inc(sh_ready, 1)
            for i, r in enumerate(ROWS):
                b = DOWN_BANKS[i % 3]
                dve.wait_ge(sh_down_done, i + 1)
                if i == 0:
                    dve.wait_ge(h1_stored, 16 * TILES)
                halves = h1[0:r, i, :].rearrange("p (b n) -> p b n", b=2)
                dve.scalar_tensor_tensor(halves, halves, ALPHA, bank[0:r, b:b + 2, :],
                                         ALU.mult, ALU.add).then_inc(sh_read, 1)
            dve.wait_ge(sh_read, TILES)
            dve_steps.append(s.n)

    wgu_loaded = [sem(f"wgu_loaded{j}") for j in range(2)]
    wd_loaded = [sem(f"wd_loaded{j}") for j in range(2)]
    pair_loaded = [sem(f"pair_loaded{j}") for j in range(2)]
    gathered = [sem(f"gathered{j}") for j in range(2)]
    wd_hi_ready, wd_lo_ready = sem("wd_hi_ready"), sem("wd_lo_ready")
    gate_ready, dve_hi = sem("gate_ready"), sem("dve_hi")

    sp_pass, pool_pass = sem("sp_pass"), sem("pool_pass")

    def blocks_to_run(eng):
        return eng.value_load(sched_row[0:1, 2:3], min_val=E, max_val=T_MAX + 1)

    def of_block(eng, t, what, top):
        return eng.value_load(sched_row[0:1, bass.ds(t * 4 + what, 1)], min_val=0, max_val=top)

    with nc.Block() as block:
        @block.sync
        def _(sp):
            n = blocks_to_run(sp)
            with sp.Fori(0, n + 2, 2) as i:
                for b in range(2):
                    t = i + b
                    row = of_block(sp, t, 0, LIST - BLOCK)
                    sp.wait_ge(pair_free, t + 1)
                    sp.sem_inc(sp_pass, 1)
                    sp.dma_start(pair[b][:, 0, :], pair_list[bass.ds(row, P), :]
                                 ).then_inc(pair_loaded[b], 16)
                    sp.dma_start(pair[b][0:REST, 1, :], pair_list[bass.ds(row + P, REST), :]
                                 ).then_inc(pair_loaded[b], 16)
                    e = of_block(sp, t, 1, E - 1)
                    sp.wait_ge(up_done, t * STEPS + STEPS)
                    sp.sem_inc(sp_pass, 1)
                    sp.dma_start(wgu[b][:, :, :],
                                 w_gu[bass.ds(e, 1)].rearrange("o (k p) c -> p (o k) c", p=P)
                                 ).then_inc(wgu_loaded[b], 16)
                    sp.wait_ge(down_done, t * STEPS + STEPS)
                    sp.sem_inc(sp_pass, 1)
                    sp.dma_start(wd_raw[b][:, :, :],
                                 w_down[bass.ds(e, 1)].rearrange("o (k p) c -> p (o k) c", p=P)
                                 ).then_inc(wd_loaded[b], 16)

        @block.gpsimd
        def _(pool):
            def fetch(t, b, i):
                pool.wait_ge(pair_loaded[b], i * 16 + 32)
                pool.wait_ge(x_turned, t * STEPS + STEPS)
                pool.sem_inc(pool_pass, 1)
                for half, r in enumerate((P, REST)):
                    pool.indirect_dma_start(
                        out=xg[b][0:r, half, :], out_offset=None, in_=h1_rows,
                        in_offset=bass.IndirectOffsetOnAxis(ap=pair[b][0:r, half, 0:1],
                                                            axis=0)).then_inc(gathered[b], 16)
                pool.wait_ge(gathered[b], i * 16 + 32)
                pool.sem_inc(pool_pass, 1)
                pool.tensor_copy(to_row[b][:, :], pair[b][:, :, 1]).then_inc(pair_free, 1)

            n = blocks_to_run(pool)
            pool.wait_ge(hid_clear, 2)
            fetch(0, 0, 0)
            with pool.Fori(0, n, 2) as i:
                for b in range(2):
                    t = i + b
                    fetch(t + 1, 1 - b, i + 2 * b)
                    pool.wait_ge(pair_free, t + 4)
                    pool.wait_ge(y_act, t * 2 + 4)
                    pool.wait_ge(y_dve, t * 2 + 4)
                    pool.sem_inc(pool_pass, 1)
                    for half, r in enumerate((P, REST)):
                        pool.indirect_dma_start(
                            out=pair_rows,
                            out_offset=bass.IndirectOffsetOnAxis(ap=to_row[b][0:r, half:half + 1],
                                                                 axis=0),
                            in_=ysb[b][0:r, half, :], in_offset=None).then_inc(y_stored[b], 16)
                    pool.wait_ge(y_stored[b], i * 16 + 32)
                    pool.sem_inc(ysb_free, 1)

        @block.tensor
        def _(pe):
            def turn(t, b, i):
                pe.wait_ge(gathered[b], i * 16 + 32)
                for q in range(QX):
                    pe.wait_ge(xT_moved, t * QX + max(q, 1))
                    for k in (2 * q, 2 * q + 1):
                        o = (k % 2) * BLOCK
                        pe.transpose(bank[:, 4 + q % 2, o:o + P], xg[b][:, 0, k * P:(k + 1) * P],
                                     ident[:, :])
                        mm = pe.transpose(bank[:, 4 + q % 2, o + P:o + BLOCK],
                                          xg[b][0:REST, 1, k * P:(k + 1) * P],
                                          ident[0:REST, 0:REST])
                    mm.then_inc(x_turned, 1)

            n = blocks_to_run(pe)
            turn(0, 0, 0)
            with pe.Fori(0, n, 2) as i:
                for b in range(2):
                    t = i + b
                    pe.wait_ge(wgu_loaded[b], i * 8 + 16)
                    pe.wait_ge(xT_moved, t * QX + QX + 1)
                    pe.wait_ge(hid_ready, t * 2 + 2)
                    for f in range(FT):
                        for half in range(2):
                            for k in range(KT):
                                mm = pe.matmul(
                                    bank[:, 2 * f + half, 0:BLOCK],
                                    wgu[b][:, k, half * F + f * P:half * F + (f + 1) * P],
                                    xT[:, k, :], start=(k == 0), stop=(k == KT - 1))
                            mm.then_inc(up_done, 1)
                    turn(t + 1, 1 - b, i + 2 * b)
                    pe.wait_ge(wd_hi_ready, t + 1)
                    pe.wait_ge(wd_lo_ready, t + 1)
                    pe.wait_ge(hid_ready, t * 2 + 4)
                    for half in range(2):
                        for c in range(2):
                            pe.wait_ge((y_act, y_dve)[c], t * 2 + half + 2)
                            for k in range(FT):
                                mm = split_product(
                                    pe, bank[:, 6 + c, :],
                                    [h[:, k, half * P:(half + 1) * P] for h in (hid_hi, hid_lo)],
                                    [w[b][:, k, c * 512:(c + 1) * 512] for w in (wd_hi, wd_lo)],
                                    k == 0, k == FT - 1)
                            mm.then_inc(down_done, 1)

        @block.scalar
        def _(act):
            def move_xT(t):
                for q in range(QX):
                    act.wait_ge(x_turned, t * STEPS + SEED + q + 1)
                    act.activation(xT[:, 2 * q:2 * q + 2, :],
                                   bank[:, 4 + q % 2, 0:2 * BLOCK].rearrange(
                                       "p (k t) -> p k t", k=2), ACT.Copy).then_inc(xT_moved, 1)

            n = blocks_to_run(act)
            move_xT(0)
            with act.Fori(0, n, 2) as i:
                for b in range(2):
                    t = i + b
                    act.wait_ge(wd_loaded[b], i * 8 + 16)
                    act.wait_ge(down_done, t * STEPS + SEED)
                    act.activation(wd_hi[b][:, :, :], wd_raw[b][:, :, :], ACT.Copy
                                   ).then_inc(wd_hi_ready, 1)
                    act.wait_ge(hid_step, t * 2 + 2)
                    for f in range(FT):
                        act.wait_ge(up_done, t * STEPS + SEED + 2 * f + 1)
                        act.activation(gact[:, f, :], bank[:, 2 * f, 0:BLOCK], ACT.Silu
                                       ).then_inc(gate_ready, 1)
                    act.wait_ge(up_done, t * STEPS + SEED + STEPS)
                    move_xT(t + 1)
                    act.wait_ge(ysb_free, t + 1)
                    for half, r in enumerate((P, REST)):
                        act.wait_ge(down_done, t * STEPS + SEED + 2 * half + 1)
                        act.activation(ysb[b][0:r, half, 0:512], bank[0:r, 6, :], ACT.Copy
                                       ).then_inc(y_act, 1)

        @block.vector
        def _(dve):
            n = blocks_to_run(dve)
            dve.wait_ge(hid_clear, 2)
            with dve.Fori(0, n, 2) as i:
                for b in range(2):
                    t = i + b
                    dve.wait_ge(wd_hi_ready, t + 1)
                    dve.tensor_tensor(wd_lo[b][:, :, :], wd_raw[b][:, :, :],
                                      wd_hi[b][:, :, :].bitcast(F32), ALU.subtract
                                      ).then_inc(wd_lo_ready, 1)
                    dve.wait_ge(down_done, t * STEPS + SEED)
                    for f in range(FT):
                        dve.wait_ge(gate_ready, t * 2 + f + 1)
                        dve.wait_ge(up_done, t * STEPS + SEED + 2 * f + 2)
                        dve.tensor_tensor(hid[:, f, :], gact[:, f, :], bank[:, 2 * f + 1, 0:BLOCK],
                                          ALU.mult).then_inc(hid_step, 1)
                        dve.wait_ge(hid_step, t * 2 + f + 3)
                        dve.tensor_copy(hid_hi[:, f, 0:BLOCK], hid[:, f, :]).then_inc(dve_hi, 1)
                        dve.wait_ge(dve_hi, t * 2 + f + 1)
                        dve.tensor_tensor(hid_lo[:, f, 0:BLOCK], hid[:, f, :],
                                          hid_hi[:, f, 0:BLOCK].bitcast(F32), ALU.subtract
                                          ).then_inc(hid_ready, 1)
                    dve.wait_ge(ysb_free, t + 1)
                    for half, r in enumerate((P, REST)):
                        dve.wait_ge(down_done, t * STEPS + SEED + 2 * half + 2)
                        dve.tensor_copy(ysb[b][0:r, half, 512:D], bank[0:r, 7, :]
                                        ).then_inc(y_dve, 1)

    lnf_loaded = sem("lnf_loaded")
    stores_done = sem("stores_done")
    got_ready = [sem(f"got_ready{j}") for j in range(2)]
    summed = sem("summed")
    var2_ready, std2_ready, normed2 = sem("var2_ready"), sem("std2_ready"), sem("normed2")
    out_ready, out_stored = sem("out_ready"), sem("out_stored")

    with nc.Block() as block:
        @block.sync
        def _(sp):
            sp.dma_start(ln_f[:, :, :], ln[2:4, :].unsqueeze(0).to_broadcast([P, 2, D])
                         ).then_inc(lnf_loaded, 16)
            def store(i):
                lo = N_META if i == 0 else 0
                sp.wait_ge(out_ready, i + 1)
                sp.dma_start(out[i * P + lo - N_META:i * P + ROWS[i] - N_META, :],
                             h1[lo:ROWS[i], i, :]).then_inc(out_stored, 16)

            sp.wait_ge(stores_done, 1)
            for i, r in enumerate(ROWS):
                if i >= 2:
                    sp.wait_ge(summed, (i - 1) * TOP_K)
                sp.dma_start(got[i % 2][0:r, :, :],
                             pair_rows[i * P * TOP_K:(i * P + r) * TOP_K, :].rearrange(
                                 "(p j) d -> p j d", j=TOP_K)).then_inc(got_ready[i % 2], 16)
                if i:
                    store(i - 1)
            store(TILES - 1)
            sp.wait_ge(out_stored, 16 * TILES)

        @block.gpsimd
        def _(pool):
            n = blocks_to_run(pool)
            for b in range(2):
                pool.wait_ge(y_stored[b], n * 16)
                pool.wait_ge(gathered[b], n * 16 + 32 * (1 - b))
                pool.wait_ge(pair_loaded[b], n * 16 + 32)
                pool.wait_ge(wgu_loaded[b], n * 8 + 16)
                pool.wait_ge(wd_loaded[b], n * 8 + 16)
            pool.sem_inc(stores_done, 1)

        @block.scalar
        def _(act):
            for i, r in enumerate(ROWS):
                act.wait_ge(var2_ready, i + 1)
                act.activation(rstd[0:r, 0:1], rstd[0:r, 0:1], ACT.Sqrt).then_inc(std2_ready, 1)

        @block.vector
        def _(dve):
            s = Chain(dve, dve_step)
            s.n = dve_steps[-1]
            dve.wait_ge(lnf_loaded, 16)
            for i, r in enumerate(ROWS):
                x = h1[0:r, i, :]
                for j in range(TOP_K):
                    q = i * TOP_K + j
                    dve.wait_ge(got_ready[i % 2], 16 * (i // 2 + 1))
                    dve.scalar_tensor_tensor(x, got[i % 2][0:r, j, :], weight[0:r, i, j:j + 1], x,
                                             ALU.mult, ALU.add).then_inc(summed, 1)
                    dve.wait_ge(summed, q + 1)
                s.step(dve.bn_stats(stats[0:r, 0, :], x[:, 0:512]))
                s.step(dve.bn_stats(stats[0:r, 1, :], x[:, 512:D]))
                s.step(dve.bn_aggr(mv[0:r, :], stats[0:r, :, :]))
                dve.tensor_scalar(rstd[0:r, 0:1], mv[0:r, 1:2], LN_EPS, None, ALU.add
                                  ).then_inc(var2_ready, 1)
                dve.wait_ge(std2_ready, i + 1)
                s.step(dve.reciprocal(rstd[0:r, 1:2], rstd[0:r, 0:1]))
                s.step(dve.tensor_scalar(x, x, mv[0:r, 0:1], rstd[0:r, 1:2], ALU.subtract,
                                         ALU.mult))
                s.step(dve.tensor_tensor(x, x, ln_f[0:r, 0, :], ALU.mult))
                dve.tensor_tensor(x, x, ln_f[0:r, 1, :], ALU.add).then_inc(out_ready, 1)


def kernel(x, meta_tokens, rg_w_in, rg_b_in, rg_conv_w, rg_conv_b, rg_w_gates, rg_b_gates,
           rg_a_param, rg_w_out, attn_w_qkv, attn_sinks, attn_w_o, rel_bias_table, ln_gain,
           ln_bias, router_w, router_bias, expert_w_gu, expert_w_down, shared_w_gu,
           shared_w_down):
    import concourse.bacc as bacc
    from concourse.bass_utils import run_bass_kernel_spmd

    h = np.concatenate([np.asarray(meta_tokens), np.asarray(x)[0]], axis=0)
    per_channel = lambda a: np.asarray(a).reshape(-1, P).T
    arrays = {
        "hT": h.T,
        "h_rows": h,
        "w_in": np.asarray(rg_w_in)[0],
        "chan": np.concatenate([per_channel(a) for a in (rg_b_in, rg_conv_w, rg_conv_b,
                                                         rg_b_gates, rg_a_param)], axis=1),
        "w_gates": np.asarray(rg_w_gates)[0],
        "w_out": np.asarray(rg_w_out)[0],
        "ln": np.stack([np.asarray(ln_gain)[0, 0], np.asarray(ln_bias)[0, 0],
                        np.asarray(ln_gain)[0, 1], np.asarray(ln_bias)[0, 1]]),
        "router_w": np.asarray(router_w)[0],
        "router_b": np.asarray(router_bias),
        "w_gu": np.asarray(expert_w_gu)[0],
        "w_down": np.asarray(expert_w_down)[0],
        "sh_gu": np.asarray(shared_w_gu)[0],
        "sh_down": np.asarray(shared_w_down)[0],
    }
    arrays = {k: np.ascontiguousarray(a) for k, a in arrays.items()}
    nc = bacc.Bacc("TRN2", target_bir_lowering=False, num_devices=1)
    args = [nc.dram_tensor(f"in_{k}", a.shape, F32, kind="ExternalInput").ap()
            for k, a in arrays.items()]
    out = nc.dram_tensor("out", (SEQ, D), F32, kind="ExternalOutput").ap()
    build(nc, *args, out)
    r = run_bass_kernel_spmd(nc, [{f"in_{k}": a for k, a in arrays.items()}], core_ids=[0])
    return r.results[0]["out"].reshape(1, SEQ, D)
```

```python
import math

import concourse.bass as bass
import numpy as np
from concourse import mybir
from concourse.alu_op_type import AluOpType as ALU

ACT = mybir.ActivationFunctionType
AX = mybir.AxisListType.X
F32 = mybir.dt.float32
F32R = mybir.dt.float32r
BF16 = mybir.dt.bfloat16
I32 = mybir.dt.int32
U32 = mybir.dt.uint32

P = 128
D = 1024
KT = D // P
N_META = 16
SEQ = 1024
L = N_META + SEQ
CHUNK = 348
LP = 3 * CHUNK
TILES = -(-L // P)
ROWS = [min(P, L - i * P) for i in range(TILES)]
LRU_BLOCKS = 4
LB = D // LRU_BLOCKS
LT = LB // P
CONV = 4
LRU_C = 8.0
E = 64
TOP_K = 8
GROUPS = 8
GSIZE = E // GROUPS
TOP_GROUPS = 4
F = 256
FT = F // P
ROUTED_SCALE = 2.5
ALPHA = 2.0 ** 0.25
LN_EPS = 1e-5
BIG = 3e38

BLOCK = 164
REST = BLOCK - P
NB_MAX = -(-L // BLOCK)
STRIDE = NB_MAX * BLOCK
LIST_COLS = -(-((E + 1) * STRIDE + 2 * BLOCK) // P)
LIST = LIST_COLS * P
T_MAX = E + (L * TOP_K) // BLOCK + 1
PAIRS = L * TOP_K
PAD = 2048
assert PAD >= STRIDE + BLOCK and PAD & (PAD - 1) == 0

QX = KT // 2
STEPS = 4
SEED = 2 * STEPS

GOT = 3
DVE_J = 5
assert STEPS == QX == 2 * FT == 2 * (D // 512)

C_BIN, C_CW, C_CB, C_BG, C_AP = 0, 16, 48, 56, 72
C_N = 80


class SbufMap:

    def __init__(self, nc):
        self.nc = nc
        self.base = -(-nc.sbuf_base // 64) * 64

    def at(self, name, offset, shape, dtype):
        return self.nc.alloc_sbuf_tensor_at(name, list(shape), dtype, offset=self.base + offset)


class Chain:

    def __init__(self, eng, sem):
        self.eng, self.sem, self.n = eng, sem, 0

    def step(self, ins):
        self.n += 1
        ins.then_inc(self.sem, 1)
        self.eng.wait_ge(self.sem, self.n)


def split_product(pe, out, lhs, rhs, first, last):
    pe.matmul(out, lhs[0], rhs[0], start=first, stop=False)
    pe.matmul(out, lhs[0], rhs[1], start=False, stop=False)
    return pe.matmul(out, lhs[1], rhs[0], start=False, stop=last)


def build(nc, hT, h_rows, w_in, chan, w_gates, w_out, ln, router_w, router_b, w_gu, w_down,
          sh_gu, sh_down, out):
    m = SbufMap(nc)
    sem = lambda name: nc.alloc_semaphore(name)
    bank = nc.alloc_psum_tensor("bank", [P, 8, 512], F32)

    h1_rows = nc.dram_tensor("h1_rows", (L + PAD // TOP_K, D), F32).ap()
    pair_list = nc.dram_tensor("pair_list", (LIST, 2), I32).ap()
    pair_rows = nc.dram_tensor("pair_rows", (PAIRS + PAD, D), F32).ap()
    sched_dram = nc.dram_tensor("sched_dram", (P, 4), I32).ap()

    o = 203520
    ident = m.at("ident", o, [P, P], F32)
    tri = m.at("tri", o + 512, [P, P], BF16)
    ones = m.at("ones", o + 768, [P, P], BF16)
    iota_e_i = m.at("iota_e_i", o + 1024, [P, E], I32)
    iota_e = m.at("iota_e", o + 1280, [P, E], F32)
    list_start_i = m.at("list_start_i", o + 1536, [P, E], I32)
    list_start = m.at("list_start", o + 1792, [P, E], F32)
    block_id = m.at("block_id", o + 2112, [P, 1], F32)
    block_id_i = m.at("block_id_i", o + 2144, [P, 1], I32)
    place = m.at("place", o + 2176, [P, TILES, TOP_K], I32)
    weight = m.at("weight", o + 2464, [P, TILES, TOP_K], F32)
    rbias = m.at("rbias", o + 2752, [P, E], F32)
    sched_row = m.at("sched_row", o + 3008, [1, 4 * P], I32)
    par = m.at("par", o + 5056, [P, C_N], F32)
    lru_coef = m.at("lru_coef", o + 5376, [P, 2, KT], F32)
    sp_tmp = m.at("sp_tmp", o + 5440, [P, 4, KT], F32)
    stats = m.at("stats", o + 5568, [P, 2, 6], F32)
    mv = m.at("mv", o + 5632, [P, 2], F32)
    rstd = m.at("rstd", o + 5664, [P, 2], F32)
    mask = m.at("mask", o + 5696, [P, E], BF16)
    cum = m.at("cum", o + 5824, [P, 2, E], BF16)

    pair_id = m.at("pair_id", 212192, [P, TILES, TOP_K, 2], I32)
    pair = [m.at(f"pair{j}", 203328 + 32 * j, [P, 2, 2], I32) for j in range(2)]
    to_row = [m.at(f"to_row{j}", 203392 + 32 * j, [P, 2], I32) for j in range(2)]

    hT_raw = m.at("hT_raw", 0, [P, KT, LP], F32)
    hT_lo = m.at("hT_lo", 0, [P, KT, LP], F32R)
    hT_hi = m.at("hT_hi", 33408, [P, KT, LP], F32R)
    NW = 3
    win_raw = [m.at(f"win_raw{j}", 66816 + 8192 * j, [P, KT, P], F32) for j in range(NW)]
    win_lo = [m.at(f"win_lo{j}", 66816 + 8192 * j, [P, KT, P], F32R) for j in range(NW)]
    win_hi = [m.at(f"win_hi{j}", 66816 + 8192 * j + 4096, [P, KT, P], F32R) for j in range(NW)]
    wg_raw = m.at("wg_raw", 91392, [P, LT, 2 * LB], F32)
    wg_lo = m.at("wg_lo", 91392, [P, LT, 2 * LB], F32R)
    wg_hi = m.at("wg_hi", 91392 + 4096, [P, LT, 2 * LB], F32R)
    zT = m.at("zT", 99584, [P, KT, LP], F32)
    xr = m.at("xr", 132992, [P, LT, LP + CONV - 1], F32)
    xc = m.at("xc", 141376, [P, LT, LP], F32)
    xc_hi = m.at("xc_hi", 149728, [P, LT, LP], F32R)
    xc_lo = m.at("xc_lo", 158080, [P, LT, LP], F32R)
    gate_x = m.at("gate_x", 166432, [P, LT, LP], F32)
    gate_a = m.at("gate_a", 174784, [P, LT, LP], F32)
    decay = m.at("decay", 183136, [P, LT, LP], F32)
    th = m.at("th", 191488, [P, LT, LP], F32)
    pads = m.at("pads", 191488, [P, LIST_COLS, 2], I32)
    wout_raw = m.at("wout_raw", 0, [P, KT, D], F32)
    wout_lo = m.at("wout_lo", 0, [P, KT, D], F32R)
    wout_hi = m.at("wout_hi", 33408, [P, KT, D], F32R)
    z_hi = [m.at(f"z_hi{j}", 66816 + 4096 * j, [P, KT, P], F32R) for j in range(2)]
    z_lo = [m.at(f"z_lo{j}", 75008 + 4096 * j, [P, KT, P], F32R) for j in range(2)]
    h_in = m.at("h_in", 83200, [P, D], F32)
    hot = m.at("hot", 87296, [P, TOP_K, E], F32)
    picked = m.at("picked", 89344, [P, TOP_K, E], F32)
    ln_b = m.at("ln_b", 91392, [P, 2, D], F32)
    rw = m.at("rw", 209600, [P, KT, E], F32)
    scores = m.at("scores", 32768, [P, E], F32)
    choice = m.at("choice", 33024, [P, E], F32)
    top_of = m.at("top_of", 66176, [P, GROUPS, 8], F32)
    rowval = m.at("rowval", 66432, [P, E], F32)
    small = m.at("small", 211648, [P, 10, 8], F32)
    idx_u = m.at("idx_u", 211968, [P, 2, 8], U32)
    ghot = m.at("ghot", 212032, [P, TOP_GROUPS, GROUPS], F32)
    expert = m.at("expert", 212160, [P, TOP_K], F32)
    h1T = m.at("h1T", 132992, [P, KT, LP], F32)
    h1 = m.at("h1", 166432, [P, TILES, D], F32)
    sgu = m.at("sgu", 0, [P, KT, 2 * F], F32)
    sg = m.at("sg", 24576, [P, FT, LP], F32)
    sh = m.at("sh", 32960, [P, FT, LP], F32)
    cnt = m.at("cnt", 123392, [P, 6, E], F32)
    sched = m.at("sched", 124928, [P, 8], F32)
    sched_i = m.at("sched_i", 124960, [P, 4], I32)
    wgu_raw = [m.at(f"wgu_raw{j}", 41472 + 16384 * j, [P, KT, 2 * F], F32) for j in range(2)]
    wgu_lo = [m.at(f"wgu_lo{j}", 166432 + 16384 * j, [P, KT, 2 * F], F32R) for j in range(2)]
    wgu_hi = [m.at(f"wgu_hi{j}", 132992 + 16384 * j, [P, KT, 2 * F], F32R) for j in range(2)]
    wd_raw = [m.at(f"wd_raw{j}", 74240 + 16384 * j, [P, FT, D], F32) for j in range(2)]
    wd_lo = [m.at(f"wd_lo{j}", 74240 + 16384 * j, [P, FT, D], F32R) for j in range(2)]
    wd_hi = [m.at(f"wd_hi{j}", 74240 + 16384 * j + 8192, [P, FT, D], F32R) for j in range(2)]
    xg = [m.at(f"xg{j}", 107008 + 8192 * j, [P, 2, D], F32) for j in range(2)]
    ysb = [m.at(f"ysb{j}", 8192 * j, [P, 2, D], F32) for j in range(2)]
    xT = m.at("xT", 16384, [P, KT, 2, BLOCK], F32R)
    gact = m.at("gact", 27136, [P, FT, BLOCK], F32)
    hid = m.at("hid", 28480, [P, FT, BLOCK], F32)
    up_lo = m.at("up_lo", 29824, [P, STEPS, BLOCK], F32)
    up_sum = m.at("up_sum", 125056, [P, STEPS, BLOCK], F32)
    hid_hi = m.at("hid_hi", 128000, [P, FT, 2 * P], F32R)
    hid_lo = m.at("hid_lo", 130048, [P, FT, 2 * P], F32R)
    got = [m.at(f"got{j}", 41472 + 32768 * j, [P, TOP_K, D], F32) for j in range(GOT)]
    ln_f = m.at("ln_f", 139776, [P, 2, D], F32)
    sdn = m.at("sdn", 147968, [P, FT, D], F32)
    part_sum = [m.at(f"part_sum{j}", 156160 + 4096 * j, [P, D], F32) for j in range(2)]

    consts_ready = sem("consts_ready")
    places_ready, pads_ready = sem("places_ready"), sem("pads_ready")
    list_cleared = sem("list_cleared")
    par_loaded = sem("par_loaded")
    hT_loaded = [sem(f"hT_loaded{k}") for k in range(KT)]
    hT_hi_ready, hT_lo_ready = sem("hT_hi_ready"), sem("hT_lo_ready")
    win_loaded = [sem(f"win_loaded{j}") for j in range(NW)]
    win_hi_ready, win_lo_ready = sem("win_hi_ready"), sem("win_lo_ready")
    wg_loaded = sem("wg_loaded")
    wg_hi_ready, wg_lo_ready = sem("wg_hi_ready"), sem("wg_lo_ready")
    tile_done = sem("tile_done")
    tile_read = sem("tile_read")
    conv_done = sem("conv_done")
    xc_split = sem("xc_split")
    coef_ready = sem("coef_ready")
    th_ready = sem("th_ready")
    mult2_ready = sem("mult2_ready")
    mult_ready = sem("mult_ready")
    scan_done = sem("scan_done")
    dve_step = sem("dve_step")
    act_step = sem("act_step")
    pool_step = sem("pool_step")
    wout_loaded = sem("wout_loaded")
    dve_steps, pool_n = [], [0]

    def in_col(n, j):
        return (D if j < LT else 0) + n * LB + (j % LT) * P

    N_IN = 2 * LT * LRU_BLOCKS
    PER = 4 * LT

    with nc.Block() as block:
        @block.sync
        def _(sp):
            def load_win(q):
                n, j = divmod(q, 2 * LT)
                if q >= NW:
                    n0, j0 = divmod(q - NW, 2 * LT)
                    sp.wait_ge(tile_done, PER * n0 + j0 + 1)
                c = in_col(n, j)
                sp.dma_start(win_raw[q % NW][:, :, :],
                             w_in[:, c:c + P].rearrange("(k p) c -> p k c", p=P)
                             ).then_inc(win_loaded[q % NW], 16)

            def load_wg(n):
                if n:
                    sp.wait_ge(tile_done, PER * n)
                sp.dma_start(wg_raw[:, :, :], w_gates[n].rearrange("(k p) c -> p k c", p=P)
                             ).then_inc(wg_loaded, 16)

            load_win(0)
            for k in range(KT):
                sp.dma_start(hT_raw[:, k, 0:L], hT[k * P:(k + 1) * P, :]).then_inc(hT_loaded[k], 16)
                if k == 0:
                    sp.dma_start(par[:, :], chan).then_inc(par_loaded, 16)
            load_win(1)
            load_win(2)
            load_wg(0)
            sp.wait_ge(pads_ready, 2)
            sp.dma_start(pair_list.rearrange("(p c) w -> p c w", p=P), pads[:, :, :]
                         ).then_inc(list_cleared, 16)
            for q in range(NW, N_IN):
                load_win(q)
                if q % (2 * LT) == 2 and q > 2 * LT:
                    load_wg(q // (2 * LT))
            sp.wait_ge(tile_done, PER * (LRU_BLOCKS - 1) + 2 * LT)
            sp.dma_start(wout_raw[:, :, :], w_out.rearrange("(k p) c -> p k c", p=P)
                         ).then_inc(wout_loaded, 16)

        @block.gpsimd
        def _(pool):
            s = Chain(pool, pool_step)
            s.step(pool.memset(hT_raw[:, :, L:LP], 0.0))
            s.step(pool.memset(xr[:, :, 0:CONV - 1], 0.0))
            s.step(pool.memset(ident[:, :], 0.0))
            s.step(pool.affine_select(out=ident[:, :], in_=ident[:, :], compare_op=ALU.not_equal,
                                      fill=1.0, base=0, pattern=[[-1, P]], channel_multiplier=1))
            s.step(pool.memset(ones[:, :], 1.0))
            s.step(pool.affine_select(out=tri[:, :], in_=ones[:, :], compare_op=ALU.is_gt,
                                      fill=0.0, base=0, pattern=[[1, P]], channel_multiplier=-1))
            s.step(pool.iota(iota_e_i[:, :], pattern=[[1, E]], base=0, channel_multiplier=0))
            s.step(pool.iota(list_start_i[:, :], pattern=[[STRIDE, E]], base=0,
                             channel_multiplier=0))
            s.step(pool.iota(block_id_i[:, :], pattern=[[1, 1]], base=0, channel_multiplier=1))
            s.step(pool.tensor_copy(iota_e[:, :], iota_e_i[:, :]))
            s.step(pool.tensor_copy(list_start[:, :], list_start_i[:, :]))
            s.step(pool.tensor_copy(block_id[:, :], block_id_i[:, :]))
            s.step(pool.memset(cum[:, 0, :], 0.0))
            for what in range(2):
                pool.iota(pads[:, :, what], pattern=[[1, LIST_COLS]], base=0,
                          channel_multiplier=LIST_COLS).then_inc(places_ready, 1)
            for b in range(2):
                s.step(pool.memset(pair[b][:, :, :], 0))
            s.step(pool.iota(pair_id[:, :, :, 0], pattern=[[P, TILES], [0, TOP_K]], base=0,
                             channel_multiplier=1))
            pool.iota(pair_id[:, :, :, 1], pattern=[[P * TOP_K, TILES], [1, TOP_K]], base=0,
                      channel_multiplier=TOP_K).then_inc(consts_ready, 1)

            def lo_win(q):
                n, j = divmod(q, 2 * LT)
                pool.wait_ge(win_hi_ready, q + 1)
                pool.tensor_tensor(win_lo[q % NW][:, :, :], win_raw[q % NW][:, :, :],
                                   win_hi[q % NW][:, :, :].bitcast(F32), ALU.subtract
                                   ).then_inc(win_lo_ready, 1)

            for n in range(LRU_BLOCKS):
                for j in range(2 * LT):
                    lo_win(2 * LT * n + j)
                pool.wait_ge(wg_hi_ready, n + 1)
                pool.tensor_tensor(wg_lo[:, :, :], wg_raw[:, :, :], wg_hi[:, :, :].bitcast(F32),
                                   ALU.subtract).then_inc(wg_lo_ready, 1)
            pool_n[0] = s.n

        @block.tensor
        def _(pe):
            for n in range(LRU_BLOCKS):
                for j in range(PER):
                    s = PER * n + j
                    b0 = 3 * (s % 2)
                    if s >= 2:
                        pe.wait_ge(tile_read, s - 1)
                    if j < 2 * LT:
                        q = 2 * LT * n + j
                        pe.wait_ge(win_hi_ready, q + 1)
                        pe.wait_ge(win_lo_ready, q + 1)
                        kt, w = KT, (win_hi[q % NW], win_lo[q % NW])
                        x, c0 = (hT_hi, hT_lo), 0
                    else:
                        pe.wait_ge(xc_split, LT * (n + 1))
                        pe.wait_ge(wg_hi_ready, n + 1)
                        pe.wait_ge(wg_lo_ready, n + 1)
                        kt, w = LT, (wg_hi, wg_lo)
                        x, c0 = (xc_hi, xc_lo), (j - 2 * LT) * P
                    for k in range(kt):
                        if s == 0:
                            pe.wait_ge(hT_hi_ready, k + 1)
                            pe.wait_ge(hT_lo_ready, k + 1)
                        for c in range(3):
                            last = split_product(
                                pe, bank[:, b0 + c, 0:CHUNK],
                                [a[:, k, c0:c0 + P] for a in w],
                                [a[:, k, c * CHUNK:(c + 1) * CHUNK] for a in x],
                                k == 0, k == kt - 1)
                    last.then_inc(tile_done, 1)

        @block.scalar
        def _(act):
            rows3 = lambda a: a.rearrange("p (c t) -> p c t", c=3)

            def psum_tile(s):
                act.wait_ge(tile_done, s + 1)
                b0 = 3 * (s % 2)
                return bank[:, b0:b0 + 3, 0:CHUNK]

            def hi_win(q):
                act.wait_ge(win_loaded[q % NW], 16 * (q // NW + 1))
                if q >= NW:
                    n0, j0 = divmod(q - NW, 2 * LT)
                    act.wait_ge(tile_done, PER * n0 + j0 + 1)
                act.activation(win_hi[q % NW][:, :, :], win_raw[q % NW][:, :, :], ACT.Copy
                               ).then_inc(win_hi_ready, 1)

            hi_win(0)
            act.wait_ge(pool_step, 1)
            for k in range(KT):
                act.wait_ge(hT_loaded[k], 16)
                act.activation(hT_hi[:, k, :], hT_raw[:, k, :], ACT.Copy).then_inc(hT_hi_ready, 1)
            hi_win(1)
            hi_win(2)
            act.wait_ge(par_loaded, 16)
            act.activation(sp_tmp[:, 0, :], par[:, C_AP:C_AP + KT], ACT.Abs).then_inc(act_step, 1)
            act.wait_ge(act_step, 1)
            act.activation(sp_tmp[:, 0, :], sp_tmp[:, 0, :], ACT.Exp, scale=-1.0
                           ).then_inc(act_step, 1)
            act.wait_ge(pool_step, 2)
            for n in range(LRU_BLOCKS):
                s = PER * n
                act.wait_ge(wg_loaded, 16 * (n + 1))
                if n:
                    act.wait_ge(tile_done, s)
                act.activation(wg_hi[:, :, :], wg_raw[:, :, :], ACT.Copy).then_inc(wg_hi_ready, 1)
                for j in range(2 * LT):
                    q = 2 * LT * n + j
                    src = psum_tile(s + j)
                    ch = n * LT + j % LT
                    if j < LT:
                        if n:
                            act.wait_ge(conv_done, LT * (n - 1) + j + 1)
                        act.activation(rows3(xr[:, j, CONV - 1:]), src, ACT.Identity,
                                       bias=par[:, C_BIN + KT + ch:C_BIN + KT + ch + 1]
                                       ).then_inc(tile_read, 1)
                    else:
                        act.activation(rows3(zT[:, ch, :]), src, ACT.Gelu_apprx_tanh,
                                       bias=par[:, C_BIN + ch:C_BIN + ch + 1]
                                       ).then_inc(tile_read, 1)
                    if q + NW < N_IN:
                        hi_win(q + NW)
                if n:
                    act.wait_ge(scan_done, LT * n)
                for j in range(2 * LT, PER):
                    c = j % LT
                    to = gate_x if j < 3 * LT else gate_a
                    b = C_BG + n * 2 * LT + j - 2 * LT
                    src = psum_tile(s + j)
                    act.activation(rows3(to[:, c, :]), src, ACT.Sigmoid, bias=par[:, b:b + 1]
                                   ).then_inc(tile_read, 1)
                act.wait_ge(tile_read, s + PER)
                if n == 0:
                    act.wait_ge(coef_ready, 1)
                    act.wait_ge(list_cleared, 16)
                for c in range(LT):
                    ch = n * LT + c
                    act.activation(decay[:, c, :], gate_a[:, c, :], ACT.Exp,
                                   scale=lru_coef[:, 0, ch:ch + 1])
                    act.activation(th[:, c, :], gate_a[:, c, :], ACT.Tanh,
                                   scale=lru_coef[:, 1, ch:ch + 1]).then_inc(th_ready, 1)
                for c in range(LT):
                    act.wait_ge(mult2_ready, LT * n + c + 1)
                    act.activation(th[:, c, :], th[:, c, :], ACT.Sqrt).then_inc(mult_ready, 1)

        @block.vector
        def _(dve):
            s = Chain(dve, dve_step)
            dve.wait_ge(pool_step, 1)
            for k in range(KT):
                dve.wait_ge(hT_hi_ready, k + 1)
                dve.tensor_tensor(hT_lo[:, k, :], hT_raw[:, k, :], hT_hi[:, k, :].bitcast(F32),
                                  ALU.subtract).then_inc(hT_lo_ready, 1)
            dve.wait_ge(places_ready, 2)
            for what, (first, window) in enumerate(((L, PAD // TOP_K), (PAIRS, PAD))):
                s.step(dve.tensor_scalar(pads[:, :, what], pads[:, :, what], window - 1, None,
                                         ALU.bitwise_and))
                dve.tensor_scalar(pads[:, :, what], pads[:, :, what], first, None, ALU.add
                                  ).then_inc(pads_ready, 1)
            a, e, r, q2 = par[:, C_AP:C_AP + KT], sp_tmp[:, 0, :], sp_tmp[:, 1, :], sp_tmp[:, 2, :]
            v = sp_tmp[:, 3, :]
            dve.wait_ge(act_step, 2)
            dve.wait_ge(par_loaded, 16)
            s.step(dve.tensor_scalar(r, e, 2.0, None, ALU.add))
            s.step(dve.reciprocal(r, r))
            s.step(dve.tensor_tensor(r, e, r, ALU.mult))
            s.step(dve.tensor_tensor(q2, r, r, ALU.mult))
            s.step(dve.tensor_scalar(v, q2, 1.0 / 19, 1.0 / 17, ALU.mult, ALU.add))
            for d in (15, 13, 11, 9, 7, 5, 3, 1):
                s.step(dve.tensor_tensor(v, v, q2, ALU.mult))
                s.step(dve.tensor_scalar(v, v, 1.0 / d, None, ALU.add))
            s.step(dve.scalar_tensor_tensor(v, v, 2.0, r, ALU.mult, ALU.mult))
            s.step(dve.tensor_scalar(r, a, -1.0, 0.0, ALU.mult, ALU.max))
            s.step(dve.tensor_tensor(v, v, r, ALU.add))
            s.step(dve.tensor_scalar(lru_coef[:, 0, :], v, -LRU_C, None, ALU.mult))
            dve.tensor_scalar(lru_coef[:, 1, :], v, LRU_C, None, ALU.mult).then_inc(coef_ready, 1)

            for n in range(LRU_BLOCKS):
                for c in range(LT):
                    ch = n * LT + c
                    cw = lambda k: par[:, C_CW + k * KT + ch:C_CW + k * KT + ch + 1]
                    dve.wait_ge(tile_read, PER * n + c + 1)
                    s.step(dve.tensor_scalar(xc[:, c, :], xr[:, c, 0:LP], cw(0),
                                             par[:, C_CB + ch:C_CB + ch + 1], ALU.mult, ALU.add))
                    for k in range(1, CONV):
                        s.step(dve.scalar_tensor_tensor(xc[:, c, :], xr[:, c, k:k + LP], cw(k),
                                                        xc[:, c, :], ALU.mult, ALU.add))
                    dve.tensor_copy(xc_hi[:, c, :], xc[:, c, :]).then_inc(conv_done, 1)
                    dve.wait_ge(conv_done, ch + 1)
                    dve.tensor_tensor(xc_lo[:, c, :], xc[:, c, :], xc_hi[:, c, :].bitcast(F32),
                                      ALU.subtract).then_inc(xc_split, 1)
                for c in range(LT):
                    dve.wait_ge(th_ready, LT * n + c + 1)
                    s.step(dve.tensor_scalar(gate_a[:, c, :], th[:, c, :], 1.0, None, ALU.add))
                    s.step(dve.reciprocal(gate_a[:, c, :], gate_a[:, c, :]))
                    dve.scalar_tensor_tensor(th[:, c, :], th[:, c, :], 2.0, gate_a[:, c, :],
                                             ALU.mult, ALU.mult).then_inc(mult2_ready, 1)
                for c in range(LT):
                    s.step(dve.tensor_tensor(gate_x[:, c, :], xc[:, c, :], gate_x[:, c, :],
                                             ALU.mult))
                    dve.wait_ge(mult_ready, LT * n + c + 1)
                    s.step(dve.tensor_tensor(gate_x[:, c, :], gate_x[:, c, :], th[:, c, :],
                                             ALU.mult))
                    s.step(dve.tensor_tensor_scan(xc[:, c, :], decay[:, c, :], gate_x[:, c, :],
                                                  0.0, ALU.mult, ALU.add))
                    ch = n * LT + c
                    dve.tensor_tensor(zT[:, ch, :], zT[:, ch, :], xc[:, c, :], ALU.mult
                                      ).then_inc(scan_done, 1)
            dve_steps.append(s.n)

    wout_hi_ready, wout_lo_ready = sem("wout_hi_ready"), sem("wout_lo_ready")
    b_loaded = sem("b_loaded")
    h_loaded, h_used = sem("h_loaded"), sem("h_used")
    z_hi_ready, z_lo_ready = sem("z_hi_ready"), sem("z_lo_ready")
    z_clear = sem("z_clear")
    mix_ready, var_ready, std_ready = sem("mix_ready"), sem("var_ready"), sem("std_ready")
    centred, norm_ready = sem("centred"), sem("norm_ready")
    turned, h1T_moved = sem("turned"), sem("h1T_moved")
    logits_ready, scores_ready = sem("logits_ready"), sem("scores_ready")
    mask_ready, rank_ready, rank_read = sem("mask_ready"), sem("rank_ready"), sem("rank_read")
    h1_stored = sem("h1_stored")
    place_ready, listed = sem("place_ready"), sem("listed")
    pool_steps = pool_n[0]

    cols = lambda i: slice(i * P, i * P + ROWS[i])

    sh_loaded = sem("sh_loaded")
    count_ready = sem("count_ready")
    sched_ready, sched_stored, sched_loaded = (sem("sched_ready"), sem("sched_stored"),
                                               sem("sched_loaded"))
    sh_up, sh_act, sh_ready = sem("sh_up"), sem("sh_act"), sem("sh_ready")
    hid_clear = sem("hid_clear")
    x_turned, up_done, down_done = sem("x_turned"), sem("up_done"), sem("down_done")
    pair_free = sem("pair_free")
    xT_moved, hid_ready, hid_step = sem("xT_moved"), sem("hid_ready"), sem("hid_step")
    y_act, y_dve, ysb_free = sem("y_act"), sem("y_dve"), sem("ysb_free")
    y_stored = [sem(f"y_stored{j}") for j in range(2)]
    rows3 = lambda a: a.rearrange("p (c t) -> p c t", c=3)

    wgu_loaded = [sem(f"wgu_loaded{j}") for j in range(2)]
    wd_loaded = [sem(f"wd_loaded{j}") for j in range(2)]
    pair_loaded = [sem(f"pair_loaded{j}") for j in range(2)]
    gathered = [sem(f"gathered{j}") for j in range(2)]
    wd_hi_ready, wd_lo_ready = sem("wd_hi_ready"), sem("wd_lo_ready")
    gate_ready, dve_hi = sem("gate_ready"), sem("dve_hi")
    wgu_hi_ready, wgu_lo_ready = sem("wgu_hi_ready"), sem("wgu_lo_ready")
    xT_hi_ready, up_lo_ready, up_summed = sem("xT_hi_ready"), sem("up_lo_ready"), sem("up_summed")
    PARTS = 4
    part_k = lambda part: slice(part * KT // PARTS, (part + 1) * KT // PARTS)

    sp_pass, pool_pass = sem("sp_pass"), sem("pool_pass")

    def blocks_to_run(eng):
        return eng.value_load(sched_row[0:1, 2:3], min_val=E, max_val=T_MAX + 1)

    def of_block(eng, t, what, top):
        return eng.value_load(sched_row[0:1, bass.ds(t * 4 + what, 1)], min_val=0, max_val=top)

    with nc.Block() as block:
        @block.sync
        def _(sp):
            sp.dma_start(ln_b[:, :, :], ln[0:2, :].unsqueeze(0).to_broadcast([P, 2, D])
                         ).then_inc(b_loaded, 16)
            sp.dma_start(rw[:, :, :], router_w.rearrange("(k p) e -> p k e", p=P)
                         ).then_inc(b_loaded, 16)
            sp.dma_start(rbias[:, :], router_b.to_broadcast([P, E])).then_inc(b_loaded, 16)
            for i, r in enumerate(ROWS):
                if i:
                    sp.wait_ge(h_used, i)
                sp.dma_start(h_in[0:r, :], h_rows[i * P:i * P + r, :]).then_inc(h_loaded, 16)
                if i >= 1:
                    sp.wait_ge(norm_ready, i)
                    sp.dma_start(h1_rows[cols(i - 1), :], h1[0:ROWS[i - 1], i - 1, :]
                                 ).then_inc(h1_stored, 16)
            sp.wait_ge(mix_ready, TILES)
            sp.dma_start(sgu[:, :, :], sh_gu.rearrange("(k p) c -> p k c", p=P)
                         ).then_inc(sh_loaded, 16)
            i = TILES - 1
            sp.wait_ge(norm_ready, TILES)
            sp.dma_start(h1_rows[cols(i), :], h1[0:ROWS[i], i, :]).then_inc(h1_stored, 16)

            sp.wait_ge(sched_ready, 3)
            sp.dma_start(sched_dram, sched_i[:, :]).then_inc(sched_stored, 16)
            sp.wait_ge(sched_stored, 16)
            sp.dma_start(sched_row[:, :], sched_dram.rearrange("(o b) c -> o (b c)", o=1)
                         ).then_inc(sched_loaded, 16)
            sp.wait_ge(sched_loaded, 16)
            sp.wait_ge(listed, 16 * TILES * TOP_K)

            n = blocks_to_run(sp)
            with sp.Fori(0, n + 2, 2) as i:
                for b in range(2):
                    t = i + b
                    row = of_block(sp, t, 0, LIST - BLOCK)
                    sp.wait_ge(pair_free, t + 1)
                    sp.sem_inc(sp_pass, 1)
                    sp.dma_start(pair[b][:, 0, :], pair_list[bass.ds(row, P), :]
                                 ).then_inc(pair_loaded[b], 16)
                    sp.dma_start(pair[b][0:REST, 1, :], pair_list[bass.ds(row + P, REST), :]
                                 ).then_inc(pair_loaded[b], 16)
                    e = of_block(sp, t, 1, E - 1)
                    sp.wait_ge(wgu_lo_ready, t * PARTS + PARTS)
                    sp.sem_inc(sp_pass, 1)
                    sp.dma_start(wgu_raw[b][:, :, :],
                                 w_gu[bass.ds(e, 1)].rearrange("o (k p) c -> p (o k) c", p=P)
                                 ).then_inc(wgu_loaded[b], 16)
                    sp.wait_ge(down_done, t * STEPS + STEPS)
                    sp.sem_inc(sp_pass, 1)
                    sp.dma_start(wd_raw[b][:, :, :],
                                 w_down[bass.ds(e, 1)].rearrange("o (k p) c -> p (o k) c", p=P)
                                 ).then_inc(wd_loaded[b], 16)

        @block.gpsimd
        def _(pool):
            s = Chain(pool, pool_step)
            s.n = pool_steps
            pool.memset(h1T[:, :, L:LP], 0.0).then_inc(z_clear, 1)
            pool.wait_ge(list_cleared, 16)

            def enlist(i):
                r = ROWS[i]
                pool.wait_ge(place_ready, i + 1)
                for j in range(TOP_K):
                    pool.indirect_dma_start(
                        out=pair_list,
                        out_offset=bass.IndirectOffsetOnAxis(ap=place[0:r, i, j:j + 1], axis=0),
                        in_=pair_id[0:r, i, j, :], in_offset=None).then_inc(listed, 16)

            for i, r in enumerate(ROWS):
                pool.wait_ge(centred, i + 1)
                if i == 0:
                    pool.wait_ge(b_loaded, 48)
                s.step(pool.tensor_tensor(h1[0:r, i, :], h1[0:r, i, :], ln_b[0:r, 0, :], ALU.mult))
                pool.tensor_tensor(h1[0:r, i, :], h1[0:r, i, :], ln_b[0:r, 1, :], ALU.add
                                   ).then_inc(norm_ready, 1)
                if i >= 3:
                    enlist(i - 3)
            pool.wait_ge(z_lo_ready, TILES)
            pool.memset(hid_hi[:, :, :].bitcast(F32), 0.0).then_inc(hid_clear, 1)
            pool.memset(hid_lo[:, :, :].bitcast(F32), 0.0).then_inc(hid_clear, 1)
            pool.wait_ge(hid_clear, 2)
            pool.dma_start(h1_rows[L:, :].rearrange("(p r) (b n) -> p (r b) n", p=P, b=2),
                           hid_hi[:, :, :].bitcast(F32).rearrange("p f t -> p (f t)").unsqueeze(1)
                           .to_broadcast([P, 2 * PAD // TOP_K // P, 512])).then_inc(y_stored[1], 16)
            pool.wait_ge(y_stored[1], 16)
            for i in range(TILES - 3, TILES):
                enlist(i)
            pool_n[0] = s.n

            def fetch(t, b, i):
                pool.wait_ge(pair_loaded[b], i * 16 + 32)
                pool.wait_ge(x_turned, t * STEPS + STEPS)
                pool.sem_inc(pool_pass, 1)
                for half, r in enumerate((P, REST)):
                    pool.indirect_dma_start(
                        out=xg[b][0:r, half, :], out_offset=None, in_=h1_rows,
                        in_offset=bass.IndirectOffsetOnAxis(ap=pair[b][0:r, half, 0:1],
                                                            axis=0)).then_inc(gathered[b], 16)

            def keep_rows(b):
                pool.tensor_copy(to_row[b][:, :], pair[b][:, :, 1]).then_inc(pair_free, 1)

            pool.wait_ge(sched_loaded, 16)
            n = blocks_to_run(pool)
            pool.wait_ge(h1_stored, 16 * TILES)
            fetch(0, 0, 0)
            fetch(1, 1, 0)
            pool.wait_ge(gathered[0], 32)
            keep_rows(0)
            with pool.Fori(0, n, 2) as i:
                for b in range(2):
                    t = i + b
                    pool.wait_ge(wd_hi_ready, t * FT + FT)
                    pool.sem_inc(pool_pass, 1)
                    pool.tensor_tensor(wd_lo[b][:, :, :], wd_raw[b][:, :, :],
                                       wd_hi[b][:, :, :].bitcast(F32), ALU.subtract
                                       ).then_inc(wd_lo_ready, 1)
                    fetch(t + 2, b, i + 2)
                    pool.wait_ge(y_stored[1 - b], i * 16 + 16 + 16 * b)
                    pool.sem_inc(ysb_free, 1)
                    pool.wait_ge(gathered[1 - b], i * 16 + 32 + 32 * b)
                    pool.sem_inc(pool_pass, 1)
                    keep_rows(1 - b)
                    pool.wait_ge(pair_free, t + 4)
                    pool.wait_ge(y_act, t * 2 + 4)
                    pool.wait_ge(y_dve, t * 2 + 4)
                    pool.sem_inc(pool_pass, 1)
                    for half, r in enumerate((P, REST)):
                        pool.indirect_dma_start(
                            out=pair_rows,
                            out_offset=bass.IndirectOffsetOnAxis(ap=to_row[b][0:r, half:half + 1],
                                                                 axis=0),
                            in_=ysb[b][0:r, half, :], in_offset=None).then_inc(y_stored[b], 16)

        @block.tensor
        def _(pe):
            def mix(i):
                if i >= 2:
                    pe.wait_ge(h_used, i - 1)
                pe.wait_ge(z_hi_ready, i + 1)
                pe.wait_ge(z_lo_ready, i + 1)
                for k in range(KT):
                    if i == 0:
                        pe.wait_ge(wout_hi_ready, k + 1)
                        pe.wait_ge(wout_lo_ready, k + 1)
                    for n in range(2):
                        mm = split_product(pe, bank[:, 2 * (i % 2) + n, :],
                                           (z_hi[i % 2][:, k, :], z_lo[i % 2][:, k, :]),
                                           [w[:, k, n * 512:(n + 1) * 512]
                                            for w in (wout_hi, wout_lo)], k == 0, k == KT - 1)
                mm.then_inc(mix_ready, 1)

            def turn(i):
                r = ROWS[i]
                pe.wait_ge(norm_ready, i + 1)
                if i == 0:
                    pe.wait_ge(consts_ready, 1)
                if i:
                    pe.wait_ge(h1T_moved, i)
                for k in range(KT):
                    mm = pe.transpose(bank[:, 4 + k // 4, (k % 4) * P:(k % 4) * P + r],
                                      h1[0:r, i, k * P:(k + 1) * P], ident[0:r, 0:r])
                mm.then_inc(turned, 1)

            def logits(i):
                r = ROWS[i]
                pe.wait_ge(h1T_moved, i + 1)
                if i == 0:
                    pe.wait_ge(b_loaded, 48)
                if i >= 2:
                    pe.wait_ge(rank_read, i - 1)
                for k in range(KT):
                    mm = pe.matmul(bank[0:r, 6 + i % 2, 0:E], h1T[:, k, cols(i)], rw[:, k, :],
                                   start=(k == 0), stop=(k == KT - 1))
                mm.then_inc(logits_ready, 1)

            def rank(i):
                r = ROWS[i]
                pe.wait_ge(mask_ready, i + 1)
                pe.matmul(bank[0:r, 6 + i % 2, E:2 * E], ones[:, 0:r], cum[:, i % 2, :],
                          start=True, stop=False)
                pe.matmul(bank[0:r, 6 + i % 2, E:2 * E], tri[0:r, 0:r], mask[0:r, :],
                          start=False, stop=True).then_inc(rank_ready, 1)

            def shared_up(f, half):
                if f:
                    pe.wait_ge((sh_act, sh_ready)[half], f)
                for k in range(KT):
                    for c in range(3):
                        mm = pe.matmul(bank[:, 3 * half + c, 0:CHUNK],
                                       sgu[:, k, half * F + f * P:half * F + (f + 1) * P],
                                       h1T[:, k, c * CHUNK:(c + 1) * CHUNK],
                                       start=(k == 0), stop=(k == KT - 1))
                mm.then_inc(sh_up, 1)

            for i in range(TILES + 3):
                if i < TILES:
                    mix(i)
                if 0 <= i - 1 < TILES:
                    turn(i - 1)
                if 0 <= i - 2 < TILES:
                    logits(i - 2)
                if i == TILES + 1:
                    pe.wait_ge(sh_loaded, 16)
                    pe.wait_ge(h1T_moved, TILES)
                    pe.wait_ge(h_used, TILES)
                    shared_up(0, 0)
                if i == TILES + 2:
                    shared_up(0, 1)
                if 0 <= i - 3:
                    rank(i - 3)
            r, t = ROWS[-1], TILES - 1
            pe.wait_ge(rank_read, TILES)
            pe.matmul(bank[:, 7, 0:E], ones[:, :], cum[:, t % 2, :], start=True, stop=False)
            pe.matmul(bank[:, 7, 0:E], ones[0:r, :], mask[0:r, :], start=False, stop=True
                      ).then_inc(count_ready, 1)
            for f in range(1, FT):
                for half in range(2):
                    shared_up(f, half)
            pe.wait_ge(sh_act, FT)
            pe.wait_ge(sh_ready, FT)
            pe.wait_ge(sched_ready, 1)

            def turn_block(t, b, groups):
                for q in groups:
                    pe.wait_ge(xT_moved, t * QX + max(q, 1))
                    for k in (2 * q, 2 * q + 1):
                        o = (k % 2) * BLOCK
                        pe.transpose(bank[:, 4 + q % 2, o:o + P], xg[b][:, 0, k * P:(k + 1) * P],
                                     ident[:, :])
                        mm = pe.transpose(bank[:, 4 + q % 2, o + P:o + BLOCK],
                                          xg[b][0:REST, 1, k * P:(k + 1) * P],
                                          ident[0:REST, 0:REST])
                    mm.then_inc(x_turned, 1)

            pe.wait_ge(sched_loaded, 16)
            n = blocks_to_run(pe)
            pe.wait_ge(gathered[0], 32)
            turn_block(0, 0, range(QX))
            with pe.Fori(0, n, 2) as i:
                for b in range(2):
                    t = i + b
                    pe.wait_ge(wgu_hi_ready, t * PARTS + PARTS)
                    pe.wait_ge(wgu_lo_ready, t * PARTS + 3 * PARTS)
                    pe.wait_ge(hid_ready, t * 2 + 2)
                    for f in range(FT):
                        for half in range(2):
                            for k in range(KT):
                                if f == 0 and half == 0 and k % 2 == 0:
                                    pe.wait_ge(xT_moved, t * QX + k // 2 + 2)
                                c = half * F + f * P
                                pe.matmul(bank[:, 2 * f + half, 0:2 * BLOCK],
                                          wgu_hi[b][:, k, c:c + P],
                                          xT[:, k, :, :].rearrange("p h t -> p (h t)"),
                                          start=(k == 0), stop=False)
                                mm = pe.matmul(bank[:, 2 * f + half, 0:BLOCK],
                                               wgu_lo[b][:, k, c:c + P], xT[:, k, 0, :],
                                               start=False, stop=(k == KT - 1))
                            mm.then_inc(up_done, 1)
                    pe.wait_ge(gathered[1 - b], i * 16 + 32 + 32 * b)
                    for half in range(2):
                        turn_block(t + 1, 1 - b, (2 * half, 2 * half + 1))
                        if half == 0:
                            pe.wait_ge(wd_hi_ready, t * FT + FT)
                            pe.wait_ge(wd_lo_ready, t + 1)
                        for k in range(FT):
                            if half == 0:
                                pe.wait_ge(hid_ready, t * 2 + k + 3)
                            for c in range(2):
                                if k == 0:
                                    pe.wait_ge((y_act, y_dve)[c], t * 2 + half + 2)
                                mm = split_product(
                                    pe, bank[:, 6 + c, :],
                                    [h[:, k, half * P:(half + 1) * P] for h in (hid_hi, hid_lo)],
                                    [w[b][:, k, c * 512:(c + 1) * 512] for w in (wd_hi, wd_lo)],
                                    k == 0, k == FT - 1)
                                if k == FT - 1:
                                    mm.then_inc(down_done, 1)

        @block.scalar
        def _(act):
            def split_z(i):
                r = ROWS[i]
                if i >= 2:
                    act.wait_ge(mix_ready, i - 1)
                act.activation(z_hi[i % 2][:, :, 0:r], zT[:, :, cols(i)], ACT.Copy
                               ).then_inc(z_hi_ready, 1)

            split_z(0)
            act.wait_ge(wout_loaded, 16)
            for k in range(KT):
                act.activation(wout_hi[:, k, :], wout_raw[:, k, :], ACT.Copy
                               ).then_inc(wout_hi_ready, 1)
            split_z(1)
            for i in range(TILES + 2):
                if i < TILES:
                    r = ROWS[i]
                    act.wait_ge(var_ready, i + 1)
                    act.activation(rstd[0:r, 0:1], rstd[0:r, 0:1], ACT.Sqrt).then_inc(std_ready, 1)
                if i + 2 < TILES:
                    split_z(i + 2)
                if 0 <= i - 1 < TILES:
                    t, r = i - 1, ROWS[i - 1]
                    act.wait_ge(turned, t + 1)
                    if t == 0:
                        act.wait_ge(z_clear, 1)
                    act.activation(h1T[:, :, cols(t)],
                                   bank[:, 4:6, :].rearrange("p b (k t) -> p (b k) t", t=P)[:, :, 0:r],
                                   ACT.Copy).then_inc(h1T_moved, 1)
                if 0 <= i - 2:
                    t, r = i - 2, ROWS[i - 2]
                    act.wait_ge(logits_ready, t + 1)
                    if t:
                        act.wait_ge(mask_ready, t)
                    act.activation(scores[0:r, :], bank[0:r, 6 + t % 2, 0:E], ACT.Sigmoid
                                   ).then_inc(scores_ready, 1)

            for f in range(FT):
                act.wait_ge(sh_up, 2 * f + 1)
                act.activation(rows3(sg[:, f, :]), bank[:, 0:3, 0:CHUNK], ACT.Silu
                               ).then_inc(sh_act, 1)

            def move_xT(t, groups):
                for q in groups:
                    act.wait_ge(x_turned, t * STEPS + SEED + q + 1)
                    act.activation(xT[:, 2 * q:2 * q + 2, 0, :],
                                   bank[:, 4 + q % 2, 0:2 * BLOCK].rearrange(
                                       "p (k t) -> p k t", k=2), ACT.Copy
                                   ).then_inc(xT_hi_ready, 1)

            def wgu_part(b, part):
                k = part_k(part)
                act.activation(wgu_hi[b][:, k, :], wgu_raw[b][:, k, :], ACT.Copy
                               ).then_inc(wgu_hi_ready, 1)

            def wd_part(b, k):
                act.activation(wd_hi[b][:, k, :], wd_raw[b][:, k, :], ACT.Copy
                               ).then_inc(wd_hi_ready, 1)

            def up_part(t, j):
                act.wait_ge(up_done, t * STEPS + SEED + j + 1)
                act.activation(up_lo[:, j, :], bank[:, j, BLOCK:2 * BLOCK], ACT.Copy
                               ).then_inc(up_lo_ready, 1)

            def silu(t, f):
                act.wait_ge(up_summed, t * STEPS + 2 * f + 1)
                act.activation(gact[:, f, :], up_sum[:, 2 * f, :], ACT.Silu).then_inc(gate_ready, 1)

            act.wait_ge(sh_up, 2 * FT)
            act.wait_ge(sched_loaded, 16)
            n = blocks_to_run(act)
            act.wait_ge(wgu_loaded[0], 16)
            for part in range(PARTS):
                wgu_part(0, part)
            act.wait_ge(wd_loaded[0], 16)
            for k in range(FT):
                wd_part(0, k)
            move_xT(0, range(QX))
            with act.Fori(0, n, 2) as i:
                for b in range(2):
                    t = i + b
                    act.wait_ge(wgu_loaded[1 - b], i * 8 + 16 + 16 * b)
                    wgu_part(1 - b, 0)
                    wgu_part(1 - b, 1)
                    up_part(t, 0)
                    wgu_part(1 - b, 2)
                    up_part(t, 1)
                    act.wait_ge(hid_step, t * 2 + 2)
                    silu(t, 0)
                    wgu_part(1 - b, 3)
                    up_part(t, 2)
                    silu(t, 1)
                    act.wait_ge(wd_loaded[1 - b], i * 8 + 16 + 16 * b)
                    wd_part(1 - b, 0)
                    up_part(t, 3)
                    act.wait_ge(ysb_free, t + 1)
                    for half, r in enumerate((P, REST)):
                        move_xT(t + 1, (2 * half, 2 * half + 1))
                        act.wait_ge(down_done, t * STEPS + SEED + 2 * half + 1)
                        act.activation(ysb[b][0:r, half, 0:512], bank[0:r, 6, :], ACT.Copy
                                       ).then_inc(y_act, 1)
                        if half == 0:
                            wd_part(1 - b, 1)

        @block.vector
        def _(dve):
            s = Chain(dve, dve_step)
            s.n = dve_steps[-1]

            def split_z(i):
                r = ROWS[i]
                dve.wait_ge(z_hi_ready, i + 1)
                dve.tensor_tensor(z_lo[i % 2][:, :, 0:r], zT[:, :, cols(i)],
                                  z_hi[i % 2][:, :, 0:r].bitcast(F32), ALU.subtract
                                  ).then_inc(z_lo_ready, 1)

            def norm_begin(i):
                r = ROWS[i]
                dve.wait_ge(mix_ready, i + 1)
                dve.wait_ge(h_loaded, 16 * (i + 1))
                dve.scalar_tensor_tensor(
                    h1[0:r, i, :].rearrange("p (b n) -> p b n", b=2),
                    h_in[0:r, :].rearrange("p (b n) -> p b n", b=2), ALPHA,
                    bank[0:r, 2 * (i % 2):2 * (i % 2) + 2, :], ALU.mult, ALU.add
                    ).then_inc(h_used, 1)
                dve.wait_ge(h_used, i + 1)
                s.step(dve.bn_stats(stats[0:r, 0, :], h1[0:r, i, 0:512]))
                s.step(dve.bn_stats(stats[0:r, 1, :], h1[0:r, i, 512:D]))
                s.step(dve.bn_aggr(mv[0:r, :], stats[0:r, :, :]))
                dve.tensor_scalar(rstd[0:r, 0:1], mv[0:r, 1:2], LN_EPS, None, ALU.add
                                  ).then_inc(var_ready, 1)

            def norm_end(i):
                r = ROWS[i]
                dve.wait_ge(std_ready, i + 1)
                s.step(dve.reciprocal(rstd[0:r, 1:2], rstd[0:r, 0:1]))
                dve.tensor_scalar(h1[0:r, i, :], h1[0:r, i, :], mv[0:r, 0:1], rstd[0:r, 1:2],
                                  ALU.subtract, ALU.mult).then_inc(centred, 1)

            def route(i):
                r = ROWS[i]
                sm = lambda j: small[0:r, j, :]
                dve.wait_ge(scores_ready, i + 1)
                s.step(dve.tensor_tensor(choice[0:r, :], scores[0:r, :], rbias[0:r, :], ALU.add))
                for g in range(GROUPS):
                    ins = dve.max(top_of[0:r, g, :], choice[0:r, g * GSIZE:(g + 1) * GSIZE])
                s.step(ins)
                s.step(dve.tensor_tensor(sm(0), top_of[0:r, :, 0], top_of[0:r, :, 1], ALU.add))
                s.step(dve.max(sm(1), sm(0)))
                s.step(dve.max_index(idx_u[0:r, 0, :], sm(1), sm(0)))
                s.step(dve.tensor_copy(sm(2), idx_u[0:r, 0, :]))
                s.step(dve.tensor_tensor(
                    ghot[0:r, :, :],
                    iota_e[0:r, 0:GROUPS].unsqueeze(1).to_broadcast([r, TOP_GROUPS, GROUPS]),
                    sm(2)[:, 0:TOP_GROUPS].unsqueeze(2).to_broadcast([r, TOP_GROUPS, GROUPS]),
                    ALU.is_equal))
                s.step(dve.tensor_reduce(sm(3), ghot[0:r, :, :].rearrange("p j g -> p g j"), AX,
                                         ALU.add))
                s.step(dve.tensor_scalar(sm(4), sm(3), -1.0, BIG, ALU.add, ALU.mult))
                by_group = choice[0:r, :].rearrange("p (g m) -> p g m", g=GROUPS)
                wide = lambda v: v.unsqueeze(2).to_broadcast([r, GROUPS, GSIZE])
                s.step(dve.tensor_tensor(by_group, by_group, wide(sm(3)), ALU.mult))
                s.step(dve.tensor_tensor(by_group, by_group, wide(sm(4)), ALU.add))
                s.step(dve.max(sm(5), choice[0:r, :]))
                s.step(dve.max_index(idx_u[0:r, 1, :], sm(5), choice[0:r, :]))
                s.step(dve.tensor_copy(expert[0:r, :], idx_u[0:r, 1, :]))
                s.step(dve.tensor_tensor(
                    hot[0:r, :, :], iota_e[0:r, :].unsqueeze(1).to_broadcast([r, TOP_K, E]),
                    expert[0:r, :].unsqueeze(2).to_broadcast([r, TOP_K, E]), ALU.is_equal))
                s.step(dve.tensor_tensor(
                    picked[0:r, :, :], hot[0:r, :, :],
                    scores[0:r, :].unsqueeze(1).to_broadcast([r, TOP_K, E]), ALU.mult))
                s.step(dve.tensor_reduce(sm(7), picked[0:r, :, :], AX, ALU.add))
                s.step(dve.tensor_reduce(sm(8)[:, 0:1], sm(7), AX, ALU.add))
                s.step(dve.tensor_scalar(sm(8)[:, 1:2], sm(8)[:, 0:1], 1e-20, None, ALU.add))
                s.step(dve.reciprocal(sm(8)[:, 2:3], sm(8)[:, 1:2]))
                s.step(dve.tensor_scalar(weight[0:r, i, :], sm(7), sm(8)[:, 2:3], ROUTED_SCALE,
                                         ALU.mult, ALU.mult))
                with nc.allow_low_precision(reason="at most one 1 is summed"):
                    dve.tensor_reduce(mask[0:r, :], hot[0:r, :, :].rearrange("p j e -> p e j"),
                                      AX, ALU.add).then_inc(mask_ready, 1)

            def places(i):
                r = ROWS[i]
                dve.wait_ge(rank_ready, i + 1)
                dve.tensor_tensor(rowval[0:r, :], list_start[0:r, :],
                                  bank[0:r, 6 + i % 2, E:2 * E], ALU.add).then_inc(rank_read, 1)
                dve.wait_ge(rank_read, i + 1)
                if i + 1 < TILES:
                    s.step(dve.tensor_tensor(cum[:, (i + 1) % 2, :], cum[:, i % 2, :],
                                             mask[:, :], ALU.add))
                s.step(dve.tensor_tensor(
                    picked[0:r, :, :], hot[0:r, :, :],
                    rowval[0:r, :].unsqueeze(1).to_broadcast([r, TOP_K, E]), ALU.mult))
                s.step(dve.tensor_reduce(small[0:r, 9, :], picked[0:r, :, :], AX, ALU.add))
                dve.tensor_copy(place[0:r, i, :], small[0:r, 9, :]).then_inc(place_ready, 1)

            dve.wait_ge(consts_ready, 1)
            dve.wait_ge(b_loaded, 48)
            split_z(0)
            for k in range(KT):
                dve.wait_ge(wout_hi_ready, k + 1)
                dve.tensor_tensor(wout_lo[:, k, :], wout_raw[:, k, :],
                                  wout_hi[:, k, :].bitcast(F32), ALU.subtract
                                  ).then_inc(wout_lo_ready, 1)
            split_z(1)
            for i in range(TILES + 3):
                if i < TILES:
                    norm_begin(i)
                if 0 <= i - 3:
                    places(i - 3)
                if i < TILES:
                    norm_end(i)
                if 0 <= i - 2 < TILES:
                    route(i - 2)
                if i + 2 < TILES:
                    split_z(i + 2)
            dve_steps.append(s.n)

            def gate_shared(f):
                dve.wait_ge(sh_act, f + 1)
                dve.wait_ge(sh_up, 2 * f + 2)
                dve.tensor_tensor(rows3(sh[:, f, :]), rows3(sg[:, f, :]), bank[:, 3:6, 0:CHUNK],
                                  ALU.mult).then_inc(sh_ready, 1)

            gate_shared(0)
            n_tok, n_blk, ends, done, part, one = (cnt[:, j, :] for j in range(6))
            sc = lambda j: sched[:, j:j + 1]
            dve.wait_ge(count_ready, 1)
            dve.tensor_copy(n_tok, bank[:, 7, 0:E]).then_inc(sched_ready, 1)
            dve.wait_ge(sched_ready, 1)
            s.step(dve.tensor_scalar(n_blk, n_tok, float(BLOCK), 1.0, ALU.is_gt, ALU.add))
            for k in range(2, NB_MAX):
                s.step(dve.scalar_tensor_tensor(n_blk, n_tok, float(k * BLOCK), n_blk, ALU.is_gt,
                                                ALU.add))
            s.step(dve.memset(one, 1.0))
            s.step(dve.tensor_tensor_scan(ends, one, n_blk, 0.0, ALU.mult, ALU.add))
            s.step(dve.tensor_scalar(done, ends, block_id[:, 0:1], None, ALU.is_le))
            s.step(dve.tensor_reduce(sc(0), done, AX, ALU.add))
            s.step(dve.tensor_tensor(part, n_blk, done, ALU.mult))
            s.step(dve.tensor_reduce(sc(1), part, AX, ALU.add))
            s.step(dve.tensor_tensor(sc(2), block_id[:, 0:1], sc(1), ALU.subtract))
            s.step(dve.tensor_scalar(sc(3), sc(0), float(STRIDE), None, ALU.mult))
            s.step(dve.scalar_tensor_tensor(sc(4), sc(2), float(BLOCK), sc(3), ALU.mult, ALU.add))
            s.step(dve.tensor_scalar(sc(5), sc(0), float(E - 1), None, ALU.min))
            s.step(dve.tensor_copy(sched_i[:, 0:1], sc(4)))
            s.step(dve.tensor_copy(sched_i[:, 1:2], sc(5)))
            s.step(dve.tensor_scalar(sc(6), ends[:, E - 1:E], 1.0, None, ALU.add))
            s.step(dve.tensor_copy(sched_i[:, 3:4], sc(6)))
            s.step(dve.tensor_scalar(sched_i[:, 2:3], sched_i[:, 3:4], 1, 1,
                                     ALU.logical_shift_right, ALU.logical_shift_left))
            dve.sem_inc(sched_ready, 2)
            for done_sem, count in ((up_done, SEED), (down_done, SEED), (x_turned, SEED),
                                    (pair_free, 2), (xT_moved, 1), (hid_ready, FT),
                                    (hid_step, FT), (wgu_lo_ready, 2 * PARTS), (y_act, 2), (y_dve, 2), (ysb_free, 1)):
                dve.sem_inc(done_sem, count)
            for f in range(1, FT):
                gate_shared(f)
            dve_steps.append(s.n)

            def wgu_part(t, b, part):
                k = part_k(part)
                dve.wait_ge(wgu_hi_ready, t * PARTS + part + 1)
                dve.tensor_tensor(wgu_lo[b][:, k, :], wgu_raw[b][:, k, :],
                                  wgu_hi[b][:, k, :].bitcast(F32), ALU.subtract
                                  ).then_inc(wgu_lo_ready, 1)

            def xT_lo(t, groups):
                for q in groups:
                    dve.wait_ge(xT_hi_ready, t * QX + q + 1)
                    dve.tensor_tensor(xT[:, 2 * q:2 * q + 2, 1, :],
                                      bank[:, 4 + q % 2, 0:2 * BLOCK].rearrange(
                                          "p (k t) -> p k t", k=2),
                                      xT[:, 2 * q:2 * q + 2, 0, :].bitcast(F32), ALU.subtract
                                      ).then_inc(xT_moved, 1)

            def up_part(t, j):
                dve.wait_ge(up_lo_ready, t * STEPS + j + 1)
                dve.tensor_tensor(up_sum[:, j, :], up_lo[:, j, :], bank[:, j, 0:BLOCK], ALU.add
                                  ).then_inc(up_summed, 1)

            def hidden(t, f):
                dve.wait_ge(gate_ready, t * 2 + f + 1)
                dve.wait_ge(up_summed, t * STEPS + 2 * f + 2)
                dve.tensor_tensor(hid[:, f, :], gact[:, f, :], up_sum[:, 2 * f + 1, :],
                                  ALU.mult).then_inc(hid_step, 1)
                dve.tensor_tensor(hid_hi[:, f, 0:BLOCK], gact[:, f, :], up_sum[:, 2 * f + 1, :],
                                  ALU.mult).then_inc(dve_hi, 1)
                dve.wait_ge(hid_step, t * 2 + f + 3)
                dve.wait_ge(dve_hi, t * 2 + f + 1)
                dve.tensor_tensor(hid_lo[:, f, 0:BLOCK], hid[:, f, :],
                                  hid_hi[:, f, 0:BLOCK].bitcast(F32), ALU.subtract
                                  ).then_inc(hid_ready, 1)

            dve.wait_ge(h1_stored, 16 * TILES)
            dve.wait_ge(sched_loaded, 16)
            n = blocks_to_run(dve)
            dve.wait_ge(hid_clear, 2)
            for part in range(PARTS):
                wgu_part(0, 0, part)
            xT_lo(0, range(QX))
            with dve.Fori(0, n, 2) as i:
                for b in range(2):
                    t = i + b
                    wgu_part(t + 1, 1 - b, 0)
                    up_part(t, 0)
                    wgu_part(t + 1, 1 - b, 1)
                    up_part(t, 1)
                    dve.wait_ge(down_done, t * STEPS + SEED)
                    hidden(t, 0)
                    up_part(t, 2)
                    wgu_part(t + 1, 1 - b, 2)
                    up_part(t, 3)
                    hidden(t, 1)
                    xT_lo(t + 1, (0, 1))
                    wgu_part(t + 1, 1 - b, 3)
                    dve.wait_ge(ysb_free, t + 1)
                    for half, r in enumerate((P, REST)):
                        if half:
                            xT_lo(t + 1, (2, 3))
                        dve.wait_ge(down_done, t * STEPS + SEED + 2 * half + 2)
                        dve.tensor_copy(ysb[b][0:r, half, 512:D], bank[0:r, 7, :]
                                        ).then_inc(y_dve, 1)

    lnf_loaded, sdn_loaded = sem("lnf_loaded"), sem("sdn_loaded")
    stores_done = sem("stores_done")
    got_ready = [sem(f"got_ready{j}") for j in range(GOT)]
    sh_down_done, sh_read = sem("sh_down_done"), sem("sh_read")
    weighed, pool_summed, summed = sem("weighed"), sem("pool_summed"), sem("summed")
    part_used = sem("part_used")
    var2_ready, std2_ready, rstd2_ready = sem("var2_ready"), sem("std2_ready"), sem("rstd2_ready")
    normed2, gained = sem("normed2"), sem("gained")
    out_ready, out_stored = sem("out_ready"), sem("out_stored")
    rest_j = range(DVE_J, TOP_K)

    with nc.Block() as block:
        @block.sync
        def _(sp):
            def store(i):
                lo = N_META if i == 0 else 0
                sp.wait_ge(out_ready, i + 1)
                sp.dma_start(out[i * P + lo - N_META:i * P + ROWS[i] - N_META, :],
                             h1[lo:ROWS[i], i, :]).then_inc(out_stored, 16)

            sp.dma_start(sdn[:, :, :], sh_down.rearrange("(k p) c -> p k c", p=P)
                         ).then_inc(sdn_loaded, 16)
            sp.wait_ge(stores_done, 1)
            for i, r in enumerate(ROWS):
                if i >= GOT:
                    sp.wait_ge(summed, (i - GOT + 1) * DVE_J)
                    sp.wait_ge(pool_summed, i - GOT + 1)
                sp.dma_start(h1[0:r, i, :], h1_rows[cols(i), :]).then_inc(got_ready[i % GOT], 16)
                sp.dma_start(got[i % GOT][0:r, :, :],
                             pair_rows[i * P * TOP_K:(i * P + r) * TOP_K, :].rearrange(
                                 "(p j) d -> p j d", j=TOP_K)).then_inc(got_ready[i % GOT], 16)
                if i == 0:
                    sp.dma_start(ln_f[:, :, :], ln[2:4, :].unsqueeze(0).to_broadcast([P, 2, D])
                                 ).then_inc(lnf_loaded, 16)
                if i >= 2:
                    store(i - 2)
            store(TILES - 2)
            store(TILES - 1)
            sp.wait_ge(out_stored, 16 * TILES)

        @block.gpsimd
        def _(pool):
            n = blocks_to_run(pool)
            for b in range(2):
                pool.wait_ge(y_stored[b], n * 16 + 16 * b)
                pool.wait_ge(gathered[b], n * 16 + 32)
                pool.wait_ge(pair_loaded[b], n * 16 + 32)
                pool.wait_ge(wgu_loaded[b], n * 8 + 16)
                pool.wait_ge(wd_loaded[b], n * 8 + 16)
            pool.sem_inc(stores_done, 1)

            s = Chain(pool, pool_step)
            s.n = pool_n[0]

            def add_rest(i):
                r, g = ROWS[i], got[i % GOT]
                for j in rest_j[1:]:
                    pool.wait_ge(weighed, i * len(rest_j) + (j - DVE_J) + 1)
                    if j == rest_j[1] and i >= 2:
                        pool.wait_ge(part_used, i - 1)
                    first = g[0:r, DVE_J, :] if j == rest_j[1] else part_sum[i % 2][0:r, :]
                    ins = pool.tensor_tensor(part_sum[i % 2][0:r, :], first, g[0:r, j, :], ALU.add)
                    if j == rest_j[-1]:
                        ins.then_inc(pool_summed, 1)
                    else:
                        s.step(ins)

            def bias(i):
                x = h1[0:ROWS[i], i, :]
                pool.wait_ge(gained, i + 1)
                pool.tensor_tensor(x, x, ln_f[0:ROWS[i], 1, :], ALU.add).then_inc(out_ready, 1)

            for i in range(TILES):
                add_rest(i)
                if i:
                    bias(i - 1)
            bias(TILES - 1)

        @block.tensor
        def _(pe):
            pe.wait_ge(sdn_loaded, 16)
            for i, r in enumerate(ROWS):
                if i >= 4:
                    pe.wait_ge(sh_read, i - 3)
                for n in range(2):
                    for k in range(FT):
                        mm = pe.matmul(bank[0:r, 2 * (i % 4) + n, :], sh[:, k, cols(i)],
                                       sdn[:, k, n * 512:(n + 1) * 512],
                                       start=(k == 0), stop=(k == FT - 1))
                mm.then_inc(sh_down_done, 1)

        @block.scalar
        def _(act):
            def weigh(i):
                r = ROWS[i]
                act.wait_ge(got_ready[i % GOT], 32 * (i // GOT + 1))
                for j in rest_j:
                    row = got[i % GOT][0:r, j, :]
                    act.activation(row, row, ACT.Copy, scale=weight[0:r, i, j:j + 1]
                                   ).then_inc(weighed, 1)

            weigh(0)
            for i, r in enumerate(ROWS):
                if i + 1 < TILES:
                    weigh(i + 1)
                act.wait_ge(var2_ready, i + 1)
                act.activation(rstd[0:r, 0:1], rstd[0:r, 0:1], ACT.Sqrt).then_inc(std2_ready, 1)
                act.wait_ge(rstd2_ready, i + 1)
                x = h1[0:r, i, :]
                act.activation(x, x, ACT.Identity, bias=mv[0:r, 0:1], scale=rstd[0:r, 1:2]
                               ).then_inc(normed2, 1)

        @block.vector
        def _(dve):
            s = Chain(dve, dve_step)
            s.n = dve_steps[-1]

            def gain(i):
                x = h1[0:ROWS[i], i, :]
                dve.wait_ge(normed2, i + 1)
                if i == 0:
                    dve.wait_ge(lnf_loaded, 16)
                dve.tensor_tensor(x, x, ln_f[0:ROWS[i], 0, :], ALU.mult).then_inc(gained, 1)

            for i, r in enumerate(ROWS):
                x = h1[0:r, i, :]
                dve.wait_ge(sh_down_done, i + 1)
                dve.wait_ge(got_ready[i % GOT], 32 * (i // GOT + 1))
                halves = x.rearrange("p (b n) -> p b n", b=2)
                b = 2 * (i % 4)
                dve.scalar_tensor_tensor(halves, halves, ALPHA, bank[0:r, b:b + 2, :],
                                         ALU.mult, ALU.add).then_inc(sh_read, 1)
                dve.wait_ge(sh_read, i + 1)
                for j in range(DVE_J):
                    dve.scalar_tensor_tensor(x, got[i % GOT][0:r, j, :], weight[0:r, i, j:j + 1],
                                             x, ALU.mult, ALU.add).then_inc(summed, 1)
                    dve.wait_ge(summed, i * DVE_J + j + 1)
                    if j == 0 and i:
                        gain(i - 1)
                dve.wait_ge(pool_summed, i + 1)
                dve.tensor_tensor(x, x, part_sum[i % 2][0:r, :], ALU.add).then_inc(part_used, 1)
                dve.wait_ge(part_used, i + 1)
                s.step(dve.bn_stats(stats[0:r, 0, :], x[:, 0:512]))
                s.step(dve.bn_stats(stats[0:r, 1, :], x[:, 512:D]))
                if i:
                    dve.wait_ge(normed2, i)
                s.step(dve.bn_aggr(mv[0:r, :], stats[0:r, :, :]))
                dve.tensor_scalar(rstd[0:r, 0:1], mv[0:r, 1:2], LN_EPS, None, ALU.add
                                  ).then_inc(var2_ready, 1)
                dve.wait_ge(std2_ready, i + 1)
                s.step(dve.reciprocal(rstd[0:r, 1:2], rstd[0:r, 0:1]))
                dve.scalar_tensor_tensor(mv[0:r, 0:1], mv[0:r, 0:1], -1.0, rstd[0:r, 1:2],
                                         ALU.mult, ALU.mult).then_inc(rstd2_ready, 1)
            gain(TILES - 1)


def kernel(x, meta_tokens, rg_w_in, rg_b_in, rg_conv_w, rg_conv_b, rg_w_gates, rg_b_gates,
           rg_a_param, rg_w_out, attn_w_qkv, attn_sinks, attn_w_o, rel_bias_table, ln_gain,
           ln_bias, router_w, router_bias, expert_w_gu, expert_w_down, shared_w_gu,
           shared_w_down):
    import concourse.bacc as bacc
    from concourse.bass_utils import run_bass_kernel_spmd

    h = np.concatenate([np.asarray(meta_tokens), np.asarray(x)[0]], axis=0)
    per_channel = lambda a: np.asarray(a).reshape(-1, P).T
    arrays = {
        "hT": h.T,
        "h_rows": h,
        "w_in": np.asarray(rg_w_in)[0],
        "chan": np.concatenate([per_channel(a) for a in (rg_b_in, rg_conv_w, rg_conv_b,
                                                         rg_b_gates, rg_a_param)], axis=1),
        "w_gates": np.asarray(rg_w_gates)[0],
        "w_out": np.asarray(rg_w_out)[0],
        "ln": np.stack([np.asarray(ln_gain)[0, 0], np.asarray(ln_bias)[0, 0],
                        np.asarray(ln_gain)[0, 1], np.asarray(ln_bias)[0, 1]]),
        "router_w": np.asarray(router_w)[0],
        "router_b": np.asarray(router_bias),
        "w_gu": np.asarray(expert_w_gu)[0],
        "w_down": np.asarray(expert_w_down)[0],
        "sh_gu": np.asarray(shared_w_gu)[0],
        "sh_down": np.asarray(shared_w_down)[0],
    }
    arrays = {k: np.ascontiguousarray(a) for k, a in arrays.items()}
    nc = bacc.Bacc("TRN2", target_bir_lowering=False, num_devices=1)
    args = [nc.dram_tensor(f"in_{k}", a.shape, F32, kind="ExternalInput").ap()
            for k, a in arrays.items()]
    out = nc.dram_tensor("out", (SEQ, D), F32, kind="ExternalOutput").ap()
    build(nc, *args, out)
    r = run_bass_kernel_spmd(nc, [{f"in_{k}": a for k, a in arrays.items()}], core_ids=[0])
    return r.results[0]["out"].reshape(1, SEQ, D)
```

```python
import concourse.bass as bass
import numpy as np
from concourse import mybir
from concourse.alu_op_type import AluOpType as ALU

ACT = mybir.ActivationFunctionType
AX = mybir.AxisListType.X
F32 = mybir.dt.float32
F32R = mybir.dt.float32r
BF16 = mybir.dt.bfloat16
I32 = mybir.dt.int32
U32 = mybir.dt.uint32

P = 128
D = 1024
KT = D // P
N_META = 16
SEQ = 1024
L = N_META + SEQ
CHUNK = 348
LP = 3 * CHUNK
TILES = -(-L // P)
ROWS = [min(P, L - i * P) for i in range(TILES)]
LRU_BLOCKS = 4
LB = D // LRU_BLOCKS
LT = LB // P
CONV = 4
LRU_C = 8.0
EARLY = KT - LT
AHEAD = 2
E = 64
TOP_K = 8
GROUPS = 8
GSIZE = E // GROUPS
TOP_GROUPS = 4
F = 256
FT = F // P
ROUTED_SCALE = 2.5
ALPHA = 2.0 ** 0.25
LN_EPS = 1e-5
BIG = 3e38

BLOCK = 164
REST = BLOCK - P
REST_HI, REST_LO = P, P + 64
assert REST <= 64
NB_MAX = -(-L // BLOCK)
STRIDE = NB_MAX * BLOCK
LIST_COLS = -(-((E + 1) * STRIDE + 2 * BLOCK) // P)
LIST = LIST_COLS * P
T_MAX = E + (L * TOP_K) // BLOCK + 1
WINDOW = 256
assert WINDOW >= BLOCK and WINDOW & (WINDOW - 1) == 0
ROW_TILES = -(-(L + WINDOW) // P)
ALL_ROWS = ROW_TILES * P

QX = KT // 2
STEPS = 4
SEED = 2 * STEPS

assert FT == 2 and 2 * CHUNK <= (TILES - 2) * P
assert STEPS == QX == 2 * FT == 2 * (D // 512)

C_BIN, C_CW, C_CB, C_BG, C_AP = 0, 16, 48, 56, 72
C_N = 80


class SbufMap:

    def __init__(self, nc):
        self.nc = nc
        self.base = -(-nc.sbuf_base // 64) * 64

    def at(self, name, offset, shape, dtype):
        return self.nc.alloc_sbuf_tensor_at(name, list(shape), dtype, offset=self.base + offset)


class Chain:

    def __init__(self, eng, sem):
        self.eng, self.sem, self.n = eng, sem, 0

    def step(self, ins):
        self.n += 1
        ins.then_inc(self.sem, 1)
        self.eng.wait_ge(self.sem, self.n)


def split_product(pe, out, lhs, rhs, first, last):
    pe.matmul(out, lhs[0], rhs[0], start=first, stop=False)
    pe.matmul(out, lhs[0], rhs[1], start=False, stop=False)
    return pe.matmul(out, lhs[1], rhs[0], start=False, stop=last)


def build(nc, hT, h_rows, w_in, chan, w_gates, w_out, ln, router_w, router_b, w_gu, w_down,
          sh_gu, sh_down, out):
    m = SbufMap(nc)
    sem = lambda name: nc.alloc_semaphore(name)
    bank = nc.alloc_psum_tensor("bank", [P, 8, 512], F32)

    h1_rows = nc.dram_tensor("h1_rows", (ALL_ROWS, D), F32).ap()
    expert_list = nc.dram_tensor("expert_list", (LIST, 2), I32).ap()
    routed_rows = nc.dram_tensor("routed_rows", (ALL_ROWS, D), F32).ap()
    sched_dram = nc.dram_tensor("sched_dram", (P, 4), I32).ap()

    o = 203520
    ident = m.at("ident", o, [P, P], F32)
    tri = m.at("tri", o + 512, [P, P], BF16)
    ones = m.at("ones", o + 768, [P, P], BF16)
    iota_e_i = m.at("iota_e_i", o + 1024, [P, E], I32)
    iota_e = m.at("iota_e", o + 1280, [P, E], F32)
    list_start_i = m.at("list_start_i", o + 1536, [P, E], I32)
    list_start = m.at("list_start", o + 1792, [P, E], F32)
    block_id = m.at("block_id", o + 2112, [P, 1], F32)
    block_id_i = m.at("block_id_i", o + 2144, [P, 1], I32)
    place = m.at("place", o + 2176, [P, TILES, TOP_K], I32)
    rbias = m.at("rbias", o + 2752, [P, E], F32)
    sched_row = m.at("sched_row", o + 3008, [1, 4 * P], I32)
    par = m.at("par", o + 5056, [P, C_N], F32)
    lru_coef = m.at("lru_coef", o + 5376, [P, 2, KT], F32)
    sp_tmp = m.at("sp_tmp", o + 5440, [P, 4, KT], F32)
    stats = m.at("stats", o + 5568, [P, 2, 6], F32)
    mv = m.at("mv", o + 5632, [P, 2], F32)
    rstd = m.at("rstd", o + 5664, [P, 2], F32)
    mask = m.at("mask", o + 5696, [P, E], BF16)
    cum = m.at("cum", o + 5824, [P, 2, E], BF16)

    entry = m.at("entry", 212192, [P, TILES, TOP_K, 2], I32)
    entries = [m.at(f"entries{j}", 203328 + 32 * j, [P, 2, 2], I32) for j in range(2)]
    to_row = [m.at(f"to_row{j}", 203392 + 32 * j, [P, 2], I32) for j in range(2)]
    weight = [m.at(f"weight{j}", 203456 + 32 * j, [P, 2], F32) for j in range(2)]
    blank = m.at("blank", 183136, [P, D], F32)

    hT_raw = m.at("hT_raw", 0, [P, KT, LP], F32)
    hT_lo = m.at("hT_lo", 0, [P, KT, LP], F32R)
    hT_hi = m.at("hT_hi", 33408, [P, KT, LP], F32R)
    NW = 3
    win_raw = [m.at(f"win_raw{j}", 66816 + 8192 * j, [P, KT, P], F32) for j in range(NW)]
    win_lo = [m.at(f"win_lo{j}", 66816 + 8192 * j, [P, KT, P], F32R) for j in range(NW)]
    win_hi = [m.at(f"win_hi{j}", 66816 + 8192 * j + 4096, [P, KT, P], F32R) for j in range(NW)]
    wg_raw = m.at("wg_raw", 91392, [P, LT, 2 * LB], F32)
    wg_lo = m.at("wg_lo", 91392, [P, LT, 2 * LB], F32R)
    wg_hi = m.at("wg_hi", 91392 + 4096, [P, LT, 2 * LB], F32R)
    zT = m.at("zT", 99584, [P, KT, LP], F32)
    xr = m.at("xr", 132992, [P, LT, LP + CONV - 1], F32)
    xc = m.at("xc", 141376, [P, LT, LP], F32)
    xc_hi = m.at("xc_hi", 149728, [P, LT, LP], F32R)
    xc_lo = m.at("xc_lo", 158080, [P, LT, LP], F32R)
    gate_x = m.at("gate_x", 166432, [P, LT, LP], F32)
    gate_a = m.at("gate_a", 174784, [P, LT, LP], F32)
    decay = m.at("decay", 183136, [P, LT, LP], F32)
    th = m.at("th", 191488, [P, LT, LP], F32)
    pads = m.at("pads", 191488, [P, LIST_COLS, 2], I32)
    wout_raw = m.at("wout_raw", 0, [P, KT, D], F32)
    wout_lo = m.at("wout_lo", 0, [P, KT, D], F32R)
    wout_hi = m.at("wout_hi", 33408, [P, KT, D], F32R)
    z_hi = [m.at(f"z_hi{j}", 66816 + 4096 * j, [P, KT, P], F32R) for j in range(2)]
    z_lo = [m.at(f"z_lo{j}", 75008 + 4096 * j, [P, KT, P], F32R) for j in range(2)]
    h_in = m.at("h_in", 83200, [P, D], F32)
    hot = m.at("hot", 87296, [P, TOP_K, E], F32)
    picked = m.at("picked", 89344, [P, TOP_K, E], F32)
    ln_b = m.at("ln_b", 91392, [P, 2, D], F32)
    rw = m.at("rw", 209600, [P, KT, E], F32)
    scores = m.at("scores", 32768, [P, E], F32)
    choice = m.at("choice", 33024, [P, E], F32)
    top_of = m.at("top_of", 66176, [P, GROUPS, 8], F32)
    rowval = m.at("rowval", 66432, [P, E], F32)
    small = m.at("small", 211648, [P, 10, 8], F32)
    idx_u = m.at("idx_u", 211968, [P, 2, 8], U32)
    ghot = m.at("ghot", 212032, [P, TOP_GROUPS, GROUPS], F32)
    expert = m.at("expert", 212160, [P, TOP_K], F32)
    h1T = m.at("h1T", 132992, [P, KT, LP], F32)
    h1 = m.at("h1", 166432, [P, TILES, D], F32)
    sgu = m.at("sgu", 99584, [P, KT, 2 * F], F32)
    sg = m.at("sg", 24576, [P, FT, LP], F32)
    sh = m.at("sh", 32960, [P, FT, LP], F32)
    cnt = m.at("cnt", 123392, [P, 6, E], F32)
    sched = m.at("sched", 124928, [P, 8], F32)
    sched_i = m.at("sched_i", 124960, [P, 4], I32)
    wgu_raw = [m.at(f"wgu_raw{j}", 41472 + 16384 * j, [P, KT, 2 * F], F32) for j in range(2)]
    wgu_lo = [m.at(f"wgu_lo{j}", (182816, 149376)[j], [P, KT, 2 * F], F32R) for j in range(2)]
    wgu_hi = [m.at(f"wgu_hi{j}", (166432, 132992)[j], [P, KT, 2 * F], F32R) for j in range(2)]
    wd_raw = [m.at(f"wd_raw{j}", 74240 + 16384 * j, [P, FT, D], F32) for j in range(2)]
    wd_lo = [m.at(f"wd_lo{j}", 74240 + 16384 * j, [P, FT, D], F32R) for j in range(2)]
    wd_hi = [m.at(f"wd_hi{j}", 74240 + 16384 * j + 8192, [P, FT, D], F32R) for j in range(2)]
    xg = [m.at(f"xg{j}", 8192 * j, [P, 2, D], F32) for j in range(2)]
    ysb = [m.at(f"ysb{j}", 107008 + 8192 * j, [P, 2, D], F32) for j in range(2)]
    xT = m.at("xT", 16384, [P, KT, 2, BLOCK], F32R)
    gact = m.at("gact", 27136, [P, FT, BLOCK], F32)
    hid = m.at("hid", 28480, [P, FT, BLOCK], F32)
    up_lo = m.at("up_lo", 29824, [P, STEPS, BLOCK], F32)
    up_sum = m.at("up_sum", 125056, [P, STEPS, BLOCK], F32)
    y_rest = m.at("y_rest", 199200, [P, 2, 512], F32)
    hid_hi = m.at("hid_hi", 128000, [P, FT, 2 * P], F32R)
    hid_lo = m.at("hid_lo", 130048, [P, FT, P], F32R)
    routed = m.at("routed", 74240, [P, TILES, D], F32)
    ln_f = m.at("ln_f", 66048, [P, 2, D], F32)
    sdn = m.at("sdn", 57856, [P, FT, D], F32)

    consts_ready = sem("consts_ready")
    places_ready, pads_ready = sem("places_ready"), sem("pads_ready")
    list_cleared = sem("list_cleared")
    blank_ready, routed_cleared = sem("blank_ready"), sem("routed_cleared")
    y_stored = [sem(f"y_stored{j}") for j in range(2)]
    par_loaded = sem("par_loaded")
    hT_loaded = [sem(f"hT_loaded{k}") for k in range(KT)]
    hT_hi_ready, hT_lo_ready = sem("hT_hi_ready"), sem("hT_lo_ready")
    win_loaded = [sem(f"win_loaded{j}") for j in range(NW)]
    win_hi_ready, win_lo_ready = sem("win_hi_ready"), sem("win_lo_ready")
    wg_loaded = sem("wg_loaded")
    wg_hi_ready, wg_lo_ready = sem("wg_hi_ready"), sem("wg_lo_ready")
    tile_done = sem("tile_done")
    tile_read = sem("tile_read")
    conv_done = sem("conv_done")
    xc_split = sem("xc_split")
    coef_ready = sem("coef_ready")
    th_ready = sem("th_ready")
    mult2_ready = sem("mult2_ready")
    mult_ready = sem("mult_ready")
    scan_done = sem("scan_done")
    dve_step = sem("dve_step")
    act_step = sem("act_step")
    pool_step = sem("pool_step")
    wout_loaded = sem("wout_loaded")
    wout_hi_ready, wout_lo_pool, wout_lo_dve = (sem("wout_hi_ready"), sem("wout_lo_pool"),
                                                sem("wout_lo_dve"))
    z_hi_ready, z_lo_ready = sem("z_hi_ready"), sem("z_lo_ready")
    dve_steps, pool_n = [], [0]

    cols = lambda i: slice(i * P, i * P + ROWS[i])

    LO_POOL, LO_DVE = (0, 1, 2, 4, 5), (3, 6, 7)
    assert sorted(LO_POOL + LO_DVE) == list(range(KT))

    def wout_lo_part(eng, k):
        eng.wait_ge(wout_hi_ready, k + 1)
        eng.tensor_tensor(wout_lo[:, k, :], wout_raw[:, k, :], wout_hi[:, k, :].bitcast(F32),
                          ALU.subtract).then_inc(wout_lo_pool if k in LO_POOL else wout_lo_dve, 1)

    def wait_wout(pe, k):
        pe.wait_ge(wout_hi_ready, k + 1)
        if k in LO_POOL:
            pe.wait_ge(wout_lo_pool, LO_POOL.index(k) + 1)
        else:
            pe.wait_ge(wout_lo_dve, LO_DVE.index(k) + 1)

    def mix_product(pe, i, k):
        for n in range(2):
            mm = split_product(pe, bank[:, 2 * (i % 2) + n, :],
                               (z_hi[i % 2][:, k, :], z_lo[i % 2][:, k, :]),
                               [w[:, k, n * 512:(n + 1) * 512] for w in (wout_hi, wout_lo)],
                               k == 0, k == KT - 1)
        return mm

    def in_col(n, j):
        return (D if j < LT else 0) + n * LB + (j % LT) * P

    N_IN = 2 * LT * LRU_BLOCKS
    PER = 4 * LT

    with nc.Block() as block:
        @block.sync
        def _(sp):
            def load_win(q):
                n, j = divmod(q, 2 * LT)
                if q >= NW:
                    n0, j0 = divmod(q - NW, 2 * LT)
                    sp.wait_ge(tile_done, PER * n0 + j0 + 1)
                c = in_col(n, j)
                sp.dma_start(win_raw[q % NW][:, :, :],
                             w_in[:, c:c + P].rearrange("(k p) c -> p k c", p=P)
                             ).then_inc(win_loaded[q % NW], 16)

            def load_wg(n):
                if n:
                    sp.wait_ge(tile_done, PER * n)
                sp.dma_start(wg_raw[:, :, :], w_gates[n].rearrange("(k p) c -> p k c", p=P)
                             ).then_inc(wg_loaded, 16)

            load_win(0)
            for k in range(KT):
                sp.dma_start(hT_raw[:, k, 0:L], hT[k * P:(k + 1) * P, :]).then_inc(hT_loaded[k], 16)
                if k == 0:
                    sp.dma_start(par[:, :], chan).then_inc(par_loaded, 16)
            load_win(1)
            load_win(2)
            load_wg(0)
            sp.wait_ge(pads_ready, 2)
            sp.wait_ge(blank_ready, 1)
            sp.dma_start(expert_list.rearrange("(p c) w -> p c w", p=P), pads[:, :, :]
                         ).then_inc(list_cleared, 16)
            for q in range(NW, N_IN):
                load_win(q)
                if q == NW:
                    sp.dma_start(routed_rows.rearrange("(p r) d -> p r d", p=P),
                                 blank[:, :].unsqueeze(1).to_broadcast([P, ROW_TILES, D])
                                 ).then_inc(routed_cleared, 16)
                if q % (2 * LT) == 2 and q > 2 * LT:
                    load_wg(q // (2 * LT))
            sp.wait_ge(tile_done, PER * (LRU_BLOCKS - 1) + 2 * LT)
            sp.dma_start(wout_raw[:, :, :], w_out.rearrange("(k p) c -> p k c", p=P)
                         ).then_inc(wout_loaded, 16)

        @block.gpsimd
        def _(pool):
            s = Chain(pool, pool_step)
            def lo_win(q):
                n, j = divmod(q, 2 * LT)
                pool.wait_ge(win_hi_ready, q + 1)
                pool.tensor_tensor(win_lo[q % NW][:, :, :], win_raw[q % NW][:, :, :],
                                   win_hi[q % NW][:, :, :].bitcast(F32), ALU.subtract
                                   ).then_inc(win_lo_ready, 1)

            s.step(pool.memset(hT_raw[:, :, L:LP], 0.0))
            s.step(pool.memset(xr[:, :, 0:CONV - 1], 0.0))
            lo_win(0)
            s.step(pool.memset(ident[:, :], 0.0))
            s.step(pool.affine_select(out=ident[:, :], in_=ident[:, :], compare_op=ALU.not_equal,
                                      fill=1.0, base=0, pattern=[[-1, P]], channel_multiplier=1))
            s.step(pool.memset(ones[:, :], 1.0))
            s.step(pool.affine_select(out=tri[:, :], in_=ones[:, :], compare_op=ALU.is_gt,
                                      fill=0.0, base=0, pattern=[[1, P]], channel_multiplier=-1))
            s.step(pool.iota(iota_e_i[:, :], pattern=[[1, E]], base=0, channel_multiplier=0))
            s.step(pool.iota(list_start_i[:, :], pattern=[[STRIDE, E]], base=0,
                             channel_multiplier=0))
            s.step(pool.iota(block_id_i[:, :], pattern=[[1, 1]], base=0, channel_multiplier=1))
            s.step(pool.tensor_copy(iota_e[:, :], iota_e_i[:, :]))
            s.step(pool.tensor_copy(list_start[:, :], list_start_i[:, :]))
            s.step(pool.tensor_copy(block_id[:, :], block_id_i[:, :]))
            s.step(pool.memset(cum[:, 0, :], 0.0))
            pool.iota(pads[:, :, 0], pattern=[[1, LIST_COLS]], base=0,
                      channel_multiplier=LIST_COLS).then_inc(places_ready, 1)
            pool.memset(pads[:, :, 1], 0).then_inc(pads_ready, 1)
            pool.memset(blank[:, :], 0.0).then_inc(blank_ready, 1)
            for b in range(2):
                s.step(pool.memset(entries[b][:, :, :], 0))
            pool.wait_ge(blank_ready, 1)
            pool.dma_start(h1_rows[L:, :].rearrange("(p r) d -> p r d", p=ROWS[-1]),
                           blank[0:ROWS[-1], :].unsqueeze(1).to_broadcast(
                               [ROWS[-1], (ALL_ROWS - L) // ROWS[-1], D])).then_inc(y_stored[1], 16)
            pool.iota(entry[:, :, :, 0], pattern=[[P, TILES], [0, TOP_K]], base=0,
                      channel_multiplier=1).then_inc(consts_ready, 1)

            for n in range(LRU_BLOCKS):
                for j in range(2 * LT):
                    if n or j:
                        lo_win(2 * LT * n + j)
                pool.wait_ge(wg_hi_ready, n + 1)
                pool.tensor_tensor(wg_lo[:, :, :], wg_raw[:, :, :], wg_hi[:, :, :].bitcast(F32),
                                   ALU.subtract).then_inc(wg_lo_ready, 1)
            for k in LO_POOL:
                wout_lo_part(pool, k)
            pool_n[0] = s.n

        @block.tensor
        def _(pe):
            for n in range(LRU_BLOCKS):
                for j in range(PER):
                    s = PER * n + j
                    b0 = 3 * (s % 2)
                    if s >= 2:
                        pe.wait_ge(tile_read, s - 1)
                    if j < 2 * LT:
                        q = 2 * LT * n + j
                        pe.wait_ge(win_hi_ready, q + 1)
                        pe.wait_ge(win_lo_ready, q + 1)
                        kt, w = KT, (win_hi[q % NW], win_lo[q % NW])
                        x, c0 = (hT_hi, hT_lo), 0
                    else:
                        pe.wait_ge(xc_split, LT * (n + 1))
                        pe.wait_ge(wg_hi_ready, n + 1)
                        pe.wait_ge(wg_lo_ready, n + 1)
                        kt, w = LT, (wg_hi, wg_lo)
                        x, c0 = (xc_hi, xc_lo), (j - 2 * LT) * P
                    for k in range(kt):
                        if s == 0:
                            pe.wait_ge(hT_hi_ready, k + 1)
                            pe.wait_ge(hT_lo_ready, k + 1)
                        for c in range(3):
                            last = split_product(
                                pe, bank[:, b0 + c, 0:CHUNK],
                                [a[:, k, c0:c0 + P] for a in w],
                                [a[:, k, c * CHUNK:(c + 1) * CHUNK] for a in x],
                                k == 0, k == kt - 1)
                    last.then_inc(tile_done, 1)
            pe.wait_ge(tile_read, PER * LRU_BLOCKS)
            pe.wait_ge(z_hi_ready, AHEAD)
            pe.wait_ge(z_lo_ready, AHEAD)
            for k in range(EARLY):
                wait_wout(pe, k)
                for i in range(AHEAD):
                    mix_product(pe, i, k)

        @block.scalar
        def _(act):
            rows3 = lambda a: a.rearrange("p (c t) -> p c t", c=3)

            def psum_tile(s):
                act.wait_ge(tile_done, s + 1)
                b0 = 3 * (s % 2)
                return bank[:, b0:b0 + 3, 0:CHUNK]

            def hi_win(q):
                act.wait_ge(win_loaded[q % NW], 16 * (q // NW + 1))
                if q >= NW:
                    n0, j0 = divmod(q - NW, 2 * LT)
                    act.wait_ge(tile_done, PER * n0 + j0 + 1)
                act.activation(win_hi[q % NW][:, :, :], win_raw[q % NW][:, :, :], ACT.Copy
                               ).then_inc(win_hi_ready, 1)

            def split_wout(ks):
                act.wait_ge(wout_loaded, 16)
                for k in ks:
                    act.activation(wout_hi[:, k, :], wout_raw[:, k, :], ACT.Copy
                                   ).then_inc(wout_hi_ready, 1)

            hi_win(0)
            act.wait_ge(pool_step, 1)
            for k in range(KT):
                act.wait_ge(hT_loaded[k], 16)
                act.activation(hT_hi[:, k, :], hT_raw[:, k, :], ACT.Copy).then_inc(hT_hi_ready, 1)
            hi_win(1)
            hi_win(2)
            act.wait_ge(par_loaded, 16)
            act.activation(sp_tmp[:, 0, :], par[:, C_AP:C_AP + KT], ACT.Abs).then_inc(act_step, 1)
            act.wait_ge(act_step, 1)
            act.activation(sp_tmp[:, 0, :], sp_tmp[:, 0, :], ACT.Exp, scale=-1.0
                           ).then_inc(act_step, 1)
            act.wait_ge(pool_step, 2)
            for n in range(LRU_BLOCKS):
                s = PER * n
                act.wait_ge(wg_loaded, 16 * (n + 1))
                if n:
                    act.wait_ge(tile_done, s)
                act.activation(wg_hi[:, :, :], wg_raw[:, :, :], ACT.Copy).then_inc(wg_hi_ready, 1)
                for j in range(2 * LT):
                    q = 2 * LT * n + j
                    src = psum_tile(s + j)
                    ch = n * LT + j % LT
                    if j < LT:
                        if n:
                            act.wait_ge(conv_done, LT * (n - 1) + j + 1)
                        act.activation(rows3(xr[:, j, CONV - 1:]), src, ACT.Identity,
                                       bias=par[:, C_BIN + KT + ch:C_BIN + KT + ch + 1]
                                       ).then_inc(tile_read, 1)
                    else:
                        act.activation(rows3(zT[:, ch, :]), src, ACT.Gelu_apprx_tanh,
                                       bias=par[:, C_BIN + ch:C_BIN + ch + 1]
                                       ).then_inc(tile_read, 1)
                    if q + NW < N_IN:
                        hi_win(q + NW)
                if n:
                    act.wait_ge(scan_done, LT * n)
                if n == LRU_BLOCKS - 1:
                    act.wait_ge(tile_done, s + 2 * LT)
                    for i in range(AHEAD):
                        act.activation(z_hi[i][:, 0:EARLY, :], zT[:, 0:EARLY, cols(i)], ACT.Copy
                                       ).then_inc(z_hi_ready, 1)
                for j in range(2 * LT, PER):
                    c = j % LT
                    to = gate_x if j < 3 * LT else gate_a
                    b = C_BG + n * 2 * LT + j - 2 * LT
                    src = psum_tile(s + j)
                    act.activation(rows3(to[:, c, :]), src, ACT.Sigmoid, bias=par[:, b:b + 1]
                                   ).then_inc(tile_read, 1)
                act.wait_ge(tile_read, s + PER)
                if n == 0:
                    act.wait_ge(coef_ready, 1)
                    act.wait_ge(list_cleared, 16)
                    act.wait_ge(routed_cleared, 16)
                    act.wait_ge(y_stored[1], 16)
                for c in range(LT):
                    ch = n * LT + c
                    act.activation(decay[:, c, :], gate_a[:, c, :], ACT.Exp,
                                   scale=lru_coef[:, 0, ch:ch + 1])
                    act.activation(th[:, c, :], gate_a[:, c, :], ACT.Tanh,
                                   scale=lru_coef[:, 1, ch:ch + 1]).then_inc(th_ready, 1)
                if n == LRU_BLOCKS - 1:
                    split_wout(range(KT // 2))
                for c in range(LT):
                    act.wait_ge(mult2_ready, LT * n + c + 1)
                    act.activation(th[:, c, :], th[:, c, :], ACT.Sqrt).then_inc(mult_ready, 1)
            split_wout(range(KT // 2, KT))

        @block.vector
        def _(dve):
            s = Chain(dve, dve_step)
            dve.wait_ge(pool_step, 1)
            for k in range(KT):
                dve.wait_ge(hT_hi_ready, k + 1)
                dve.tensor_tensor(hT_lo[:, k, :], hT_raw[:, k, :], hT_hi[:, k, :].bitcast(F32),
                                  ALU.subtract).then_inc(hT_lo_ready, 1)
            dve.wait_ge(places_ready, 1)
            s.step(dve.tensor_scalar(pads[:, :, 0], pads[:, :, 0], WINDOW - 1, None,
                                     ALU.bitwise_and))
            dve.tensor_scalar(pads[:, :, 0], pads[:, :, 0], L, None, ALU.add
                              ).then_inc(pads_ready, 1)
            a, e, r, q2 = par[:, C_AP:C_AP + KT], sp_tmp[:, 0, :], sp_tmp[:, 1, :], sp_tmp[:, 2, :]
            v = sp_tmp[:, 3, :]
            dve.wait_ge(act_step, 2)
            dve.wait_ge(par_loaded, 16)
            s.step(dve.tensor_scalar(r, e, 2.0, None, ALU.add))
            s.step(dve.reciprocal(r, r))
            s.step(dve.tensor_tensor(r, e, r, ALU.mult))
            s.step(dve.tensor_tensor(q2, r, r, ALU.mult))
            s.step(dve.tensor_scalar(v, q2, 1.0 / 19, 1.0 / 17, ALU.mult, ALU.add))
            for d in (15, 13, 11, 9, 7, 5, 3, 1):
                s.step(dve.tensor_tensor(v, v, q2, ALU.mult))
                s.step(dve.tensor_scalar(v, v, 1.0 / d, None, ALU.add))
            s.step(dve.scalar_tensor_tensor(v, v, 2.0, r, ALU.mult, ALU.mult))
            s.step(dve.tensor_scalar(r, a, -1.0, 0.0, ALU.mult, ALU.max))
            s.step(dve.tensor_tensor(v, v, r, ALU.add))
            s.step(dve.tensor_scalar(lru_coef[:, 0, :], v, -LRU_C, None, ALU.mult))
            dve.tensor_scalar(lru_coef[:, 1, :], v, LRU_C, None, ALU.mult).then_inc(coef_ready, 1)

            for n in range(LRU_BLOCKS):
                for c in range(LT):
                    ch = n * LT + c
                    cw = lambda k: par[:, C_CW + k * KT + ch:C_CW + k * KT + ch + 1]
                    dve.wait_ge(tile_read, PER * n + c + 1)
                    s.step(dve.tensor_scalar(xc[:, c, :], xr[:, c, 0:LP], cw(0),
                                             par[:, C_CB + ch:C_CB + ch + 1], ALU.mult, ALU.add))
                    for k in range(1, CONV):
                        s.step(dve.scalar_tensor_tensor(xc[:, c, :], xr[:, c, k:k + LP], cw(k),
                                                        xc[:, c, :], ALU.mult, ALU.add))
                    dve.tensor_copy(xc_hi[:, c, :], xc[:, c, :]).then_inc(conv_done, 1)
                    dve.wait_ge(conv_done, ch + 1)
                    dve.tensor_tensor(xc_lo[:, c, :], xc[:, c, :], xc_hi[:, c, :].bitcast(F32),
                                      ALU.subtract).then_inc(xc_split, 1)
                if n == LRU_BLOCKS - 1:
                    for i in range(AHEAD):
                        dve.wait_ge(z_hi_ready, i + 1)
                        dve.tensor_tensor(z_lo[i][:, 0:EARLY, :], zT[:, 0:EARLY, cols(i)],
                                          z_hi[i][:, 0:EARLY, :].bitcast(F32), ALU.subtract
                                          ).then_inc(z_lo_ready, 1)
                for c in range(LT):
                    dve.wait_ge(th_ready, LT * n + c + 1)
                    s.step(dve.tensor_tensor(gate_a[:, c, :], decay[:, c, :], decay[:, c, :],
                                             ALU.mult))
                    dve.scalar_tensor_tensor(th[:, c, :], gate_a[:, c, :], 1.0, th[:, c, :],
                                             ALU.add, ALU.mult).then_inc(mult2_ready, 1)
                if n == LRU_BLOCKS - 1:
                    wout_lo_part(dve, LO_DVE[0])
                for c in range(LT):
                    s.step(dve.tensor_tensor(gate_x[:, c, :], xc[:, c, :], gate_x[:, c, :],
                                             ALU.mult))
                    dve.wait_ge(mult_ready, LT * n + c + 1)
                    s.step(dve.tensor_tensor(gate_x[:, c, :], gate_x[:, c, :], th[:, c, :],
                                             ALU.mult))
                    s.step(dve.tensor_tensor_scan(xc[:, c, :], decay[:, c, :], gate_x[:, c, :],
                                                  0.0, ALU.mult, ALU.add))
                    ch = n * LT + c
                    dve.tensor_tensor(zT[:, ch, :], zT[:, ch, :], xc[:, c, :], ALU.mult
                                      ).then_inc(scan_done, 1)
            for k in LO_DVE[1:]:
                wout_lo_part(dve, k)
            dve_steps.append(s.n)

    b_loaded = sem("b_loaded")
    h_loaded, h_used = sem("h_loaded"), sem("h_used")
    z_clear = sem("z_clear")
    mix_ready, var_ready, std_ready = sem("mix_ready"), sem("var_ready"), sem("std_ready")
    centred, norm_ready = sem("centred"), sem("norm_ready")
    turned, h1T_moved = sem("turned"), sem("h1T_moved")
    logits_ready, scores_ready = sem("logits_ready"), sem("scores_ready")
    mask_ready, rank_ready, rank_read = sem("mask_ready"), sem("rank_ready"), sem("rank_read")
    h1_stored = sem("h1_stored")
    place_ready, listed = sem("place_ready"), sem("listed")
    pool_steps = pool_n[0]


    sh_loaded = sem("sh_loaded")
    count_ready = sem("count_ready")
    sched_ready, sched_stored, sched_loaded = (sem("sched_ready"), sem("sched_stored"),
                                               sem("sched_loaded"))
    sh_up, sh_act, sh_ready = sem("sh_up"), sem("sh_act"), sem("sh_ready")
    hid_clear = sem("hid_clear")
    x_turned, up_done, down_done = sem("x_turned"), sem("up_done"), sem("down_done")
    entries_free = sem("entries_free")
    xT_moved, hid_ready, hid_step = sem("xT_moved"), sem("hid_ready"), sem("hid_step")
    y_act, y_dve, ysb_free = sem("y_act"), sem("y_dve"), sem("ysb_free")
    rows3 = lambda a: a.rearrange("p (c t) -> p c t", c=3)

    wgu_loaded = [sem(f"wgu_loaded{j}") for j in range(2)]
    wd_loaded = [sem(f"wd_loaded{j}") for j in range(2)]
    entries_loaded = [sem(f"entries_loaded{j}") for j in range(2)]
    gathered = [sem(f"gathered{j}") for j in range(2)]
    wd_hi_ready, wd_lo_ready = sem("wd_hi_ready"), sem("wd_lo_ready")
    lnf_loaded, sdn_loaded = sem("lnf_loaded"), sem("sdn_loaded")
    y_rest_ready = sem("y_rest_ready")
    gate_ready, dve_hi = sem("gate_ready"), sem("dve_hi")
    wgu_hi_ready, wgu_lo_ready = sem("wgu_hi_ready"), sem("wgu_lo_ready")
    xT_hi_ready, up_lo_ready, up_summed = sem("xT_hi_ready"), sem("up_lo_ready"), sem("up_summed")
    PARTS = 4
    part_k = lambda part: slice(part * KT // PARTS, (part + 1) * KT // PARTS)

    sp_pass, pool_pass = sem("sp_pass"), sem("pool_pass")

    def blocks_to_run(eng):
        return eng.value_load(sched_row[0:1, 2:3], min_val=E, max_val=T_MAX + 1)

    def of_block(eng, t, what, top):
        return eng.value_load(sched_row[0:1, bass.ds(t * 4 + what, 1)], min_val=0, max_val=top)

    with nc.Block() as block:
        @block.sync
        def _(sp):
            for i, r in enumerate(ROWS):
                if i == TILES - 1:
                    sp.wait_ge(z_lo_ready, AHEAD + TILES)
                    sp.dma_start(sgu[:, :, :], sh_gu.rearrange("(k p) c -> p k c", p=P)
                                 ).then_inc(sh_loaded, 16)
                if i:
                    sp.wait_ge(h_used, i)
                sp.dma_start(h_in[0:r, :], h_rows[i * P:i * P + r, :]).then_inc(h_loaded, 16)
                if i == 0:
                    sp.dma_start(ln_b[:, :, :], ln[0:2, :].unsqueeze(0).to_broadcast([P, 2, D])
                                 ).then_inc(b_loaded, 16)
                    sp.dma_start(rw[:, :, :], router_w.rearrange("(k p) e -> p k e", p=P)
                                 ).then_inc(b_loaded, 16)
                    sp.dma_start(rbias[:, :], router_b.to_broadcast([P, E])).then_inc(b_loaded, 16)
                if i >= 1:
                    sp.wait_ge(norm_ready, i)
                    sp.dma_start(h1_rows[cols(i - 1), :], h1[0:ROWS[i - 1], i - 1, :]
                                 ).then_inc(h1_stored, 16)
            i = TILES - 1
            sp.wait_ge(norm_ready, TILES)
            sp.dma_start(h1_rows[cols(i), :], h1[0:ROWS[i], i, :]).then_inc(h1_stored, 16)

            sp.wait_ge(sched_ready, 3)
            sp.dma_start(sched_dram, sched_i[:, :]).then_inc(sched_stored, 16)
            sp.wait_ge(sched_stored, 16)
            sp.dma_start(sched_row[:, :], sched_dram.rearrange("(o b) c -> o (b c)", o=1)
                         ).then_inc(sched_loaded, 16)
            sp.wait_ge(mix_ready, TILES)
            sp.wait_ge(place_ready, TILES)
            sp.dma_start(wgu_raw[0][:, :, :], w_gu[0].rearrange("(k p) c -> p k c", p=P)
                         ).then_inc(wgu_loaded[0], 16)
            sp.dma_start(wd_raw[0][:, :, :], w_down[0].rearrange("(k p) c -> p k c", p=P)
                         ).then_inc(wd_loaded[0], 16)
            sp.wait_ge(sched_loaded, 16)
            sp.wait_ge(listed, 16 * TILES * TOP_K)

            n = blocks_to_run(sp)
            def load_entries(t, b):
                row = of_block(sp, t, 0, LIST - BLOCK)
                sp.wait_ge(entries_free, t + 1)
                sp.sem_inc(sp_pass, 1)
                sp.dma_start(entries[b][:, 0, :], expert_list[bass.ds(row, P), :]
                             ).then_inc(entries_loaded[b], 16)
                sp.dma_start(entries[b][0:REST, 1, :], expert_list[bass.ds(row + P, REST), :]
                             ).then_inc(entries_loaded[b], 16)

            def load_block(t, b):
                load_entries(t, b)
                e = of_block(sp, t, 1, E - 1)
                sp.wait_ge(wgu_lo_ready, t * PARTS + PARTS)
                sp.sem_inc(sp_pass, 1)
                sp.dma_start(wgu_raw[b][:, :, :],
                             w_gu[bass.ds(e, 1)].rearrange("o (k p) c -> p (o k) c", p=P)
                             ).then_inc(wgu_loaded[b], 16)
                sp.wait_ge(down_done, t * STEPS + STEPS)
                sp.sem_inc(sp_pass, 1)
                sp.dma_start(wd_raw[b][:, :, :],
                             w_down[bass.ds(e, 1)].rearrange("o (k p) c -> p (o k) c", p=P)
                             ).then_inc(wd_loaded[b], 16)

            load_entries(0, 0)
            sp.wait_ge(gathered[0], 32)
            with sp.Fori(0, n - 2, 2) as i:
                for b in range(2):
                    load_block(i + (b + 1), 1 - b)
            load_block(n - 1, 1)
            load_entries(n, 0)
            sp.wait_ge(wgu_lo_ready, n * PARTS + PARTS)
            sp.sem_inc(sp_pass, 1)
            sp.dma_start(wgu_raw[0][:, 0, 0:16], w_gu[0, 0:P, 0:16]).then_inc(wgu_loaded[0], 16)
            load_entries(n + 1, 1)
            sp.wait_ge(wgu_lo_ready, n * PARTS + 2 * PARTS)
            sp.sem_inc(sp_pass, 1)
            sp.dma_start(sdn[:, :, :], sh_down.rearrange("(k p) c -> p k c", p=P)
                         ).then_inc(sdn_loaded, 16)
            sp.dma_start(ln_f[:, :, :], ln[2:4, :].unsqueeze(0).to_broadcast([P, 2, D])
                         ).then_inc(lnf_loaded, 16)
            sp.wait_ge(down_done, n * STEPS + STEPS)
            sp.sem_inc(sp_pass, 1)
            sp.dma_start(wd_raw[0][:, :, :], w_down[0].rearrange("(k p) c -> p k c", p=P)
                         ).then_inc(wd_loaded[0], 16)

        @block.gpsimd
        def _(pool):
            s = Chain(pool, pool_step)
            s.n = pool_steps
            pool.memset(h1T[:, :, L:LP], 0.0).then_inc(z_clear, 1)
            pool.wait_ge(list_cleared, 16)

            def enlist(i):
                r = ROWS[i]
                pool.wait_ge(place_ready, i + 1)
                for j in range(TOP_K):
                    pool.indirect_dma_start(
                        out=expert_list,
                        out_offset=bass.IndirectOffsetOnAxis(ap=place[0:r, i, j:j + 1], axis=0),
                        in_=entry[0:r, i, j, :], in_offset=None).then_inc(listed, 16)

            for i, r in enumerate(ROWS):
                pool.wait_ge(centred, i + 1)
                if i == 0:
                    pool.wait_ge(b_loaded, 48)
                s.step(pool.tensor_tensor(h1[0:r, i, :], h1[0:r, i, :], ln_b[0:r, 0, :], ALU.mult))
                pool.tensor_tensor(h1[0:r, i, :], h1[0:r, i, :], ln_b[0:r, 1, :], ALU.add
                                   ).then_inc(norm_ready, 1)
                if i >= 3:
                    enlist(i - 3)
            pool.wait_ge(z_lo_ready, AHEAD + TILES)
            pool.memset(hid_hi[:, :, :].bitcast(F32), 0.0).then_inc(hid_clear, 1)
            pool.memset(hid_lo[:, :, :].bitcast(F32), 0.0).then_inc(hid_clear, 1)
            for i in range(TILES - 3, TILES):
                enlist(i)
            pool_n[0] = s.n

            def fetch(t, b, i):
                pool.wait_ge(entries_loaded[b], i * 16 + 32)
                pool.wait_ge(x_turned, t * STEPS + STEPS)
                pool.sem_inc(pool_pass, 1)
                for half, r in enumerate((P, REST)):
                    pool.indirect_dma_start(
                        out=xg[b][0:r, half, :], out_offset=None, in_=h1_rows,
                        in_offset=bass.IndirectOffsetOnAxis(ap=entries[b][0:r, half, 0:1],
                                                            axis=0)).then_inc(gathered[b], 16)

            def keep_rows(b):
                pool.tensor_copy(to_row[b][:, :], entries[b][:, :, 0])
                pool.tensor_copy(weight[b][:, :], entries[b][:, :, 1].bitcast(F32)
                                 ).then_inc(entries_free, 1)

            pool.wait_ge(sched_loaded, 16)
            pool.wait_ge(routed_cleared, 16)
            n = blocks_to_run(pool)
            pool.wait_ge(h1_stored, 16 * TILES)
            def lo_wd(b):
                pool.tensor_tensor(wd_lo[b][:, :, :], wd_raw[b][:, :, :],
                                   wd_hi[b][:, :, :].bitcast(F32), ALU.subtract
                                   ).then_inc(wd_lo_ready, 1)

            fetch(0, 0, 0)
            fetch(1, 1, 0)
            pool.wait_ge(gathered[0], 32)
            keep_rows(0)
            pool.wait_ge(wd_hi_ready, FT)
            lo_wd(0)
            with pool.Fori(0, n, 2) as i:
                for b in range(2):
                    t = i + b
                    fetch(t + 2, b, i + 2)
                    pool.wait_ge(y_stored[1 - b], i * 16 + 16 + 16 * b)
                    pool.sem_inc(ysb_free, 1)
                    pool.wait_ge(gathered[1 - b], i * 16 + 32 + 32 * b)
                    pool.sem_inc(pool_pass, 1)
                    keep_rows(1 - b)
                    pool.wait_ge(wd_hi_ready, t * FT + 2 * FT)
                    pool.sem_inc(pool_pass, 1)
                    lo_wd(1 - b)
                    pool.wait_ge(entries_free, t + 4)
                    pool.wait_ge(y_act, t + 1)
                    pool.wait_ge(y_dve, t * 4 + 8)
                    pool.sem_inc(pool_pass, 1)
                    for half, r in enumerate((P, REST)):
                        pool.indirect_dma_start(
                            out=routed_rows,
                            out_offset=bass.IndirectOffsetOnAxis(ap=to_row[b][0:r, half:half + 1],
                                                                 axis=0),
                            in_=ysb[b][0:r, half, :], in_offset=None, compute_op=ALU.add
                            ).then_inc(y_stored[b], 16)

        @block.tensor
        def _(pe):
            def mix(i):
                if i >= 2:
                    pe.wait_ge(h_used, i - 1)
                pe.wait_ge(z_hi_ready, AHEAD + i + 1)
                pe.wait_ge(z_lo_ready, AHEAD + i + 1)
                for k in range(EARLY if i < AHEAD else 0, KT):
                    if i == 0:
                        wait_wout(pe, k)
                    mm = mix_product(pe, i, k)
                mm.then_inc(mix_ready, 1)

            def turn(i):
                r = ROWS[i]
                pe.wait_ge(norm_ready, i + 1)
                if i == 0:
                    pe.wait_ge(consts_ready, 1)
                if i:
                    pe.wait_ge(h1T_moved, i)
                for k in range(KT):
                    mm = pe.transpose(bank[:, 4 + k // 4, (k % 4) * P:(k % 4) * P + r],
                                      h1[0:r, i, k * P:(k + 1) * P], ident[0:r, 0:r])
                mm.then_inc(turned, 1)

            def logits(i):
                r = ROWS[i]
                pe.wait_ge(h1T_moved, i + 1)
                if i == 0:
                    pe.wait_ge(b_loaded, 48)
                if i >= 2:
                    pe.wait_ge(rank_read, i - 1)
                for k in range(KT):
                    mm = pe.matmul(bank[0:r, 6 + i % 2, 0:E], h1T[:, k, cols(i)], rw[:, k, :],
                                   start=(k == 0), stop=(k == KT - 1))
                mm.then_inc(logits_ready, 1)

            def rank(i):
                r = ROWS[i]
                pe.wait_ge(mask_ready, i + 1)
                pe.matmul(bank[0:r, 6 + i % 2, E:2 * E], ones[:, 0:r], cum[:, i % 2, :],
                          start=True, stop=False)
                pe.matmul(bank[0:r, 6 + i % 2, E:2 * E], tri[0:r, 0:r], mask[0:r, :],
                          start=False, stop=True).then_inc(rank_ready, 1)

            def shared_up(f, half, c):
                if f and c == 0:
                    pe.wait_ge((sh_act, sh_ready)[half], f)
                for k in range(KT):
                    mm = pe.matmul(bank[:, 3 * half + c, 0:CHUNK],
                                   sgu[:, k, half * F + f * P:half * F + (f + 1) * P],
                                   h1T[:, k, c * CHUNK:(c + 1) * CHUNK],
                                   start=(k == 0), stop=(k == KT - 1))
                if c == 2:
                    mm.then_inc(sh_up, 1)

            for i in range(TILES + 3):
                if i < TILES:
                    mix(i)
                if i == TILES:
                    pe.wait_ge(sh_loaded, 16)
                    pe.wait_ge(h_used, TILES)
                    for c in range(2):
                        shared_up(0, 0, c)
                if i == 2:
                    turn(0)
                if 2 <= i <= TILES:
                    turn(i - 1)
                if 0 <= i - 2 < TILES:
                    logits(i - 2)
                if i == TILES + 1:
                    pe.wait_ge(h1T_moved, TILES)
                    for half, c in ((0, 2), (1, 0), (1, 1)):
                        shared_up(0, half, c)
                if i == TILES + 2:
                    shared_up(0, 1, 2)
                    shared_up(1, 0, 0)
                if 0 <= i - 3:
                    rank(i - 3)
            r, t = ROWS[-1], TILES - 1
            pe.wait_ge(rank_read, TILES)
            pe.matmul(bank[:, 7, 0:E], ones[:, :], cum[:, t % 2, :], start=True, stop=False)
            pe.matmul(bank[:, 7, 0:E], ones[0:r, :], mask[0:r, :], start=False, stop=True
                      ).then_inc(count_ready, 1)
            for half, c in ((0, 1), (0, 2), (1, 0), (1, 1), (1, 2)):
                shared_up(1, half, c)
            pe.wait_ge(sh_act, FT)
            pe.wait_ge(sh_ready, FT)
            pe.wait_ge(sched_ready, 1)

            def turn_block(t, b, groups):
                for q in groups:
                    pe.wait_ge(xT_moved, t * QX + max(q, 1))
                    for k in (2 * q, 2 * q + 1):
                        o = (k % 2) * BLOCK
                        pe.transpose(bank[:, 4 + q % 2, o:o + P], xg[b][:, 0, k * P:(k + 1) * P],
                                     ident[:, :])
                        mm = pe.transpose(bank[:, 4 + q % 2, o + P:o + BLOCK],
                                          xg[b][0:REST, 1, k * P:(k + 1) * P],
                                          ident[0:REST, 0:REST])
                    mm.then_inc(x_turned, 1)

            pe.wait_ge(sched_loaded, 16)
            n = blocks_to_run(pe)
            pe.wait_ge(gathered[0], 32)
            turn_block(0, 0, range(QX))
            with pe.Fori(0, n, 2) as i:
                for b in range(2):
                    t = i + b
                    pe.wait_ge(wgu_hi_ready, t * PARTS + PARTS)
                    pe.wait_ge(wgu_lo_ready, t * PARTS + 3 * PARTS)
                    pe.wait_ge(hid_ready, t * 2 + 2)
                    for f in range(FT):
                        for half in range(2):
                            for k in range(KT):
                                if f == 0 and half == 0 and k % 2 == 0:
                                    pe.wait_ge(xT_moved, t * QX + k // 2 + 2)
                                c = half * F + f * P
                                pe.matmul(bank[:, 2 * f + half, 0:2 * BLOCK],
                                          wgu_hi[b][:, k, c:c + P],
                                          xT[:, k, :, :].rearrange("p h t -> p (h t)"),
                                          start=(k == 0), stop=False)
                                mm = pe.matmul(bank[:, 2 * f + half, 0:BLOCK],
                                               wgu_lo[b][:, k, c:c + P], xT[:, k, 0, :],
                                               start=False, stop=(k == KT - 1))
                            mm.then_inc(up_done, 1)
                    pe.wait_ge(gathered[1 - b], i * 16 + 32 + 32 * b)
                    for half in range(2):
                        turn_block(t + 1, 1 - b, (2 * half, 2 * half + 1))
                        if half == 0:
                            pe.wait_ge(wd_hi_ready, t * FT + FT)
                            pe.wait_ge(wd_lo_ready, t + 1)
                        for k in range(FT):
                            if half == 0:
                                pe.wait_ge(hid_ready, t * 2 + k + 3)
                            for c in range(2):
                                w = [w[b][:, k, c * 512:(c + 1) * 512] for w in (wd_hi, wd_lo)]
                                first, last = k == 0, k == FT - 1
                                if half == 0:
                                    if first:
                                        pe.wait_ge(y_dve, t * 4 + 2 + c)
                                    mm = split_product(pe, bank[:, 6 + c, :],
                                                       (hid_hi[:, k, 0:P], hid_lo[:, k, :]), w,
                                                       first, last)
                                else:
                                    if first and c == 0:
                                        pe.wait_ge(y_act, t + 1)
                                    elif first:
                                        pe.wait_ge(y_dve, t * 4 + 5)
                                    pe.matmul(bank[:, 6 + c, :], hid_hi[:, k, P:2 * P], w[0],
                                              start=first, stop=False)
                                    mm = pe.matmul(bank[:, 6 + c, :], hid_hi[:, k, P:2 * P], w[1],
                                                   start=False, stop=last)
                                if last:
                                    mm.then_inc(down_done, 1)

        @block.scalar
        def _(act):
            def split_z(i):
                r = ROWS[i]
                if i >= 2:
                    act.wait_ge(mix_ready, i - 1)
                k = slice(EARLY if i < AHEAD else 0, KT)
                act.activation(z_hi[i % 2][:, k, 0:r], zT[:, k, cols(i)], ACT.Copy
                               ).then_inc(z_hi_ready, 1)

            split_z(0)
            split_z(1)
            for i in range(TILES + 2):
                if i + 2 < TILES:
                    split_z(i + 2)
                if i < TILES:
                    r = ROWS[i]
                    act.wait_ge(var_ready, i + 1)
                    act.activation(rstd[0:r, 0:1], rstd[0:r, 0:1], ACT.Sqrt).then_inc(std_ready, 1)
                if 0 <= i - 1 < TILES:
                    t, r = i - 1, ROWS[i - 1]
                    act.wait_ge(turned, t + 1)
                    if t == 0:
                        act.wait_ge(z_clear, 1)
                    act.activation(h1T[:, :, cols(t)],
                                   bank[:, 4:6, :].rearrange("p b (k t) -> p (b k) t", t=P)[:, :, 0:r],
                                   ACT.Copy).then_inc(h1T_moved, 1)
                if 0 <= i - 2:
                    t, r = i - 2, ROWS[i - 2]
                    act.wait_ge(logits_ready, t + 1)
                    if t:
                        act.wait_ge(mask_ready, t)
                    act.activation(scores[0:r, :], bank[0:r, 6 + t % 2, 0:E], ACT.Sigmoid
                                   ).then_inc(scores_ready, 1)

            for f in range(FT):
                act.wait_ge(sh_up, 2 * f + 1)
                act.activation(rows3(sg[:, f, :]), bank[:, 0:3, 0:CHUNK], ACT.Silu
                               ).then_inc(sh_act, 1)

            def move_xT(t, groups):
                for q in groups:
                    act.wait_ge(x_turned, t * STEPS + SEED + q + 1)
                    act.activation(xT[:, 2 * q:2 * q + 2, 0, :],
                                   bank[:, 4 + q % 2, 0:2 * BLOCK].rearrange(
                                       "p (k t) -> p k t", k=2), ACT.Copy
                                   ).then_inc(xT_hi_ready, 1)

            def wgu_part(b, part):
                k = part_k(part)
                act.activation(wgu_hi[b][:, k, :], wgu_raw[b][:, k, :], ACT.Copy
                               ).then_inc(wgu_hi_ready, 1)

            def wd_part(b, k):
                act.activation(wd_hi[b][:, k, :], wd_raw[b][:, k, :], ACT.Copy
                               ).then_inc(wd_hi_ready, 1)

            def up_part(t, j):
                act.wait_ge(up_done, t * STEPS + SEED + j + 1)
                act.activation(up_lo[:, j, :], bank[:, j, BLOCK:2 * BLOCK], ACT.Copy
                               ).then_inc(up_lo_ready, 1)

            def silu(t, f):
                act.wait_ge(up_summed, t * STEPS + 2 * f + 1)
                act.activation(gact[:, f, :], up_sum[:, 2 * f, :], ACT.Silu).then_inc(gate_ready, 1)

            act.wait_ge(h1_stored, 16 * TILES)
            act.wait_ge(sched_loaded, 16)
            n = blocks_to_run(act)
            act.wait_ge(wgu_loaded[0], 16)
            for part in range(PARTS):
                wgu_part(0, part)
            act.wait_ge(wd_loaded[0], 16)
            for k in range(FT):
                wd_part(0, k)
            move_xT(0, range(QX))
            act.wait_ge(sh_up, 2 * FT)
            with act.Fori(0, n, 2) as i:
                for b in range(2):
                    t = i + b
                    act.wait_ge(wgu_loaded[1 - b], i * 8 + 16 + 16 * b)
                    wgu_part(1 - b, 0)
                    wgu_part(1 - b, 1)
                    up_part(t, 0)
                    wgu_part(1 - b, 2)
                    up_part(t, 1)
                    act.wait_ge(hid_step, t * 2 + 2)
                    silu(t, 0)
                    wgu_part(1 - b, 3)
                    up_part(t, 2)
                    silu(t, 1)
                    act.wait_ge(wd_loaded[1 - b], i * 8 + 16 + 16 * b)
                    wd_part(1 - b, 0)
                    up_part(t, 3)
                    act.wait_ge(ysb_free, t + 1)
                    act.wait_ge(entries_free, t + 3)
                    move_xT(t + 1, (0, 1))
                    act.wait_ge(down_done, t * STEPS + SEED + 1)
                    act.activation(ysb[b][:, 0, 0:512], bank[:, 6, :], ACT.Copy,
                                   scale=weight[b][:, 0:1]).then_inc(y_act, 1)
                    wd_part(1 - b, 1)
                    move_xT(t + 1, (2, 3))
                    for c in range(2):
                        act.wait_ge(down_done, t * STEPS + SEED + 3 + c)
                        act.activation(y_rest[0:REST, c, :],
                                       bank[REST_LO - P:REST_LO - P + REST, 6 + c, :], ACT.Copy
                                       ).then_inc(y_rest_ready, 1)

        @block.vector
        def _(dve):
            s = Chain(dve, dve_step)
            s.n = dve_steps[-1]

            def split_z(i):
                r = ROWS[i]
                k = slice(EARLY if i < AHEAD else 0, KT)
                dve.wait_ge(z_hi_ready, AHEAD + i + 1)
                dve.tensor_tensor(z_lo[i % 2][:, k, 0:r], zT[:, k, cols(i)],
                                  z_hi[i % 2][:, k, 0:r].bitcast(F32), ALU.subtract
                                  ).then_inc(z_lo_ready, 1)

            def norm_begin(i):
                r = ROWS[i]
                dve.wait_ge(mix_ready, i + 1)
                dve.wait_ge(h_loaded, 16 * (i + 1))
                dve.scalar_tensor_tensor(
                    h1[0:r, i, :].rearrange("p (b n) -> p b n", b=2),
                    h_in[0:r, :].rearrange("p (b n) -> p b n", b=2), ALPHA,
                    bank[0:r, 2 * (i % 2):2 * (i % 2) + 2, :], ALU.mult, ALU.add
                    ).then_inc(h_used, 1)
                dve.wait_ge(h_used, i + 1)
                s.step(dve.bn_stats(stats[0:r, 0, :], h1[0:r, i, 0:512]))
                s.step(dve.bn_stats(stats[0:r, 1, :], h1[0:r, i, 512:D]))
                s.step(dve.bn_aggr(mv[0:r, :], stats[0:r, :, :]))
                dve.tensor_scalar(rstd[0:r, 0:1], mv[0:r, 1:2], LN_EPS, None, ALU.add
                                  ).then_inc(var_ready, 1)

            def norm_end(i):
                r = ROWS[i]
                dve.wait_ge(std_ready, i + 1)
                s.step(dve.reciprocal(rstd[0:r, 1:2], rstd[0:r, 0:1]))
                dve.tensor_scalar(h1[0:r, i, :], h1[0:r, i, :], mv[0:r, 0:1], rstd[0:r, 1:2],
                                  ALU.subtract, ALU.mult).then_inc(centred, 1)

            def route(i):
                r = ROWS[i]
                if i == 0:
                    dve.wait_ge(b_loaded, 48)
                sm = lambda j: small[0:r, j, :]
                dve.wait_ge(scores_ready, i + 1)
                s.step(dve.tensor_tensor(choice[0:r, :], scores[0:r, :], rbias[0:r, :], ALU.add))
                for g in range(GROUPS):
                    ins = dve.max(top_of[0:r, g, :], choice[0:r, g * GSIZE:(g + 1) * GSIZE])
                s.step(ins)
                s.step(dve.tensor_tensor(sm(0), top_of[0:r, :, 0], top_of[0:r, :, 1], ALU.add))
                s.step(dve.max(sm(1), sm(0)))
                s.step(dve.max_index(idx_u[0:r, 0, :], sm(1), sm(0)))
                s.step(dve.tensor_copy(sm(2), idx_u[0:r, 0, :]))
                s.step(dve.tensor_tensor(
                    ghot[0:r, :, :],
                    iota_e[0:r, 0:GROUPS].unsqueeze(1).to_broadcast([r, TOP_GROUPS, GROUPS]),
                    sm(2)[:, 0:TOP_GROUPS].unsqueeze(2).to_broadcast([r, TOP_GROUPS, GROUPS]),
                    ALU.is_equal))
                s.step(dve.tensor_reduce(sm(3), ghot[0:r, :, :].rearrange("p j g -> p g j"), AX,
                                         ALU.add))
                s.step(dve.tensor_scalar(sm(4), sm(3), -1.0, BIG, ALU.add, ALU.mult))
                by_group = choice[0:r, :].rearrange("p (g m) -> p g m", g=GROUPS)
                wide = lambda v: v.unsqueeze(2).to_broadcast([r, GROUPS, GSIZE])
                s.step(dve.tensor_tensor(by_group, by_group, wide(sm(3)), ALU.mult))
                s.step(dve.tensor_tensor(by_group, by_group, wide(sm(4)), ALU.add))
                s.step(dve.max(sm(5), choice[0:r, :]))
                s.step(dve.max_index(idx_u[0:r, 1, :], sm(5), choice[0:r, :]))
                s.step(dve.tensor_copy(expert[0:r, :], idx_u[0:r, 1, :]))
                s.step(dve.tensor_tensor(
                    hot[0:r, :, :], iota_e[0:r, :].unsqueeze(1).to_broadcast([r, TOP_K, E]),
                    expert[0:r, :].unsqueeze(2).to_broadcast([r, TOP_K, E]), ALU.is_equal))
                s.step(dve.tensor_tensor(
                    picked[0:r, :, :], hot[0:r, :, :],
                    scores[0:r, :].unsqueeze(1).to_broadcast([r, TOP_K, E]), ALU.mult))
                s.step(dve.tensor_reduce(sm(7), picked[0:r, :, :], AX, ALU.add))
                s.step(dve.tensor_reduce(sm(8)[:, 0:1], sm(7), AX, ALU.add))
                s.step(dve.tensor_scalar(sm(8)[:, 1:2], sm(8)[:, 0:1], 1e-20, None, ALU.add))
                s.step(dve.reciprocal(sm(8)[:, 2:3], sm(8)[:, 1:2]))
                s.step(dve.tensor_scalar(entry[0:r, i, :, 1].bitcast(F32), sm(7),
                                         sm(8)[:, 2:3], ROUTED_SCALE,
                                         ALU.mult, ALU.mult))
                with nc.allow_low_precision(reason="at most one 1 is summed"):
                    dve.tensor_reduce(mask[0:r, :], hot[0:r, :, :].rearrange("p j e -> p e j"),
                                      AX, ALU.add).then_inc(mask_ready, 1)

            def places(i):
                r = ROWS[i]
                dve.wait_ge(rank_ready, i + 1)
                dve.tensor_tensor(rowval[0:r, :], list_start[0:r, :],
                                  bank[0:r, 6 + i % 2, E:2 * E], ALU.add).then_inc(rank_read, 1)
                dve.wait_ge(rank_read, i + 1)
                if i + 1 < TILES:
                    s.step(dve.tensor_tensor(cum[:, (i + 1) % 2, :], cum[:, i % 2, :],
                                             mask[:, :], ALU.add))
                s.step(dve.tensor_tensor(
                    picked[0:r, :, :], hot[0:r, :, :],
                    rowval[0:r, :].unsqueeze(1).to_broadcast([r, TOP_K, E]), ALU.mult))
                s.step(dve.tensor_reduce(small[0:r, 9, :], picked[0:r, :, :], AX, ALU.add))
                dve.tensor_copy(place[0:r, i, :], small[0:r, 9, :]).then_inc(place_ready, 1)

            dve.wait_ge(consts_ready, 1)
            split_z(0)
            split_z(1)
            for i in range(TILES + 3):
                if i + 2 < TILES:
                    split_z(i + 2)
                if i < TILES:
                    norm_begin(i)
                if 0 <= i - 3:
                    places(i - 3)
                if i < TILES:
                    norm_end(i)
                if 0 <= i - 2 < TILES:
                    route(i - 2)
            dve_steps.append(s.n)

            def gate_shared(f):
                dve.wait_ge(sh_act, f + 1)
                dve.wait_ge(sh_up, 2 * f + 2)
                dve.tensor_tensor(rows3(sh[:, f, :]), rows3(sg[:, f, :]), bank[:, 3:6, 0:CHUNK],
                                  ALU.mult).then_inc(sh_ready, 1)

            gate_shared(0)
            n_tok, n_blk, ends, done, part, one = (cnt[:, j, :] for j in range(6))
            sc = lambda j: sched[:, j:j + 1]
            dve.wait_ge(count_ready, 1)
            dve.tensor_copy(n_tok, bank[:, 7, 0:E]).then_inc(sched_ready, 1)
            dve.wait_ge(sched_ready, 1)
            s.step(dve.tensor_scalar(n_blk, n_tok, float(BLOCK), 1.0, ALU.is_gt, ALU.add))
            for k in range(2, NB_MAX):
                s.step(dve.scalar_tensor_tensor(n_blk, n_tok, float(k * BLOCK), n_blk, ALU.is_gt,
                                                ALU.add))
            s.step(dve.memset(one, 1.0))
            s.step(dve.tensor_tensor_scan(ends, one, n_blk, 0.0, ALU.mult, ALU.add))
            s.step(dve.tensor_scalar(done, ends, block_id[:, 0:1], None, ALU.is_le))
            s.step(dve.tensor_reduce(sc(0), done, AX, ALU.add))
            s.step(dve.tensor_tensor(part, n_blk, done, ALU.mult))
            s.step(dve.tensor_reduce(sc(1), part, AX, ALU.add))
            s.step(dve.tensor_tensor(sc(2), block_id[:, 0:1], sc(1), ALU.subtract))
            s.step(dve.tensor_scalar(sc(3), sc(0), float(STRIDE), None, ALU.mult))
            s.step(dve.scalar_tensor_tensor(sc(4), sc(2), float(BLOCK), sc(3), ALU.mult, ALU.add))
            s.step(dve.tensor_scalar(sc(5), sc(0), float(E - 1), None, ALU.min))
            s.step(dve.tensor_copy(sched_i[:, 0:1], sc(4)))
            s.step(dve.tensor_copy(sched_i[:, 1:2], sc(5)))
            s.step(dve.tensor_scalar(sc(6), ends[:, E - 1:E], 1.0, None, ALU.add))
            s.step(dve.tensor_copy(sched_i[:, 3:4], sc(6)))
            s.step(dve.tensor_scalar(sched_i[:, 2:3], sched_i[:, 3:4], 1, 1,
                                     ALU.logical_shift_right, ALU.logical_shift_left))
            dve.sem_inc(sched_ready, 2)
            for done_sem, count in ((up_done, SEED), (down_done, SEED), (x_turned, SEED),
                                    (entries_free, 2), (xT_moved, 1), (hid_ready, FT),
                                    (hid_step, FT), (wgu_lo_ready, 2 * PARTS), (y_dve, 4),
                                    (ysb_free, 1)):
                dve.sem_inc(done_sem, count)
            dve_steps.append(s.n)

            def wgu_part(t, b, part):
                k = part_k(part)
                dve.wait_ge(wgu_hi_ready, t * PARTS + part + 1)
                dve.tensor_tensor(wgu_lo[b][:, k, :], wgu_raw[b][:, k, :],
                                  wgu_hi[b][:, k, :].bitcast(F32), ALU.subtract
                                  ).then_inc(wgu_lo_ready, 1)

            def xT_lo(t, groups):
                for q in groups:
                    dve.wait_ge(xT_hi_ready, t * QX + q + 1)
                    dve.tensor_tensor(xT[:, 2 * q:2 * q + 2, 1, :],
                                      bank[:, 4 + q % 2, 0:2 * BLOCK].rearrange(
                                          "p (k t) -> p k t", k=2),
                                      xT[:, 2 * q:2 * q + 2, 0, :].bitcast(F32), ALU.subtract
                                      ).then_inc(xT_moved, 1)

            def up_part(t, j):
                dve.wait_ge(up_lo_ready, t * STEPS + j + 1)
                dve.tensor_tensor(up_sum[:, j, :], up_lo[:, j, :], bank[:, j, 0:BLOCK], ALU.add
                                  ).then_inc(up_summed, 1)

            def hidden(t, f):
                dve.wait_ge(gate_ready, t * 2 + f + 1)
                dve.wait_ge(up_summed, t * STEPS + 2 * f + 2)
                dve.tensor_tensor(hid[:, f, :], gact[:, f, :], up_sum[:, 2 * f + 1, :],
                                  ALU.mult).then_inc(hid_step, 1)
                dve.tensor_tensor(hid_hi[:, f, 0:BLOCK], gact[:, f, :], up_sum[:, 2 * f + 1, :],
                                  ALU.mult).then_inc(dve_hi, 1)
                dve.wait_ge(hid_step, t * 2 + f + 3)
                dve.wait_ge(dve_hi, t * 2 + f + 1)
                dve.tensor_tensor(hid_lo[:, f, :], hid[:, f, 0:P], hid_hi[:, f, 0:P].bitcast(F32),
                                  ALU.subtract)
                dve.tensor_tensor(hid_hi[:, f, REST_LO:REST_LO + REST], hid[:, f, P:BLOCK],
                                  hid_hi[:, f, REST_HI:BLOCK].bitcast(F32), ALU.subtract
                                  ).then_inc(hid_ready, 1)

            dve.wait_ge(h1_stored, 16 * TILES)
            dve.wait_ge(sched_loaded, 16)
            n = blocks_to_run(dve)
            dve.wait_ge(hid_clear, 2)
            for part in range(PARTS):
                wgu_part(0, 0, part)
            for f in range(1, FT):
                gate_shared(f)
            xT_lo(0, range(QX))
            with dve.Fori(0, n, 2) as i:
                for b in range(2):
                    t = i + b
                    wgu_part(t + 1, 1 - b, 0)
                    up_part(t, 0)
                    wgu_part(t + 1, 1 - b, 1)
                    up_part(t, 1)
                    dve.wait_ge(down_done, t * STEPS + SEED)
                    hidden(t, 0)
                    up_part(t, 2)
                    wgu_part(t + 1, 1 - b, 2)
                    up_part(t, 3)
                    hidden(t, 1)
                    xT_lo(t + 1, (0, 1))
                    wgu_part(t + 1, 1 - b, 3)
                    dve.wait_ge(ysb_free, t + 1)
                    dve.wait_ge(entries_free, t + 3)
                    dve.wait_ge(down_done, t * STEPS + SEED + 2)
                    dve.tensor_scalar(ysb[b][:, 0, 512:D], bank[:, 7, :], weight[b][:, 0:1], None,
                                      ALU.mult).then_inc(y_dve, 1)
                    xT_lo(t + 1, (2, 3))
                    rest = ysb[b][0:REST, 1, :]
                    for c in range(2):
                        dve.wait_ge(y_rest_ready, t * 2 + c + 1)
                        dve.tensor_tensor(rest[:, c * 512:(c + 1) * 512], y_rest[0:REST, c, :],
                                          bank[0:REST, 6 + c, :], ALU.add).then_inc(y_dve, 1)
                    dve.wait_ge(y_dve, t * 4 + 7)
                    dve.tensor_scalar(rest, rest, weight[b][0:REST, 1:2], None, ALU.mult
                                      ).then_inc(y_dve, 1)

    stores_done = sem("stores_done")
    h1_ready = [sem(f"h1_ready{i}") for i in range(TILES)]
    routed_ready = [sem(f"routed_ready{i}") for i in range(TILES)]
    sh_down_done, sh_read, summed = sem("sh_down_done"), sem("sh_read"), sem("summed")
    var2_ready, std2_ready, rstd2_ready = sem("var2_ready"), sem("std2_ready"), sem("rstd2_ready")
    normed2, gained = sem("normed2"), sem("gained")
    out_ready, out_stored = sem("out_ready"), sem("out_stored")
    ORDER = [TILES - 1] + list(range(TILES - 1))

    with nc.Block() as block:
        @block.sync
        def _(sp):
            for n, i in enumerate(ORDER):
                sp.dma_start(h1[0:ROWS[i], i, :], h1_rows[cols(i), :]).then_inc(h1_ready[i], 16)
                if n == 3:
                    sp.wait_ge(stores_done, 1)
                    for j in ORDER:
                        sp.dma_start(routed[0:ROWS[j], j, :], routed_rows[cols(j), :]
                                     ).then_inc(routed_ready[j], 16)
            for n, i in enumerate(ORDER):
                lo = N_META if i == 0 else 0
                sp.wait_ge(out_ready, n + 1)
                sp.dma_start(out[i * P + lo - N_META:i * P + ROWS[i] - N_META, :],
                             h1[lo:ROWS[i], i, :]).then_inc(out_stored, 16)
            sp.wait_ge(out_stored, 16 * TILES)

        @block.gpsimd
        def _(pool):
            n = blocks_to_run(pool)
            for b in range(2):
                pool.wait_ge(y_stored[b], n * 16 + 16 * b)
                pool.wait_ge(gathered[b], n * 16 + 32)
                pool.wait_ge(entries_loaded[b], n * 16 + 32)
                pool.wait_ge(wgu_loaded[b], n * 8 + 16 * (1 - b))
                pool.wait_ge(wd_loaded[b], n * 8 + 16 * (1 - b))
            pool.sem_inc(stores_done, 1)
            for n, i in enumerate(ORDER):
                x = h1[0:ROWS[i], i, :]
                pool.wait_ge(normed2, n + 1)
                if n == 0:
                    pool.wait_ge(lnf_loaded, 16)
                pool.tensor_tensor(x, x, ln_f[0:ROWS[i], 0, :], ALU.mult).then_inc(gained, 1)
                pool.wait_ge(gained, n + 1)
                pool.tensor_tensor(x, x, ln_f[0:ROWS[i], 1, :], ALU.add).then_inc(out_ready, 1)

        @block.tensor
        def _(pe):
            pe.wait_ge(sdn_loaded, 16)
            for n, i in enumerate(ORDER):
                r = ROWS[i]
                if n >= 4:
                    pe.wait_ge(sh_read, n - 3)
                for c in range(2):
                    for k in range(FT):
                        mm = pe.matmul(bank[0:r, 2 * (n % 4) + c, :], sh[:, k, cols(i)],
                                       sdn[:, k, c * 512:(c + 1) * 512],
                                       start=(k == 0), stop=(k == FT - 1))
                mm.then_inc(sh_down_done, 1)

        @block.scalar
        def _(act):
            for n, i in enumerate(ORDER):
                r = ROWS[i]
                act.wait_ge(var2_ready, n + 1)
                act.activation(rstd[0:r, 0:1], rstd[0:r, 0:1], ACT.Sqrt).then_inc(std2_ready, 1)
                act.wait_ge(rstd2_ready, n + 1)
                x = h1[0:r, i, :]
                act.activation(x, x, ACT.Identity, bias=mv[0:r, 0:1], scale=rstd[0:r, 1:2]
                               ).then_inc(normed2, 1)

        @block.vector
        def _(dve):
            s = Chain(dve, dve_step)
            s.n = dve_steps[-1]

            def add_shared(n):
                i = ORDER[n]
                dve.wait_ge(sh_down_done, n + 1)
                dve.wait_ge(h1_ready[i], 16)
                halves = h1[0:ROWS[i], i, :].rearrange("p (b n) -> p b n", b=2)
                b = 2 * (n % 4)
                dve.scalar_tensor_tensor(halves, halves, ALPHA, bank[0:ROWS[i], b:b + 2, :],
                                         ALU.mult, ALU.add).then_inc(sh_read, 1)

            add_shared(0)
            for n, i in enumerate(ORDER):
                r, x = ROWS[i], h1[0:ROWS[i], i, :]
                dve.wait_ge(sh_read, n + 1)
                dve.wait_ge(routed_ready[i], 16)
                dve.tensor_tensor(x, x, routed[0:r, i, :], ALU.add).then_inc(summed, 1)
                dve.wait_ge(summed, n + 1)
                dve.bn_stats(stats[0:r, 0, :], x[:, 0:512])
                s.step(dve.bn_stats(stats[0:r, 1, :], x[:, 512:D]))
                if n:
                    dve.wait_ge(normed2, n)
                s.step(dve.bn_aggr(mv[0:r, :], stats[0:r, :, :]))
                dve.tensor_scalar(rstd[0:r, 0:1], mv[0:r, 1:2], LN_EPS, None, ALU.add
                                  ).then_inc(var2_ready, 1)
                if n + 1 < TILES:
                    add_shared(n + 1)
                dve.wait_ge(std2_ready, n + 1)
                s.step(dve.reciprocal(rstd[0:r, 1:2], rstd[0:r, 0:1]))
                dve.scalar_tensor_tensor(mv[0:r, 0:1], mv[0:r, 0:1], -1.0, rstd[0:r, 1:2],
                                         ALU.mult, ALU.mult).then_inc(rstd2_ready, 1)


def kernel(x, meta_tokens, rg_w_in, rg_b_in, rg_conv_w, rg_conv_b, rg_w_gates, rg_b_gates,
           rg_a_param, rg_w_out, attn_w_qkv, attn_sinks, attn_w_o, rel_bias_table, ln_gain,
           ln_bias, router_w, router_bias, expert_w_gu, expert_w_down, shared_w_gu,
           shared_w_down):
    import concourse.bacc as bacc
    from concourse.bass_utils import run_bass_kernel_spmd

    h = np.concatenate([np.asarray(meta_tokens), np.asarray(x)[0]], axis=0)
    per_channel = lambda a: np.asarray(a).reshape(-1, P).T
    arrays = {
        "hT": h.T,
        "h_rows": h,
        "w_in": np.asarray(rg_w_in)[0],
        "chan": np.concatenate([per_channel(a) for a in (rg_b_in, rg_conv_w, rg_conv_b,
                                                         rg_b_gates, rg_a_param)], axis=1),
        "w_gates": np.asarray(rg_w_gates)[0],
        "w_out": np.asarray(rg_w_out)[0],
        "ln": np.stack([np.asarray(ln_gain)[0, 0], np.asarray(ln_bias)[0, 0],
                        np.asarray(ln_gain)[0, 1], np.asarray(ln_bias)[0, 1]]),
        "router_w": np.asarray(router_w)[0],
        "router_b": np.asarray(router_bias),
        "w_gu": np.asarray(expert_w_gu)[0],
        "w_down": np.asarray(expert_w_down)[0],
        "sh_gu": np.asarray(shared_w_gu)[0],
        "sh_down": np.asarray(shared_w_down)[0],
    }
    arrays = {k: np.ascontiguousarray(a) for k, a in arrays.items()}
    nc = bacc.Bacc("TRN2", target_bir_lowering=False, num_devices=1)
    args = [nc.dram_tensor(f"in_{k}", a.shape, F32, kind="ExternalInput").ap()
            for k, a in arrays.items()]
    out = nc.dram_tensor("out", (SEQ, D), F32, kind="ExternalOutput").ap()
    build(nc, *args, out)
    r = run_bass_kernel_spmd(nc, [{f"in_{k}": a for k, a in arrays.items()}], core_ids=[0])
    return r.results[0]["out"].reshape(1, SEQ, D)
```
